# Optimizing a Trainium2 kernel written in Bass

```python
import math
import jax, jax.numpy as jnp
from jax import lax
import numpy as np
import jax
import jax.numpy as jnp

D_MODEL = 1024
BATCH = 1
SEQ = 512
DEPTH = 1

EPS = 1e-6
MLA_HEADS = 8
QK_NOPE = 64
QK_ROPE = 32
QK_HEAD = QK_NOPE + QK_ROPE
V_HEAD = 64
Q_LORA = 256
KV_LORA = 128
ROPE_THETA = 10000.0
Q_BLOCK = 128
RWKV_HEADS = 8
RWKV_HEAD = 64
RWKV_DIM = RWKV_HEADS * RWKV_HEAD
DECAY_LORA = 64
AAA_LORA = 64
GATE_LORA = 128
GN_EPS = 64e-5
PEER_HEADS = 8
N_KEYS = 128
N_EXPERTS = N_KEYS * N_KEYS
D_KEY = 256
HALF_KEY = D_KEY // 2
TOPK_HALF = 16
TOPK = 16
PEER_BLOCK = 64
N_BRANCH = 2
MLA_IN = Q_LORA + KV_LORA + QK_ROPE
RWKV_IN = 3 * RWKV_DIM + DECAY_LORA + AAA_LORA + GATE_LORA
GATE_IN = N_BRANCH * D_MODEL
IN_DIM = MLA_IN + RWKV_IN + GATE_IN
N_MOD = 6


def rms_norm(x, g, eps=EPS):
    xf = x.astype(jnp.float32)
    y = xf * lax.rsqrt(jnp.mean(xf * xf, axis=-1, keepdims=True) + eps)
    return (y * g.astype(jnp.float32)).astype(x.dtype)

def modulate(h, shift, scale):
    return h * (1.0 + scale[:, None, :]) + shift[:, None, :]

def rope(x, positions):
    half = x.shape[-1] // 2
    inv_freq = ROPE_THETA ** (-jnp.arange(half, dtype=jnp.float32) / half)
    ang = positions.astype(jnp.float32)[..., None] * inv_freq
    cos = jnp.cos(ang)[:, :, None, :]
    sin = jnp.sin(ang)[:, :, None, :]
    xf = x.astype(jnp.float32)
    x1, x2 = xf[..., :half], xf[..., half:]
    return jnp.concatenate([x1 * cos - x2 * sin, x1 * sin + x2 * cos], axis=-1).astype(x.dtype)

def causal_block_attention(q, k, v):
    B, S, H, Dq = q.shape
    nb = S // Q_BLOCK
    scale = Dq ** -0.5
    qb = q.reshape(B, nb, Q_BLOCK, H, Dq).transpose(1, 0, 2, 3, 4)
    kpos = jnp.arange(S)

    def one_block(args):
        i, q_blk = args
        s = jnp.einsum('bqhd,bkhd->bhqk', q_blk, k).astype(jnp.float32) * scale
        qpos = i * Q_BLOCK + jnp.arange(Q_BLOCK)
        mask = kpos[None, :] <= qpos[:, None]
        s = jnp.where(mask[None, None], s, -jnp.inf)
        p = jax.nn.softmax(s, axis=-1).astype(v.dtype)
        return jnp.einsum('bhqk,bkhd->bqhd', p, v)

    out = lax.map(one_block, (jnp.arange(nb), qb))
    return out.transpose(1, 0, 2, 3, 4).reshape(B, S, H, v.shape[-1])

def mla_branch(q_a, kv_a, k_rope_raw, positions, q_a_norm, w_uq, kv_a_norm, w_ukv, q_norm, k_norm, w_o_mla):
    B, S, _ = q_a.shape
    cq = rms_norm(q_a, q_a_norm)
    q = (cq @ w_uq).reshape(B, S, MLA_HEADS, QK_HEAD)
    ckv = rms_norm(kv_a, kv_a_norm)
    kv = (ckv @ w_ukv).reshape(B, S, MLA_HEADS, QK_NOPE + V_HEAD)
    k_nope, v = kv[..., :QK_NOPE], kv[..., QK_NOPE:]
    q_nope = rms_norm(q[..., :QK_NOPE], q_norm[:QK_NOPE])
    q_pe = rope(rms_norm(q[..., QK_NOPE:], q_norm[QK_NOPE:]), positions)
    k_nope = rms_norm(k_nope, k_norm[:QK_NOPE])
    k_pe = rope(rms_norm(k_rope_raw[:, :, None, :], k_norm[QK_NOPE:]), positions)
    k_pe = jnp.broadcast_to(k_pe, (B, S, MLA_HEADS, QK_ROPE))
    qh = jnp.concatenate([q_nope, q_pe], axis=-1)
    kh = jnp.concatenate([k_nope, k_pe], axis=-1)
    o = causal_block_attention(qh, kh, v)
    return o.reshape(B, S, MLA_HEADS * V_HEAD) @ w_o_mla

def token_shift(p, mu):
    prev = jnp.pad(p, ((0, 0), (1, 0), (0, 0)))[:, :-1]
    return p + (prev - p) * mu

def rwkv7_scan(r, decay, k, v, kk, a):
    B, S, H, N = r.shape
    b = kk * a

    def step(state, inp):
        r_t, w_t, k_t, v_t, kk_t, b_t = inp
        sa = jnp.einsum('bhvk,bhk->bhv', state, -kk_t)
        state = (state * w_t[:, :, None, :] + sa[..., None] * b_t[:, :, None, :]
                 + v_t[..., None] * k_t[:, :, None, :])
        y = jnp.einsum('bhvk,bhk->bhv', state, r_t)
        return state, y

    xs = tuple(t.transpose(1, 0, 2, 3) for t in (r, decay, k, v, kk, b))
    s0 = jnp.zeros((B, H, N, N), jnp.float32)
    _, y = lax.scan(step, s0, xs)
    return y.transpose(1, 0, 2, 3)

def rwkv7_branch(p, mu_shift, w_decay_up, decay_base, w_aaa_up, aaa_base, w_gate_up,
                 k_k, k_a, r_k, ln_x_w, ln_x_b, w_o_rwkv):
    B, S, _ = p.shape
    p = token_shift(p, mu_shift)
    splits = [RWKV_DIM, 2 * RWKV_DIM, 3 * RWKV_DIM, 3 * RWKV_DIM + DECAY_LORA,
              3 * RWKV_DIM + DECAY_LORA + AAA_LORA]
    r, k, v, wd, ad, gd = jnp.split(p, splits, axis=-1)
    w = -jax.nn.softplus(-(decay_base + jnp.tanh(wd) @ w_decay_up)) - 0.5
    decay = jnp.exp(-jnp.exp(w.astype(jnp.float32)))
    a = jax.nn.sigmoid(aaa_base + ad @ w_aaa_up)
    g = jax.nn.sigmoid(gd) @ w_gate_up

    def heads(t):
        return t.reshape(B, S, RWKV_HEADS, RWKV_HEAD).astype(jnp.float32)

    kk = heads(k * k_k)
    kk = kk / jnp.maximum(jnp.linalg.norm(kk, axis=-1, keepdims=True), 1e-12)
    a_h = heads(a)
    k_h = heads(k) * (1.0 + (a_h - 1.0) * k_a.reshape(RWKV_HEADS, RWKV_HEAD).astype(jnp.float32))
    r_h, v_h = heads(r), heads(v)
    y = rwkv7_scan(r_h, heads(decay), k_h, v_h, kk, a_h)
    mu = jnp.mean(y, axis=-1, keepdims=True)
    var = jnp.mean(jnp.square(y - mu), axis=-1, keepdims=True)
    y = (y - mu) * lax.rsqrt(var + GN_EPS)
    y = y * ln_x_w.reshape(RWKV_HEADS, RWKV_HEAD) + ln_x_b.reshape(RWKV_HEADS, RWKV_HEAD)
    y = y + jnp.sum(r_h * k_h * r_k, axis=-1, keepdims=True) * v_h
    y = y.reshape(B, S, RWKV_DIM).astype(p.dtype) * g
    return y @ w_o_rwkv

def token_mixer(h, positions, w_in, mu_shift, q_a_norm, w_uq, kv_a_norm, w_ukv, q_norm, k_norm, w_o_mla,
                w_decay_up, decay_base, w_aaa_up, aaa_base, w_gate_up, k_k, k_a, r_k, ln_x_w, ln_x_b,
                w_o_rwkv, w_out):
    proj = h @ w_in
    q_a, kv_a, k_rope_raw, rwkv_in, gate_logits = jnp.split(
        proj, [Q_LORA, Q_LORA + KV_LORA, MLA_IN, MLA_IN + RWKV_IN], axis=-1)
    o_mla = mla_branch(q_a, kv_a, k_rope_raw, positions, q_a_norm, w_uq, kv_a_norm, w_ukv,
                       q_norm, k_norm, w_o_mla)
    o_rwkv = rwkv7_branch(rwkv_in, mu_shift, w_decay_up, decay_base, w_aaa_up, aaa_base, w_gate_up,
                          k_k, k_a, r_k, ln_x_w, ln_x_b, w_o_rwkv)
    g_mla, g_rwkv = jnp.split(jax.nn.sigmoid(gate_logits), 2, axis=-1)
    return (g_mla * o_mla + g_rwkv * o_rwkv) @ w_out

def peer_ffn(h, w_query, sub_keys1, sub_keys2, expert_down, expert_up):
    B, S, D = h.shape
    q = (h @ w_query).reshape(B, S, PEER_HEADS, 2, HALF_KEY)
    s1 = jnp.einsum('bshd,nd->bshn', q[..., 0, :], sub_keys1).astype(jnp.float32)
    s2 = jnp.einsum('bshd,nd->bshn', q[..., 1, :], sub_keys2).astype(jnp.float32)
    v1, i1 = lax.top_k(s1, TOPK_HALF)
    v2, i2 = lax.top_k(s2, TOPK_HALF)
    cand = (v1[..., :, None] + v2[..., None, :]).reshape(B, S, PEER_HEADS, TOPK_HALF * TOPK_HALF)
    cand_idx = (i1[..., :, None] * N_KEYS + i2[..., None, :]).reshape(B, S, PEER_HEADS, TOPK_HALF * TOPK_HALF)
    top_v, pos = lax.top_k(cand, TOPK)
    expert_idx = jnp.take_along_axis(cand_idx, pos, axis=-1)
    gates = jax.nn.softmax(top_v, axis=-1).astype(h.dtype)
    nb = S // PEER_BLOCK
    hb = h.reshape(B, nb, PEER_BLOCK, D).transpose(1, 0, 2, 3)
    idxb = expert_idx.reshape(B, nb, PEER_BLOCK, PEER_HEADS, TOPK).transpose(1, 0, 2, 3, 4)
    gb = gates.reshape(B, nb, PEER_BLOCK, PEER_HEADS, TOPK).transpose(1, 0, 2, 3, 4)

    def one_block(args):
        h_blk, idx_blk, g_blk = args
        u = jnp.take(expert_down, idx_blk, axis=0)
        act = jax.nn.gelu(jnp.einsum('bpd,bphkd->bphk', h_blk, u))
        vv = jnp.take(expert_up, idx_blk, axis=0)
        return jnp.einsum('bphk,bphkd->bpd', g_blk * act, vv)

    out = lax.map(one_block, (hb, idxb, gb))
    return out.transpose(1, 0, 2, 3).reshape(B, S, D)

def first_inputs(seed: int = 0) -> dict:
    key = jax.random.key(seed)
    ks = jax.random.split(key, 40)
    f32 = jnp.float32

    def nrm(k, shape, scale):
        return jax.random.normal(k, (DEPTH,) + shape, f32) * scale

    def gain(k, shape):
        return 1.0 + 0.1 * jax.random.normal(k, (DEPTH,) + shape, f32)

    x = jax.random.normal(ks[0], (BATCH, SEQ, D_MODEL), f32)
    c = jax.random.normal(ks[1], (BATCH, D_MODEL), f32)
    offsets = jax.random.randint(ks[2], (BATCH, 1), 0, 1024, dtype=jnp.int32)
    positions = offsets + jnp.arange(SEQ, dtype=jnp.int32)[None, :]
    return {
        "x": x, "c": c, "positions": positions,
        "w_ada": nrm(ks[3], (D_MODEL, N_MOD * D_MODEL), 0.3 * D_MODEL ** -0.5),
        "b_ada": nrm(ks[4], (N_MOD * D_MODEL,), 0.05),
        "norm_mix": gain(ks[5], (D_MODEL,)),
        "w_in": nrm(ks[6], (D_MODEL, IN_DIM), D_MODEL ** -0.5),
        "mu_shift": jax.random.uniform(ks[7], (DEPTH, RWKV_IN), f32),
        "q_a_norm": gain(ks[8], (Q_LORA,)),
        "w_uq": nrm(ks[9], (Q_LORA, MLA_HEADS * QK_HEAD), Q_LORA ** -0.5),
        "kv_a_norm": gain(ks[10], (KV_LORA,)),
        "w_ukv": nrm(ks[11], (KV_LORA, MLA_HEADS * (QK_NOPE + V_HEAD)), KV_LORA ** -0.5),
        "q_norm": gain(ks[12], (QK_HEAD,)),
        "k_norm": gain(ks[13], (QK_HEAD,)),
        "w_o_mla": nrm(ks[14], (MLA_HEADS * V_HEAD, D_MODEL), (MLA_HEADS * V_HEAD) ** -0.5),
        "w_decay_up": nrm(ks[15], (DECAY_LORA, RWKV_DIM), 0.1),
        "decay_base": jax.random.uniform(ks[16], (DEPTH, RWKV_DIM), f32, -6.0, 2.0),
        "w_aaa_up": nrm(ks[17], (AAA_LORA, RWKV_DIM), 0.1),
        "aaa_base": nrm(ks[18], (RWKV_DIM,), 0.5),
        "w_gate_up": nrm(ks[19], (GATE_LORA, RWKV_DIM), GATE_LORA ** -0.5),
        "k_k": 0.85 + nrm(ks[20], (RWKV_DIM,), 0.1),
        "k_a": gain(ks[21], (RWKV_DIM,)),
        "r_k": nrm(ks[22], (RWKV_HEADS, RWKV_HEAD), 0.1),
        "ln_x_w": gain(ks[23], (RWKV_DIM,)),
        "ln_x_b": nrm(ks[24], (RWKV_DIM,), 0.02),
        "w_o_rwkv": nrm(ks[25], (RWKV_DIM, D_MODEL), RWKV_DIM ** -0.5),
        "w_out": nrm(ks[26], (D_MODEL, D_MODEL), D_MODEL ** -0.5),
        "norm_ffn": gain(ks[27], (D_MODEL,)),
        "w_query": nrm(ks[28], (D_MODEL, PEER_HEADS * D_KEY), D_MODEL ** -0.5),
        "sub_keys1": nrm(ks[29], (N_KEYS, HALF_KEY), HALF_KEY ** -0.5),
        "sub_keys2": nrm(ks[30], (N_KEYS, HALF_KEY), HALF_KEY ** -0.5),
        "expert_down": nrm(ks[31], (N_EXPERTS, D_MODEL), D_MODEL ** -0.5),
        "expert_up": nrm(ks[32], (N_EXPERTS, D_MODEL), PEER_HEADS ** -0.5),
    }

def first_block(x, c, positions, w_ada, b_ada, norm_mix, w_in, mu_shift, q_a_norm, w_uq, kv_a_norm, w_ukv,
              q_norm, k_norm, w_o_mla, w_decay_up, decay_base, w_aaa_up, aaa_base, w_gate_up, k_k, k_a, r_k,
              ln_x_w, ln_x_b, w_o_rwkv, w_out, norm_ffn, w_query, sub_keys1, sub_keys2, expert_down, expert_up):
    for l in range(DEPTH):
        mod = jax.nn.silu(c) @ w_ada[l] + b_ada[l]
        sh1, sc1, gt1, sh2, sc2, gt2 = jnp.split(mod, N_MOD, axis=-1)
        h = modulate(rms_norm(x, norm_mix[l]), sh1, sc1)
        mix = token_mixer(h, positions, w_in[l], mu_shift[l], q_a_norm[l], w_uq[l], kv_a_norm[l], w_ukv[l],
                          q_norm[l], k_norm[l], w_o_mla[l], w_decay_up[l], decay_base[l], w_aaa_up[l],
                          aaa_base[l], w_gate_up[l], k_k[l], k_a[l], r_k[l], ln_x_w[l], ln_x_b[l],
                          w_o_rwkv[l], w_out[l])
        x = x + gt1[:, None, :] * mix
        h = modulate(rms_norm(x, norm_ffn[l]), sh2, sc2)
        x = x + gt2[:, None, :] * peer_ffn(h, w_query[l], sub_keys1[l], sub_keys2[l], expert_down[l], expert_up[l])
    return x


N_MEM = 256
BLOCK = 128
FOX_HEADS = 8
FOX_HD = 64
SWA_HEADS = 8
SWA_KV_HEADS = 2
SWA_HD = 64
WINDOW = 128
MEM_HEADS = 4
MEM_HD = 128
N_BRANCH_2 = 3
N_EXPERTS_2 = N_KEYS * N_KEYS
PEER_QD = 256
PEER_TOPK = 16
PEER_CHUNK = 128
NEG_INF = -1e30

FOX_W = FOX_HEADS * FOX_HD
SWA_W = SWA_HEADS * SWA_HD
SWA_KV_W = SWA_KV_HEADS * SWA_HD
MEM_W = MEM_HEADS * MEM_HD
IN_WIDTHS = (FOX_W, FOX_W, FOX_W, FOX_HEADS, SWA_W, SWA_KV_W, SWA_KV_W, MEM_W, N_BRANCH_2 * D_MODEL)
IN_COLS = 3 * FOX_W + FOX_HEADS + SWA_W + 2 * SWA_KV_W + MEM_W + N_BRANCH_2 * D_MODEL


def rmsnorm(x, g):
    xf = x.astype(jnp.float32)
    y = xf * lax.rsqrt(jnp.mean(xf * xf, axis=-1, keepdims=True) + EPS)
    return (y * g.astype(jnp.float32)).astype(x.dtype)

def head_rmsnorm(x, g):
    xf = x.astype(jnp.float32)
    return xf * lax.rsqrt(jnp.mean(xf * xf, axis=-1, keepdims=True) + EPS) * g.astype(jnp.float32)

def alibi_slopes(n):
    return 2.0 ** (-8.0 * (jnp.arange(n, dtype=jnp.float32) + 1.0) / n)

def fox_attention(q, k, v, log_f):
    B, S, H, d = q.shape
    nb = S // BLOCK
    c = jnp.cumsum(log_f, axis=1).transpose(0, 2, 1)
    q_blocks = q.reshape(B, nb, BLOCK, H, d).transpose(1, 0, 2, 3, 4)
    c_blocks = c.reshape(B, H, nb, BLOCK).transpose(2, 0, 1, 3)
    vf = v.astype(jnp.float32)
    kpos = jnp.arange(S)
    scale = d ** -0.5

    def one_block(args):
        i, q_i, c_i = args
        s = jnp.einsum('bqhd,bkhd->bhqk', q_i, k) * scale
        s = s + (c_i[..., :, None] - c[..., None, :])
        qpos = i * BLOCK + jnp.arange(BLOCK)
        s = jnp.where(kpos[None, :] <= qpos[:, None], s, NEG_INF)
        p = jax.nn.softmax(s, axis=-1)
        return jnp.einsum('bhqk,bkhd->bqhd', p, vf)

    o = lax.map(one_block, (jnp.arange(nb), q_blocks, c_blocks))
    return o.transpose(1, 0, 2, 3, 4).reshape(B, S, H, d)

def swa_attention(q, k, v, sinks, slopes):
    B, S, Hq, d = q.shape
    G = k.shape[2]
    R = Hq // G
    nb = S // BLOCK
    qb = q.reshape(B, nb, BLOCK, G, R, d)

    def band(t):
        t = t.astype(jnp.float32)
        tp = jnp.concatenate([jnp.zeros((B, BLOCK, G, d), jnp.float32), t], axis=1)
        tp = tp.reshape(B, nb + 1, BLOCK, G, d)
        return jnp.concatenate([tp[:, :-1], tp[:, 1:]], axis=2)

    kb = band(k)
    vb = band(v)
    s = jnp.einsum('bnqgrd,bnkgd->bngrqk', qb, kb) * d ** -0.5
    qi = jnp.arange(BLOCK)[:, None]
    kj = jnp.arange(2 * BLOCK)[None, :]
    dist_i = qi + BLOCK - kj
    in_window = (dist_i >= 0) & (dist_i < WINDOW)
    blk_ok = (jnp.arange(nb)[:, None] > 0) | (jnp.arange(2 * BLOCK)[None, :] >= BLOCK)
    mask = in_window[None] & blk_ok[:, None, :]
    s = s - slopes.astype(jnp.float32).reshape(G, R)[:, :, None, None] * dist_i.astype(jnp.float32)
    s = jnp.where(mask[None, :, None, None], s, NEG_INF)
    sink = jnp.broadcast_to(sinks.astype(jnp.float32).reshape(1, 1, G, R, 1, 1), s.shape[:-1] + (1,))
    p = jax.nn.softmax(jnp.concatenate([s, sink], axis=-1), axis=-1)[..., :-1]
    o = jnp.einsum('bngrqk,bnkgd->bnqgrd', p, vb)
    return o.reshape(B, S, Hq, d)

def memory_attention(q, k, v):
    d = q.shape[-1]
    s = jnp.einsum('bshd,bmhd->bhsm', q, k) * d ** -0.5
    p = jax.nn.softmax(s, axis=-1)
    return jnp.einsum('bhsm,bmhd->bshd', p, v.astype(jnp.float32))

def peer_ffn_2(h, w_q, keys1, keys2, u, v):
    B, S, D = h.shape
    half = PEER_QD // 2
    q = (h @ w_q).astype(jnp.float32).reshape(B, S, PEER_HEADS, 2, half)
    s1 = jnp.einsum('bshd,hkd->bshk', q[..., 0, :], keys1.astype(jnp.float32))
    s2 = jnp.einsum('bshd,hkd->bshk', q[..., 1, :], keys2.astype(jnp.float32))
    v1, i1 = lax.top_k(s1, PEER_TOPK)
    v2, i2 = lax.top_k(s2, PEER_TOPK)
    cand = (v1[..., :, None] + v2[..., None, :]).reshape(B, S, PEER_HEADS, PEER_TOPK * PEER_TOPK)
    sv, si = lax.top_k(cand, PEER_TOPK)
    e1 = jnp.take_along_axis(i1, si // PEER_TOPK, axis=-1)
    e2 = jnp.take_along_axis(i2, si % PEER_TOPK, axis=-1)
    experts = e1 * N_KEYS + e2
    gates = jax.nn.softmax(sv, axis=-1)
    n_act = PEER_HEADS * PEER_TOPK
    n_chunks = (B * S) // PEER_CHUNK
    hc = h.reshape(n_chunks, PEER_CHUNK, D)
    ec = experts.reshape(n_chunks, PEER_CHUNK, n_act)
    gc = gates.reshape(n_chunks, PEER_CHUNK, n_act)

    def chunk(args):
        h_c, e_c, g_c = args
        a = jnp.einsum('cd,ced->ce', h_c.astype(jnp.float32), u[e_c].astype(jnp.float32))
        act = jax.nn.gelu(a, approximate=False) * g_c
        return jnp.einsum('ce,ced->cd', act, v[e_c].astype(jnp.float32))

    out = lax.map(chunk, (hc, ec, gc))
    return out.reshape(B, S, D).astype(h.dtype)

def second_inputs(seed: int = 0) -> dict:
    key = jax.random.key(seed)
    ks = jax.random.split(key, 25)
    L = DEPTH
    D = D_MODEL

    def nrm(k, shape, scale):
        return scale * jax.random.normal(k, shape, jnp.float32)

    return {
        'x': nrm(ks[0], (BATCH, SEQ, D), 1.0),
        'mem': nrm(ks[1], (BATCH, N_MEM, D), 1.0),
        'norm1_g': 1.0 + nrm(ks[2], (L, D), 0.02),
        'w_in': nrm(ks[3], (L, D, IN_COLS), D ** -0.5),
        'b_gate': nrm(ks[4], (L, N_BRANCH_2 * D), 0.02),
        'b_forget': 2.0 + nrm(ks[5], (L, FOX_HEADS), 0.5),
        'fox_q_g': 1.0 + nrm(ks[6], (L, FOX_HD), 0.02),
        'fox_k_g': 1.0 + nrm(ks[7], (L, FOX_HD), 0.02),
        'swa_q_g': 1.0 + nrm(ks[8], (L, SWA_HD), 0.02),
        'swa_k_g': 1.0 + nrm(ks[9], (L, SWA_HD), 0.02),
        'swa_sinks': nrm(ks[10], (L, SWA_HEADS), 0.5),
        'mem_norm_g': 1.0 + nrm(ks[11], (L, D), 0.02),
        'w_mem_kv': nrm(ks[12], (L, D, 2 * MEM_W), D ** -0.5),
        'mem_q_g': 1.0 + nrm(ks[13], (L, MEM_HD), 0.02),
        'mem_k_g': 1.0 + nrm(ks[14], (L, MEM_HD), 0.02),
        'w_fox_o': nrm(ks[15], (L, FOX_W, D), FOX_W ** -0.5),
        'w_swa_o': nrm(ks[16], (L, SWA_W, D), SWA_W ** -0.5),
        'w_mem_o': nrm(ks[17], (L, MEM_W, D), MEM_W ** -0.5),
        'w_out': nrm(ks[18], (L, D, D), D ** -0.5),
        'norm2_g': 1.0 + nrm(ks[19], (L, D), 0.02),
        'w_peer_q': nrm(ks[20], (L, D, PEER_HEADS * PEER_QD), D ** -0.5),
        'peer_keys1': nrm(ks[21], (L, PEER_HEADS, N_KEYS, PEER_QD // 2), (PEER_QD // 2) ** -0.5),
        'peer_keys2': nrm(ks[22], (L, PEER_HEADS, N_KEYS, PEER_QD // 2), (PEER_QD // 2) ** -0.5),
        'peer_u': nrm(ks[23], (L, N_EXPERTS_2, D), D ** -0.5),
        'peer_v': nrm(ks[24], (L, N_EXPERTS_2, D), (PEER_HEADS * PEER_TOPK) ** -0.5),
    }

def second_block(x, mem, norm1_g, w_in, b_gate, b_forget, fox_q_g, fox_k_g, swa_q_g, swa_k_g,
              swa_sinks, mem_norm_g, w_mem_kv, mem_q_g, mem_k_g, w_fox_o, w_swa_o, w_mem_o,
              w_out, norm2_g, w_peer_q, peer_keys1, peer_keys2, peer_u, peer_v):
    B, S, D = x.shape
    M = mem.shape[1]
    splits = [int(c) for c in np.cumsum(IN_WIDTHS)[:-1]]
    slopes = alibi_slopes(SWA_HEADS)
    for l in range(DEPTH):
        h = rmsnorm(x, norm1_g[l])
        z = h @ w_in[l]
        fq, fk, fv, ff, sq, sk, sv, mq, gl = jnp.split(z, splits, axis=-1)

        fq = head_rmsnorm(fq.reshape(B, S, FOX_HEADS, FOX_HD), fox_q_g[l])
        fk = head_rmsnorm(fk.reshape(B, S, FOX_HEADS, FOX_HD), fox_k_g[l])
        log_f = jax.nn.log_sigmoid((ff + b_forget[l]).astype(jnp.float32))
        o_fox = fox_attention(fq, fk, fv.reshape(B, S, FOX_HEADS, FOX_HD), log_f)
        o_fox = o_fox.reshape(B, S, FOX_W).astype(x.dtype)

        sq = head_rmsnorm(sq.reshape(B, S, SWA_HEADS, SWA_HD), swa_q_g[l])
        sk = head_rmsnorm(sk.reshape(B, S, SWA_KV_HEADS, SWA_HD), swa_k_g[l])
        o_swa = swa_attention(sq, sk, sv.reshape(B, S, SWA_KV_HEADS, SWA_HD), swa_sinks[l], slopes)
        o_swa = o_swa.reshape(B, S, SWA_W).astype(x.dtype)

        mn = rmsnorm(mem, mem_norm_g[l])
        mk, mv = jnp.split(mn @ w_mem_kv[l], 2, axis=-1)
        mk = head_rmsnorm(mk.reshape(B, M, MEM_HEADS, MEM_HD), mem_k_g[l])
        mq = head_rmsnorm(mq.reshape(B, S, MEM_HEADS, MEM_HD), mem_q_g[l])
        o_mem = memory_attention(mq, mk, mv.reshape(B, M, MEM_HEADS, MEM_HD))
        o_mem = o_mem.reshape(B, S, MEM_W).astype(x.dtype)

        gates = jax.nn.sigmoid((gl + b_gate[l]).astype(jnp.float32)).astype(x.dtype)
        gates = gates.reshape(B, S, N_BRANCH_2, D)
        merged = (gates[:, :, 0] * (o_fox @ w_fox_o[l])
                  + gates[:, :, 1] * (o_swa @ w_swa_o[l])
                  + gates[:, :, 2] * (o_mem @ w_mem_o[l]))
        x = x + merged @ w_out[l]

        x = x + peer_ffn_2(rmsnorm(x, norm2_g[l]), w_peer_q[l], peer_keys1[l], peer_keys2[l],
                         peer_u[l], peer_v[l])
    return x


def setup_inputs(seed=0):
    out = dict(first_inputs(seed))
    for name, value in second_inputs(seed + 1).items():
        if name != "x":
            out[name + "_2"] = value
    return out


def reference(
    x, c, positions, w_ada, b_ada, norm_mix, w_in, mu_shift, q_a_norm, w_uq, kv_a_norm, w_ukv,
    q_norm, k_norm, w_o_mla, w_decay_up, decay_base, w_aaa_up, aaa_base, w_gate_up, k_k, k_a,
    r_k, ln_x_w, ln_x_b, w_o_rwkv, w_out, norm_ffn, w_query, sub_keys1, sub_keys2, expert_down,
    expert_up, mem_2, norm1_g_2, w_in_2, b_gate_2, b_forget_2, fox_q_g_2, fox_k_g_2, swa_q_g_2,
    swa_k_g_2, swa_sinks_2, mem_norm_g_2, w_mem_kv_2, mem_q_g_2, mem_k_g_2, w_fox_o_2,
    w_swa_o_2, w_mem_o_2, w_out_2, norm2_g_2, w_peer_q_2, peer_keys1_2, peer_keys2_2, peer_u_2,
    peer_v_2,
):
    x = first_block(
        x, c, positions, w_ada, b_ada, norm_mix, w_in, mu_shift, q_a_norm, w_uq, kv_a_norm,
        w_ukv, q_norm, k_norm, w_o_mla, w_decay_up, decay_base, w_aaa_up, aaa_base, w_gate_up,
        k_k, k_a, r_k, ln_x_w, ln_x_b, w_o_rwkv, w_out, norm_ffn, w_query, sub_keys1, sub_keys2,
        expert_down, expert_up,
    )
    return second_block(
        x, mem_2, norm1_g_2, w_in_2, b_gate_2, b_forget_2, fox_q_g_2, fox_k_g_2, swa_q_g_2,
        swa_k_g_2, swa_sinks_2, mem_norm_g_2, w_mem_kv_2, mem_q_g_2, mem_k_g_2, w_fox_o_2,
        w_swa_o_2, w_mem_o_2, w_out_2, norm2_g_2, w_peer_q_2, peer_keys1_2, peer_keys2_2,
        peer_u_2, peer_v_2,
    )


_drawn_inputs = setup_inputs


def setup_inputs(seed=0):
    import zlib

    import numpy as np

    out = dict(_drawn_inputs(seed))
    spreads = {}
    factors = {'norm_mix': 4.233,
     'q_a_norm': 8.0,
     'w_uq': 3.4,
     'kv_a_norm': 8.0,
     'q_norm': 8.0,
     'k_norm': 8.0,
     'w_decay_up': 25.36,
     'w_aaa_up': 3.107,
     'aaa_base': 5.052,
     'k_k': 63.072,
     'k_a': 6.852,
     'r_k': 3.221,
     'ln_x_w': 62.384,
     'ln_x_b': 64.0,
     'norm_ffn': 33.328,
     'norm1_g_2': 6.217,
     'b_gate_2': 64.0,
     'fox_q_g_2': 35.367,
     'fox_k_g_2': 34.523,
     'swa_q_g_2': 31.282,
     'swa_k_g_2': 30.807,
     'swa_sinks_2': 40.504,
     'mem_norm_g_2': 8.0,
     'mem_q_g_2': 21.927,
     'mem_k_g_2': 25.319,
     'norm2_g_2': 64.0,
     'decay_base': 3.85,
     'w_query': 2.755,
     'sub_keys1': 2.858,
     'sub_keys2': 2.8,
     'expert_down': 3.497,
     'expert_up': 2.895}
    for name, (base, spread) in spreads.items():
        noise = np.random.default_rng([zlib.crc32(name.encode()), seed]).standard_normal(out[name].shape)
        drawn = base * np.exp(spread * noise) if base else spread * noise
        out[name] = jnp.asarray(drawn.astype(out[name].dtype))
    for name, factor in factors.items():
        out[name] = (out[name] * factor).astype(out[name].dtype)
    return out
```

```python
import numpy as np
import concourse.bass as bass
from concourse import mybir
from contextlib import ExitStack

F32 = mybir.dt.float32
F32R = mybir.dt.float32r
U32 = mybir.dt.uint32
I32 = mybir.dt.int32
ALU = mybir.AluOpType
ACT = mybir.ActivationFunctionType
AX = mybir.AxisListType.X
ds = bass.ds

P = 128
S = 512
D = 1024
TT = S // P
DC = D // P
EPS = 1e-6
NEG = -1e30
MH, NOPE, ROPE, VH = 8, 64, 32, 64
QH = NOPE + ROPE
RH, RN = 8, 64
RP = RH // 2
GN_EPS = 64e-5
Z_QA, Z_KV, Z_R, Z_K, Z_V, Z_WA, Z_GD, Z_GATE, Z_ROPE, Z_N = 0, 2, 3, 7, 11, 15, 16, 17, 33, 34
FH, FD = 8, 64
SH, SG, SD = 8, 2, 64
GH, GD = 4, 128
NMEM = 256
Y_FQ, Y_FK, Y_FV, Y_SQ, Y_SKV, Y_MQ, Y_GATE, Y_FF, Y_N = 0, 4, 8, 12, 16, 18, 22, 46, 47
PH, NK, K16 = 8, 128, 16
NJ = PH * K16
SUB = 64


class Chain:

    def __init__(self, eng, sem):
        self.eng, self.sem, self.n = eng, sem, 0

    def __call__(self, ins):
        self.n += 1
        ins.then_inc(self.sem, 1)
        self.eng.wait_ge(self.sem, self.n)

    def announce(self, ins, sem, count):
        ins.then_inc(sem, 1)
        self.eng.wait_ge(sem, count)


class Room:

    def __init__(self, nc, stack, name):
        self.nc, self.stack, self.name, self.sems = nc, stack, name, []
        stack.callback(lambda: [nc.gpsimd.sem_clear(s) for s in self.sems])

    def sb(self, name, shape, dt=F32):
        return self.stack.enter_context(self.nc.sbuf_tensor(f"{self.name}_{name}", shape, dt))

    def ps(self, name, shape=(P, 512), dt=F32):
        return self.stack.enter_context(self.nc.psum_tensor(f"{self.name}_{name}", list(shape), dt))

    def sem(self, *names):
        got = [self.stack.enter_context(self.nc.semaphore(f"{self.name}_{n}")) for n in names]
        self.sems += got
        return got[0] if len(got) == 1 else got


def bcast(ap, n, axis):
    shape = list(ap.shape)
    a = ap.unsqueeze(axis)
    shape.insert(axis, n)
    return a.to_broadcast(shape)


def row(t, m):
    return t[:, m, :] if isinstance(m, int) else t[:, ds(m, 1), :].rearrange("p a t -> p (a t)")


def col(t, m):
    return t[:, m:m + 1] if isinstance(m, int) else t[:, ds(m, 1)]


def load_stage(nc, name, pairs):
    with ExitStack() as stack:
        r = Room(nc, stack, name)
        loaded = r.sem("loaded")
        with nc.Block() as block:
            @block.sync
            def _(sp):
                for dst, src in pairs:
                    sp.dma_start(dst, src).then_inc(loaded, 16)
                sp.wait_ge(loaded, 16 * len(pairs))


def ada_stage(nc, ccol, w_ada, bcol, mod):
    groups = w_ada.shape[1] // 512
    with ExitStack() as stack:
        r = Room(nc, stack, "ada")
        sig, sc = r.sb("sig", [P, DC]), r.sb("silu", [P, DC])
        w = [r.sb(f"w{u}", [P, DC, 512]) for u in range(2)]
        ps = [r.ps(f"ps{u}") for u in range(2)]
        sig_ready, silu_ready, product_ready, product_used = r.sem(
            "sig_ready", "silu_ready", "product_ready", "product_used")
        w_ready = [r.sem(f"w_ready{u}") for u in range(2)]
        w_src = w_ada.rearrange("(c p) (g n) -> g p c n", p=P, n=512)
        with nc.Block() as block:
            @block.sync
            def _(sp):
                for u in range(2):
                    sp.dma_start(w[u][:], w_src[u]).then_inc(w_ready[u], 16)
                with sp.Fori(1, groups // 2) as i:
                    for u in range(2):
                        sp.wait_ge(product_ready, 2 * i + u - 1)
                        sp.dma_start(w[u][:], w_src[ds(2 * i + u, 1)].rearrange("a p c n -> (a p) c n")).then_inc(w_ready[u], 16)

            @block.scalar
            def _(act):
                act.activation(sig[:], ccol, ACT.Sigmoid).then_inc(sig_ready, 1)

            @block.tensor
            def _(pe):
                pe.wait_ge(silu_ready, 1)
                with pe.Fori(0, groups // 2) as i:
                    for u in range(2):
                        pe.wait_ge(w_ready[u], 16 * i + 16)
                        pe.wait_ge(product_used, 2 * i + 1)
                        for j in range(4):
                            for c in range(DC):
                                last = pe.matmul(ps[u][:, j:j + 1], w[u][:, c, j * P:(j + 1) * P], sc[:, c:c + 1],
                                                 start=c == 0, stop=c == DC - 1)
                        last.then_inc(product_ready, 1)

            @block.vector
            def _(dve):
                dve.sem_inc(product_used, 1)
                dve.wait_ge(sig_ready, 1)
                dve.tensor_tensor(sc[:], ccol, sig[:], ALU.mult).then_inc(silu_ready, 1)
                with dve.Fori(0, groups // 2) as i:
                    for u in range(2):
                        dve.wait_ge(product_ready, 2 * i + u + 1)
                        dve.tensor_tensor(mod[:, ds(8 * i + 4 * u, 4)], ps[u][:, 0:4], bcol[:, ds(8 * i + 4 * u, 4)],
                                          ALU.add).then_inc(product_used, 1)


def norm_stage(nc, name, k, src, chunks, width, gain, dst, shift=None, tokens=S):
    with ExitStack() as stack:
        r = Room(nc, stack, name)
        sq, mean, root, rstd = r.sb("sq", [P, chunks, tokens]), r.sb("mean", [P, tokens]), r.sb("root", [P, tokens]), r.sb("rstd", [P, tokens])
        ss = r.ps("ss")
        sq_ready, ss_ready, mean_ready, root_ready, chain = r.sem("sq_ready", "ss_ready", "mean_ready", "root_ready", "chain")
        with nc.Block() as block:
            @block.scalar
            def _(act):
                for c in range(chunks):
                    act.activation(sq[:, c, :], src[:, c, :], ACT.Square).then_inc(sq_ready, 1)
                act.wait_ge(mean_ready, 1)
                act.activation(root[:], mean[:], ACT.Sqrt).then_inc(root_ready, 1)

            @block.tensor
            def _(pe):
                for c in range(chunks):
                    pe.wait_ge(sq_ready, c + 1)
                    last = pe.matmul(ss[:, 0:tokens], k.ones[:], sq[:, c, :], start=c == 0, stop=c == chunks - 1)
                last.then_inc(ss_ready, 1)

            @block.vector
            def _(dve):
                link = Chain(dve, chain)
                dve.wait_ge(ss_ready, 1)
                dve.tensor_scalar(mean[:], ss[:, 0:tokens], 1.0 / width, EPS, ALU.mult, ALU.add).then_inc(mean_ready, 1)
                dve.wait_ge(root_ready, 1)
                link(dve.reciprocal(rstd[:], root[:]))
                for c in range(chunks):
                    ins = dve.scalar_tensor_tensor(dst[:, c, :], src[:, c, :], gain[:, c:c + 1], rstd[:], ALU.mult, ALU.mult)
                    if shift is not None:
                        link(ins)
                        dve.tensor_scalar(dst[:, c, :], dst[:, c, :], shift[:, c:c + 1], None, ALU.add)


def project_stage(nc, name, w_dram, act_in, kc, chunks, dst, tokens=S, add=None):
    with ExitStack() as stack:
        r = Room(nc, stack, name)
        w = [r.sb(f"w{u}", [P, kc, 2 * P]) for u in range(2)]
        ps = [r.ps(f"ps{u}") for u in range(4)]
        chunk_ready, chunk_used = r.sem("chunk_ready", "chunk_used")
        w_ready = [r.sem(f"w_ready{u}") for u in range(2)]
        turns, rest = divmod(chunks, 4)
        w_src = w_dram.rearrange("(c p) (m n) -> m p c n", p=P, n=P)

        def weights(m0, n):
            src = w_src[m0:m0 + n] if isinstance(m0, int) else w_src[ds(m0, n)]
            return src.rearrange("m p c n -> p c m n")

        def wview(u, n):
            return w[u][:, :, 0:n * P].rearrange("p c (m n) -> p c m n", n=P)

        with nc.Block() as block:
            @block.sync
            def _(sp):
                def load(u, m0, n):
                    for j in range(n):
                        sp.dma_start(w[u][:, :, j * P:(j + 1) * P], weights(m0 + j, 1).rearrange("p c m n -> p c (m n)")).then_inc(w_ready[u], 16)

                if turns:
                    for u in range(2):
                        load(u, 2 * u, 2)
                if turns > 1:
                    with sp.Fori(1, turns) as i:
                        for u in range(2):
                            sp.wait_ge(chunk_ready, 4 * i + 2 * u - 2)
                            load(u, 4 * i + 2 * u, 2)
                for u in range((rest + 1) // 2):
                    if turns:
                        sp.wait_ge(chunk_ready, 4 * turns + 2 * u - 2)
                    load(u, 4 * turns + 2 * u, min(2, rest - 2 * u))

            @block.tensor
            def _(pe):
                def make(u, j):
                    for c in range(kc):
                        last = pe.matmul(ps[2 * u + j][:, 0:tokens], w[u][:, c, j * P:(j + 1) * P], act_in[:, c, :],
                                         start=c == 0, stop=c == kc - 1)
                    last.then_inc(chunk_ready, 1)

                if turns:
                    with pe.Fori(0, turns) as i:
                        for u in range(2):
                            pe.wait_ge(w_ready[u], 32 * i + 32)
                            for j in range(2):
                                pe.wait_ge(chunk_used, 4 * i + 1)
                                make(u, j)
                for q in range(rest):
                    u, j = divmod(q, 2)
                    if j == 0:
                        pe.wait_ge(w_ready[u], 32 * turns + 16 * min(2, rest - 2 * u))
                        if turns:
                            pe.wait_ge(chunk_used, 4 * turns + 1)
                    make(u, j)

            @block.vector
            def _(dve):
                def take(q, m):
                    if add is None:
                        ins = dve.tensor_copy(row(dst, m), ps[q][:, 0:tokens])
                    else:
                        gain, base = add
                        ins = dve.scalar_tensor_tensor(row(dst, m), ps[q][:, 0:tokens], col(gain, m), row(base, m), ALU.mult, ALU.add)
                    ins.then_inc(chunk_used, 1)

                dve.sem_inc(chunk_used, 1)
                if turns:
                    with dve.Fori(0, turns) as i:
                        for q in range(4):
                            dve.wait_ge(chunk_ready, 4 * i + q + 1)
                            take(q, 4 * i + q)
                for q in range(rest):
                    dve.wait_ge(chunk_ready, 4 * turns + q + 1)
                    take(q, 4 * turns + q)

def mla_heads_stage(nc, k, z, g, cq, ckv, w_uq_in, w_ukv_in, qT, kT, v_tp, spare):
    with ExitStack() as stack:
        r = Room(nc, stack, "mlah")
        w_uq, w_ukv = r.sb("w_uq", [P, 2, MH * QH]), r.sb("w_ukv", [P, MH * (NOPE + VH)])
        gq, gk = r.sb("gq", [P, QH]), r.sb("gk", [P, QH])
        pos_i, pos = r.sb("pos_i", [P, TT], I32), r.sb("pos", [P, TT])
        freq = r.sb("freq", [P, 16])
        ang, turns, trig = r.sb("ang", [P, TT, 16]), r.sb("turns", [P, TT, 16]), r.sb("trig", [P, 2, TT, 16])
        q, kk = r.sb("q", [P, TT, MH, QH]), r.sb("kk", [P, TT, MH, QH])
        kr = r.sb("kr", [P, TT, ROPE])
        sq = r.sb("sq", [P, TT * MH, QH])
        ss, root = r.sb("ss", [P, 4, TT * MH]), r.sb("root", [P, 4, TT * MH])
        rot = spare[:, 0:4, :].rearrange("p a (g n) -> p a g n", n=16)
        ps = [r.ps(f"ps{u}") for u in range(4)]
        pt = [r.ps(f"pt{u}") for u in range(2)]
        loaded, made, taken, sums, roots, heads, turned, turned_used, reduced, sines, chain = r.sem(
            "loaded", "made", "taken", "sums", "roots", "heads", "turned", "turned_used", "reduced", "sines", "chain")
        TWO_PI = 2 * np.pi
        C1 = float(np.float32(6.28125))
        C2 = float(np.float32(np.float32((TWO_PI - C1) * 4096) // 1 / 4096))
        C3 = float(np.float32(TWO_PI - C1 - C2))
        MAGIC = 12582912.0
        with nc.Block() as block:
            @block.sync
            def _(sp):
                sp.dma_start(w_uq[:], w_uq_in.rearrange("(c p) n -> p c n", p=P)).then_inc(loaded, 16)
                sp.dma_start(w_ukv[:], w_ukv_in).then_inc(loaded, 16)
                sp.dma_start(gq[:], g["q_norm"].to_broadcast([P, QH])).then_inc(loaded, 16)
                sp.dma_start(gk[:], g["k_norm"].to_broadcast([P, QH])).then_inc(loaded, 16)
                sp.dma_start(pos_i[:], g["positions"]).then_inc(loaded, 16)
                sp.dma_start(freq[:], g["inv_freq"].to_broadcast([P, 16])).then_inc(loaded, 16)

            @block.tensor
            def _(pe):
                pe.wait_ge(loaded, 96)
                for t in range(TT):
                    tok = slice(t * P, t * P + P)
                    if t:
                        pe.wait_ge(taken, t)
                    for u, n0, n1 in ((0, 0, 384), (1, 384, 768)):
                        for c in range(2):
                            pe.matmul(ps[u][:, 0:384], cq[:, c, tok], w_uq[:, c, n0:n1], start=c == 0, stop=c == 1)
                    for u in range(2):
                        pe.matmul(ps[2 + u][:], ckv[:, 0, tok], w_ukv[:, u * 512:(u + 1) * 512], start=True, stop=True)
                    pe.transpose(pt[0][:, 0:P], z[:, Z_ROPE, tok], k.ident[:]).then_inc(made, 1)
                pe.wait_ge(taken, TT)
                for n in range(2 * MH):
                    src, h = (q, n) if n < MH else (kk, n - MH)
                    pe.wait_ge(heads, TT if n < MH else TT + 1)
                    if n >= 2:
                        pe.wait_ge(turned_used, n - 1)
                    for t in range(TT):
                        last = pe.transpose(pt[n % 2][0:QH, t * P:(t + 1) * P], src[:, t, h, :], k.ident[:])
                    last.then_inc(turned, 1)

            @block.scalar
            def _(act):
                act.wait_ge(sines, 2)
                act.activation(trig[:], trig[:], ACT.Sin).then_inc(sines, 1)
                act.wait_ge(sums, 4)
                act.activation(root[:], ss[:], ACT.Sqrt).then_inc(roots, 1)
                for n in range(2 * MH):
                    dst, h = (qT, n) if n < MH else (kT, n - MH)
                    act.wait_ge(turned, n + 1)
                    act.activation(dst[:, h, :], pt[n % 2][0:QH, :], ACT.Copy).then_inc(turned_used, 1)

            @block.vector
            def _(dve):
                link = Chain(dve, chain)
                dve.wait_ge(loaded, 96)
                link(dve.tensor_scalar(gq[:], gq[:], QH ** -0.5, None, ALU.mult))
                link(dve.tensor_copy(pos[:], pos_i[:]))
                link(dve.tensor_tensor(ang[:], bcast(pos[:], 16, 2), bcast(freq[:], TT, 1), ALU.mult))
                for j in range(2):
                    link(dve.tensor_scalar(turns[:], ang[:], 1 / TWO_PI, 0.25 * j, ALU.mult, ALU.add))
                    link(dve.tensor_scalar(turns[:], turns[:], MAGIC, None, ALU.add))
                    link(dve.tensor_scalar(turns[:], turns[:], MAGIC, None, ALU.subtract))
                    link(dve.scalar_tensor_tensor(trig[:, j], turns[:], -C1, ang[:], ALU.mult, ALU.add))
                    link(dve.scalar_tensor_tensor(trig[:, j], turns[:], -C2, trig[:, j], ALU.mult, ALU.add))
                    link(dve.scalar_tensor_tensor(trig[:, j], turns[:], -C3, trig[:, j], ALU.mult, ALU.add))
                    if j:
                        link(dve.tensor_scalar(trig[:, j], trig[:, j], np.pi / 2, None, ALU.add))
                    link.announce(dve.tensor_scalar(trig[:, j], trig[:, j], 3.1415925, -3.1415925, ALU.min, ALU.max), sines, j + 1)
                for t in range(TT):
                    dve.wait_ge(made, t + 1)
                    dve.tensor_copy(q[:, t, 0:4, :], ps[0][:, 0:384].rearrange("p (h d) -> p h d", h=4))
                    dve.tensor_copy(q[:, t, 4:8, :], ps[1][:, 0:384].rearrange("p (h d) -> p h d", h=4))
                    for u in range(2):
                        both = ps[2 + u][:].rearrange("p (h d) -> p h d", h=4)
                        dve.tensor_copy(kk[:, t, 4 * u:4 * u + 4, 0:NOPE], both[:, :, 0:NOPE])
                        dve.tensor_copy(v_tp[:, t, 4 * u:4 * u + 4, :], both[:, :, NOPE:NOPE + VH])
                    link.announce(dve.tensor_copy(kr[:, t, :], pt[0][:, 0:ROPE]), taken, t + 1)
                qg, kg = q[:].rearrange("p t h d -> p (t h) d"), kk[:].rearrange("p t h d -> p (t h) d")
                link(dve.tensor_tensor(sq[:], qg, qg, ALU.mult))
                link(dve.reduce_sum(ss[:, 0], sq[:, :, 0:NOPE], AX))
                link(dve.reduce_sum(ss[:, 1], sq[:, :, NOPE:QH], AX))
                link(dve.tensor_tensor(sq[:, :, 0:NOPE], kg[:, :, 0:NOPE], kg[:, :, 0:NOPE], ALU.mult))
                link(dve.reduce_sum(ss[:, 2], sq[:, :, 0:NOPE], AX))
                link(dve.tensor_tensor(sq[:, 0:TT, 0:ROPE], kr[:], kr[:], ALU.mult))
                link(dve.memset(ss[:, 3], 1.0))
                link(dve.reduce_sum(ss[:, 3, 0:TT], sq[:, 0:TT, 0:ROPE], AX))
                for j, n in enumerate((NOPE, ROPE, NOPE, ROPE)):
                    link.announce(dve.tensor_scalar(ss[:, j], ss[:, j], 1.0 / n, EPS, ALU.mult, ALU.add), sums, j + 1)
                dve.wait_ge(roots, 1)
                link(dve.reciprocal(ss[:], root[:]))
                TH = TT * MH
                link(dve.tensor_tensor(qg[:, :, 0:NOPE], qg[:, :, 0:NOPE], bcast(ss[:, 0], NOPE, 2), ALU.mult))
                link(dve.tensor_tensor(qg[:, :, NOPE:QH], qg[:, :, NOPE:QH], bcast(ss[:, 1], ROPE, 2), ALU.mult))
                link(dve.tensor_tensor(kg[:, :, 0:NOPE], kg[:, :, 0:NOPE], bcast(ss[:, 2], NOPE, 2), ALU.mult))
                link(dve.tensor_tensor(kr[:], kr[:], bcast(ss[:, 3, 0:TT], ROPE, 2), ALU.mult))
                link(dve.tensor_tensor(qg, qg, bcast(gq[:], TH, 1), ALU.mult))
                link(dve.tensor_tensor(kg[:, :, 0:NOPE], kg[:, :, 0:NOPE], bcast(gk[:, 0:NOPE], TH, 1), ALU.mult))
                link(dve.tensor_tensor(kr[:], kr[:], bcast(gk[:, NOPE:QH], TT, 1), ALU.mult))
                dve.wait_ge(sines, 3)
                r4 = rot.rearrange("p a (t h) n -> p a t h n", t=TT)
                for t in range(TT):
                    x1, x2 = q[:, t, :, NOPE:NOPE + 16], q[:, t, :, NOPE + 16:QH]
                    sin, cos = bcast(trig[:, 0, t], MH, 1), bcast(trig[:, 1, t], MH, 1)
                    dve.tensor_tensor(r4[:, 0, t], x1, cos, ALU.mult)
                    dve.tensor_tensor(r4[:, 1, t], x2, sin, ALU.mult)
                    dve.tensor_tensor(r4[:, 2, t], x1, sin, ALU.mult)
                    link(dve.tensor_tensor(r4[:, 3, t], x2, cos, ALU.mult))
                    dve.tensor_tensor(x1, r4[:, 0, t], r4[:, 1, t], ALU.subtract)
                    link.announce(dve.tensor_tensor(x2, r4[:, 2, t], r4[:, 3, t], ALU.add), heads, t + 1)
                x1, x2 = kr[:, :, 0:16], kr[:, :, 16:32]
                sin, cos = trig[:, 0], trig[:, 1]
                dve.tensor_tensor(rot[:, 0, 0:TT], x1, cos, ALU.mult)
                dve.tensor_tensor(rot[:, 1, 0:TT], x2, sin, ALU.mult)
                dve.tensor_tensor(rot[:, 2, 0:TT], x1, sin, ALU.mult)
                link(dve.tensor_tensor(rot[:, 3, 0:TT], x2, cos, ALU.mult))
                dve.tensor_tensor(x1, rot[:, 0, 0:TT], rot[:, 1, 0:TT], ALU.subtract)
                link(dve.tensor_tensor(x2, rot[:, 2, 0:TT], rot[:, 3, 0:TT], ALU.add))
                dve.tensor_copy(kk[:, :, :, NOPE:QH], bcast(kr[:], MH, 2)).then_inc(heads, 1)


def attention_stage(nc, name, k, items, heads, vdim, oT, sinks=None):
    per = P // vdim
    N = len(items)
    with ExitStack() as stack:
        r = Room(nc, stack, name)
        s = [r.sb(f"s{u}", [P, 512]) for u in range(2)]
        p = [r.sb(f"p{u}", [P, 512]) for u in range(2)]
        pT = [r.sb(f"pT{u}", [P, 512]) for u in range(2)]
        nmax, total, inv = r.sb("nmax", [P, N]), r.sb("total", [P, N]), r.sb("inv", [P, N])
        esink = r.sb("esink", [P, N])
        ps = [r.ps(f"ps{u}") for u in range(2)]
        pt = [r.ps(f"pt{u}") for u in range(2)]
        po = [r.ps(f"po{u}") for u in range(2)]
        scored, biased, maxed, exped, sunk, weighed, turned, copied, summed, taken, chain = r.sem(
            "scored", "biased", "maxed", "exped", "sunk", "weighed", "turned", "copied", "summed", "taken", "chain")
        with nc.Block() as block:
            @block.tensor
            def _(pe):
                def score(n):
                    q_ap, k_ap = items[n][0], items[n][1]
                    if n >= 2:
                        pe.wait_ge(biased, n - 1)
                    more, out = items[n][6], ps[n % 2][:, 0:k_ap.shape[-1]]
                    last = pe.matmul(out, q_ap, k_ap, start=True, stop=more is None)
                    if more is not None:
                        last = pe.matmul(out, more[0], more[1], start=False, stop=True)
                    last.then_inc(scored, 1)

                score(0)
                for n, (_, k_ap, _, vs, h, t, _) in enumerate(items):
                    if n + 1 < N:
                        score(n + 1)
                    pe.wait_ge(weighed, n + 1)
                    if n >= 2:
                        pe.wait_ge(copied, n - 1)
                    for j in range(len(vs)):
                        last = pe.transpose(pt[n % 2][:, j * P:(j + 1) * P], p[n % 2][:, j * P:(j + 1) * P], k.ident[:])
                    last.then_inc(turned, 1)
                    pe.wait_ge(copied, n + 1)
                    if n >= 2:
                        pe.wait_ge(taken, n - 1)
                    at = (h % per) * vdim
                    for j, v in enumerate(vs):
                        last = pe.matmul(po[n % 2][at:at + vdim, 0:P], v, pT[n % 2][:, j * P:(j + 1) * P],
                                         start=j == 0, stop=j == len(vs) - 1)
                    last.then_inc(summed, 1)

            @block.scalar
            def _(act):
                def copy(n):
                    w = items[n][1].shape[-1]
                    act.wait_ge(turned, n + 1)
                    if n >= 2:
                        act.wait_ge(summed, n - 1)
                    act.activation(pT[n % 2][:, 0:w], pt[n % 2][:, 0:w], ACT.Copy).then_inc(copied, 1)

                for n in range(N + 1):
                    if n < N:
                        w = items[n][1].shape[-1]
                        act.wait_ge(maxed, n + 1)
                        if n >= 2:
                            act.wait_ge(turned, n - 1)
                        act.activation(p[n % 2][:, 0:w], s[n % 2][:, 0:w], ACT.Exp, bias=nmax[:, n:n + 1],
                                       accum_out=total[:, n:n + 1]).then_inc(exped, 1)
                        if sinks is not None:
                            h = items[n][4]
                            act.activation(esink[:, n:n + 1], sinks[:, h:h + 1], ACT.Exp,
                                           bias=nmax[:, n:n + 1]).then_inc(sunk, 1)
                    if n >= 1:
                        copy(n - 1)

            @block.vector
            def _(dve):
                link = Chain(dve, chain)

                def take(n):
                    h, t = items[n][4], items[n][5]
                    at = (h % per) * vdim
                    dve.wait_ge(summed, n + 1)
                    dve.tensor_copy(oT[at:at + vdim, h // per, t * P:(t + 1) * P], po[n % 2][at:at + vdim, 0:P]).then_inc(taken, 1)

                def weigh(n):
                    w = items[n][1].shape[-1]
                    dve.wait_ge(exped, n + 1)
                    if sinks is not None:
                        dve.wait_ge(sunk, n + 1)
                        link(dve.tensor_tensor(total[:, n:n + 1], total[:, n:n + 1], esink[:, n:n + 1], ALU.add))
                    link(dve.reciprocal(inv[:, n:n + 1], total[:, n:n + 1]))
                    dve.tensor_scalar(p[n % 2][:, 0:w], p[n % 2][:, 0:w], inv[:, n:n + 1], None, ALU.mult).then_inc(weighed, 1)

                for n in range(N + 2):
                    if n < N:
                        bias, w, h = items[n][2], items[n][1].shape[-1], items[n][4]
                        dve.wait_ge(scored, n + 1)
                        if n >= 2:
                            dve.wait_ge(exped, n - 1)
                        if bias is None:
                            dve.tensor_copy(s[n % 2][:, 0:w], ps[n % 2][:, 0:w]).then_inc(biased, 1)
                        else:
                            b0 = w - bias.shape[-1]
                            if b0:
                                dve.tensor_copy(s[n % 2][:, 0:b0], ps[n % 2][:, 0:b0])
                            dve.tensor_tensor(s[n % 2][:, b0:w], ps[n % 2][:, b0:w], bias, ALU.add).then_inc(biased, 1)
                        dve.wait_ge(biased, n + 1)
                        link(dve.reduce_max(nmax[:, n:n + 1], s[n % 2][:, 0:w], AX))
                        if sinks is not None:
                            link(dve.tensor_tensor(nmax[:, n:n + 1], nmax[:, n:n + 1], sinks[:, h:h + 1], ALU.max))
                        dve.tensor_scalar(nmax[:, n:n + 1], nmax[:, n:n + 1], -1.0, None, ALU.mult).then_inc(maxed, 1)
                    if 1 <= n <= N:
                        weigh(n - 1)
                    if n >= 2:
                        take(n - 2)

def rwkv_prepare_stage(nc, k, z, g, cols, hT, KR, rk, sgate, mid_e, end_e):
    with ExitStack() as stack:
        r = Room(nc, stack, "rprep")
        d = r.sb("d", [P, 14, S])
        kk, kh, b = d[:, 0:4, :], d[:, 4:8, :], d[:, 8:12, :]
        ld, a, c, eprev = [r.sb(n, [P, RP, S]) for n in ("ld", "a", "c", "eprev")]
        einc, eneg = hT[:, 0:4, :], hT[:, 4:8, :]
        pair_ones, ones = k.pair_ones, k.ones
        lora, tw = rk[:, 0, :], rk[0:64, 1, :]
        ps = [r.ps(f"ps{u}") for u in range(8)]
        loaded, shifted, squashed, products, gated, used, squares, norms, roots, cums, exps, chain = r.sem(
            "loaded", "shifted", "squashed", "products", "gated", "used", "squares", "norms", "roots", "cums", "exps", "chain")
        with nc.Block() as block:
            @block.sync
            def _(sp):
                sp.dma_start(lora[0:64, :], g["w_decay_up"]).then_inc(loaded, 16)
                sp.dma_start(lora[64:128, :], g["w_aaa_up"]).then_inc(loaded, 16)

            @block.tensor
            def _(pe):
                pe.wait_ge(loaded, 32)
                pe.wait_ge(squashed, 1)
                for m in range(4):
                    pe.matmul(ps[m][:], lora[0:64, m * P:(m + 1) * P], tw, start=True, stop=True).then_inc(products, 1)
                for m in range(4):
                    pe.matmul(ps[4 + m][:], lora[64:128, m * P:(m + 1) * P], z[64:128, Z_WA, :], start=True, stop=True).then_inc(products, 1)
                pe.wait_ge(gated, 8)
                pe.wait_ge(squares, 1)
                for m in range(4):
                    pe.matmul(ps[m][:], pair_ones[:], c[:, m, :], start=True, stop=True).then_inc(norms, 1)

            @block.scalar
            def _(act):
                act.wait_ge(shifted, 1)
                act.activation(tw, z[0:64, Z_WA, :], ACT.Tanh).then_inc(squashed, 1)
                act.activation(sgate[:], z[:, Z_GD, :], ACT.Sigmoid)
                for m in range(8):
                    act.wait_ge(products, m + 1)
                    dst, base = (ld, cols("decay_base")) if m < 4 else (a, cols("aaa_base"))
                    act.activation(dst[:, m % 4, :], ps[m][:], ACT.Sigmoid, bias=base[:, m % 4:m % 4 + 1]).then_inc(gated, 1)
                for m in range(4):
                    act.wait_ge(norms, m + 1)
                    act.activation(eprev[:, m, :], ps[m][:], ACT.Sqrt).then_inc(roots, 1)
                act.wait_ge(cums, 1)
                act.activation(einc, c[:], ACT.Exp).then_inc(exps, 1)
                act.activation(eneg, c[:], ACT.Exp, scale=-1.0).then_inc(exps, 1)
                act.wait_ge(cums, 2)
                act.activation(eprev[:], ld[:], ACT.Exp).then_inc(exps, 1)
                act.activation(mid_e[:], mid_e[:], ACT.Exp).then_inc(exps, 1)

            @block.vector
            def _(dve):
                link = Chain(dve, chain)
                zs = z[:, Z_R:Z_GATE, :]
                link(dve.tensor_tensor(d[:, :, 1:S], zs[:, :, 0:S - 1], zs[:, :, 1:S], ALU.subtract))
                link(dve.tensor_scalar(d[:, :, 0:1], zs[:, :, 0:1], -1.0, None, ALU.mult))
                mu = cols("mu_shift")
                for m in range(14):
                    ins = dve.scalar_tensor_tensor(zs[:, m, :], d[:, m, :], mu[:, m:m + 1], zs[:, m, :], ALU.mult, ALU.add)
                link.announce(ins, shifted, 1)
                rr, kz = z[:, Z_R:Z_K, :], z[:, Z_K:Z_V, :]
                for m in range(4):
                    ins = dve.tensor_scalar(kk[:, m, :], kz[:, m, :], cols("k_k")[:, m:m + 1], None, ALU.mult)
                link(ins)
                dve.tensor_tensor(c[:], kk, kk, ALU.mult).then_inc(squares, 1)
                dve.wait_ge(gated, 8)
                for m in range(4):
                    ins = dve.tensor_scalar(kh[:, m, :], a[:, m, :], 1.0, cols("k_a")[:, m:m + 1], ALU.subtract, ALU.mult)
                link(ins)
                link(dve.scalar_tensor_tensor(kh, kh, 1.0, kz, ALU.add, ALU.mult))
                for m in range(4):
                    ins = dve.scalar_tensor_tensor(rk[:, m, :], rr[:, m, :], cols("r_k")[:, m:m + 1], kh[:, m, :], ALU.mult, ALU.mult)
                link(ins)
                dve.wait_ge(roots, 4)
                link(dve.tensor_scalar(eprev[:], eprev[:], 1e-12, None, ALU.max))
                link(dve.reciprocal(eprev[:], eprev[:]))
                link(dve.tensor_tensor(kk, kk, eprev[:], ALU.mult))
                link(dve.tensor_tensor(b, kk, a[:], ALU.mult))
                link(dve.tensor_scalar(ld[:], ld[:], -float(np.exp(-0.5)), None, ALU.mult))
                for m in range(RP):
                    for t in range(TT):
                        seg = slice(t * P, t * P + P)
                        ins = dve.tensor_tensor_scan(c[:, m, seg], ones[:], ld[:, m, seg], 0.0, ALU.mult, ALU.add)
                link(ins)
                c3, ld3 = c[:].rearrange("p m (t n) -> p (m t) n", n=P), ld[:].rearrange("p m (t n) -> p (m t) n", n=P)
                link(dve.tensor_copy(mid_e[:], c3[:, :, P // 2 - 1]))
                ins = dve.tensor_tensor(c3, c3, bcast(mid_e[:], P, 2), ALU.subtract)
                link.announce(ins, cums, 1)
                link.announce(dve.tensor_tensor(ld[:], c[:], ld[:], ALU.subtract), cums, 2)
                dve.wait_ge(exps, 1)
                cut = lambda ap: ap.rearrange("p m (t n) -> p m t n", n=P)
                link(dve.tensor_tensor(KR[:, :, :, 1, :], cut(rr), cut(einc), ALU.mult))
                dve.tensor_copy(end_e[:], einc.rearrange("p m (t n) -> p (m t) n", n=P)[:, :, P - 1])
                dve.wait_ge(exps, 2)
                dve.tensor_tensor(rr, b, eneg, ALU.mult)
                dve.tensor_tensor(kz, kh, eneg, ALU.mult)
                dve.wait_ge(exps, 3)
                dve.tensor_tensor(KR[:, :, :, 0, :], cut(kk), cut(eprev[:]), ALU.mult)


def rwkv_turn_stage(nc, k, z, g, KR, rk, kkT, bT, kdT, vT, bonus):
    with ExitStack() as stack:
        r = Room(nc, stack, "rturn")
        pt = [r.ps(f"pt{u}") for u in range(4)]
        pb = r.ps("pb")
        sel = r.sb("sel", [P, 2])
        loaded, turned, copied, summed = r.sem("loaded", "turned", "copied", "summed")
        kz, rr, vz = z[:, Z_K:Z_V, :], z[:, Z_R:Z_K, :], z[:, Z_V:Z_WA, :]
        units = [(src, dst, m) for src, dst in ((vz, vT), (rr, bT), (None, kkT), (kz, kdT)) for m in range(RP)]
        with nc.Block() as block:
            @block.sync
            def _(sp):
                sp.dma_start(sel[:], g["pair_sel"]).then_inc(loaded, 16)

            @block.tensor
            def _(pe):
                for n, (src, _, m) in enumerate(units):
                    if n >= 4:
                        pe.wait_ge(copied, n - 3)
                    for t in range(TT):
                        data = KR[:, m, t, 0, :] if src is None else src[:, m, t * P:(t + 1) * P]
                        last = pe.transpose(pt[n % 4][:, t * P:(t + 1) * P], data, k.ident[:])
                    last.then_inc(turned, 1)
                pe.wait_ge(loaded, 16)
                for t in range(TT):
                    for m in range(RP):
                        last = pe.matmul(pb[:, t * 8 + 2 * m:t * 8 + 2 * m + 2], rk[:, m, t * P:(t + 1) * P], sel[:], start=True, stop=True)
                last.then_inc(summed, 1)

            @block.vector
            def _(dve):
                for n, (_, dst, m) in enumerate(units):
                    dve.wait_ge(turned, max(n + 1, RP + 1 if n >= 3 * RP else 0))
                    dve.tensor_copy(dst[:, m, :, :], pt[n % 4][:].rearrange("p (t n) -> p t n", n=P)).then_inc(copied, 1)
                dve.wait_ge(summed, 1)
                dve.tensor_copy(bonus[:], pb[:, 0:TT * RH].rearrange("p (t h) -> p t h", h=RH))


def rwkv_solve_stage(nc, k, g, KR, Bd, Kd, kkT, bT, kdT, vT, mid_e, end_e, y):
    with ExitStack() as stack:
        r = Room(nc, stack, "rsolve")
        masks = r.sb("masks", [P, 5, P])
        MdT, Md, Moff, T, A2T, A3T, A4T, Pa, Pb, Pc, Pd = [
            r.sb(n, [P, RH, P]) for n in ("MdT", "Md", "Moff", "T", "A2T", "A3T", "A4T", "Pa", "Pb", "Pc", "Pd")]
        state = r.sb("state", [P, RP, RN])
        id64 = r.sb("id64", [P, RN])
        escale = r.sb("escale", [P, RP, TT])
        bank = [r.ps(f"bank{u}") for u in range(8)]
        loaded, made, taken, ready = r.sem("loaded", "made", "taken", "ready")
        STEPS = 27
        N, NT, X, X1, WU, RtT, PTI, Z = Md, MdT, Moff, Md, MdT, Pa, Pb, Pd

        def products(pe, c, step, h, out):
            o, m = divmod(h, 4)
            half = slice(o * RN, o * RN + RN)
            seg = slice(c * P, c * P + P)
            KKd, Rd = KR[half, m, c, 0, :], KR[half, m, c, 1, :]
            bd, kd = Bd[half, m, seg], Kd[half, m, seg]
            V, bt, kt = [x[:, m, c, half] for x in (vT, bT, kdT)]
            U0, W = WU[:, h, RN:P], WU[:, h, 0:RN]
            s0 = state[half, m, :]
            table = {
                0: [(bd, KKd)], 1: [(KKd, bd)], 2: [(kd, KKd)], 3: [(bd, Rd)], 4: [(kd, Rd)],
                5: [(MdT[:, h], Md[:, h])], 6: [(Md[:, h], MdT[:, h])], 7: [(Pa[:, h], T[:, h])],
                8: [(Pb[:, h], Pa[:, h])], 9: [(Pa[:, h], Pb[:, h])], 10: [(Pc[:, h], T[:, h])],
                11: [(Pd[:, h], Pc[:, h])], 12: [(Pa[:, h], T[:, h])],
                13: [(T[:, h], Moff[:, h])], 14: [(Moff[:, h], T[:, h])],
                15: [(NT[:, h], N[:, h])], 16: [(N[:, h], NT[:, h])], 17: [(Pa[:, h], Z[:, h])],
                18: [(Pb[:, h], Pa[:, h])], 19: [(Pc[:, h], Z[:, h])],
                20: [(A2T[:, h], V)], 21: [(T[:, h], X[:, h])], 22: [(Z[:, h], X1[:, h])],
                23: [(W, A3T[:, h])], 24: [(W, bt)],
                25: [(A3T[:, h], U0), (A4T[:, h], V), (RtT[half, m, :], s0)],
                26: [(bt, U0), (kt, V), (PTI[half, m, 0:RN], s0)],
            }[step]
            for n, (lhs, rhs) in enumerate(table):
                last = pe.matmul(out, lhs, rhs, start=n == 0, stop=n == len(table) - 1)
            return last

        def out_of(step, h, ps):
            o, m = divmod(h, 4)
            rows = slice(o * RN, o * RN + RN) if step in (23, 24, 26) else slice(0, P)
            return ps[rows, m * P:m * P + (RN if step in (20, 24, 25, 26) else P)]

        with nc.Block() as block:
            @block.sync
            def _(sp):
                sp.dma_start(masks[:], g["masks"].rearrange("m p n -> p m n")).then_inc(loaded, 16)
                sp.dma_start(id64[:], g["id64"]).then_inc(loaded, 16)

            @block.tensor
            def _(pe):
                pe.wait_ge(ready, 1)
                n = 0
                for c in range(TT):
                    for step in range(STEPS):
                        for hf in range(2):
                            if n >= 2:
                                pe.wait_ge(taken, n - 1)
                            for h in range(4 * hf, 4 * hf + 4):
                                last = products(pe, c, step, h, out_of(step, h, bank[n % 8]))
                            last.then_inc(made, 1)
                            n += 1

            @block.vector
            def _(dve):
                dve.wait_ge(loaded, 32)
                dve.memset(state[:], 0.0)
                dve.tensor_copy(escale[:, :, TT - 1:TT], end_e[:].rearrange("p (m t) -> p m t", t=TT)[:, :, TT - 1:TT])
                dve.tensor_tensor(escale[:, :, 0:TT - 1], end_e[:].rearrange("p (m t) -> p m t", t=TT)[:, :, 0:TT - 1],
                                  mid_e[:].rearrange("p (m t) -> p m t", t=TT)[:, :, 1:TT], ALU.mult).then_inc(ready, 1)
                dve.wait_ge(ready, 1)
                mask = lambda j: bcast(masks[:, j, :], 4, 1)
                ident = bcast(k.ident[:], 4, 1)
                n = 0
                for c in range(TT):
                    for step in range(STEPS):
                        for hf in range(2):
                            hs, half = slice(4 * hf, 4 * hf + 4), slice(RN * hf, RN * hf + RN)
                            full = bank[n % 8][:].rearrange("p (h n) -> p h n", n=P)
                            dve.wait_ge(made, n + 1)
                            tt, cp = dve.tensor_tensor, dve.tensor_copy
                            if step == 0:
                                tt(MdT[:, hs], full, mask(0), ALU.mult).then_inc(ready, 1)
                                dve.wait_ge(ready, 2 + 2 * c + hf)
                                ins = tt(T[:, hs], MdT[:, hs], ident, ALU.add)
                            elif step == 1:
                                tt(Md[:, hs], full, mask(1), ALU.mult)
                                ins = tt(Moff[:, hs], full, mask(2), ALU.mult)
                            elif step == 2:
                                ins = tt(A2T[:, hs], full, mask(3), ALU.mult)
                            elif step in (3, 4):
                                ins = tt((A3T if step == 3 else A4T)[:, hs], full, mask(4), ALU.mult)
                            elif step in (7, 10, 12):
                                ins = tt(T[:, hs], full, T[:, hs], ALU.add)
                            elif step in (17, 19):
                                ins = tt(Z[:, hs], full, Z[:, hs], ALU.add)
                            elif step in (5, 6, 8, 9, 11, 13, 15, 16, 18, 21):
                                dst = {5: Pa, 6: Pb, 8: Pc, 9: Pd, 11: Pa, 13: N, 15: Pa, 16: Pb, 18: Pc, 21: X1}[step]
                                ins = cp(dst[:, hs], full)
                            elif step == 14:
                                cp(NT[:, hs], full)
                                ins = tt(Z[:, hs], full, ident, ALU.add)
                            elif step == 20:
                                cp(X[:, hs, 0:RN], kkT[:, :, c, half])
                                ins = cp(X[:, hs, RN:P], full[:, :, 0:RN])
                            elif step == 22:
                                ins = dve.tensor_scalar(WU[:, hs], full, -1.0, None, ALU.mult)
                            elif step == 23:
                                ins = tt(RtT[half, 0:4], full[half], KR[half, :, c, 1, :], ALU.add)
                            elif step == 24:
                                ins = tt(PTI[half, 0:4, 0:RN], full[half, :, 0:RN], bcast(id64[half], 4, 1), ALU.add)
                            elif step == 25:
                                ins = cp(y[:, c].rearrange("p (m o) n -> p m o n", o=2)[:, :, hf, :], full[:, :, 0:RN])
                            else:
                                for m in range(RP):
                                    ins = dve.tensor_scalar(state[half, m, :], full[half, m, 0:RN], escale[half, m, c:c + 1], None, ALU.mult)
                            ins.then_inc(taken, 1)
                            n += 1


def rwkv_finish_stage(nc, k, g, y, v_tp, bonus, sgate, oT, bufs):
    with ExitStack() as stack:
        r = Room(nc, stack, "rfin")
        lnw, lnb, wg = r.sb("lnw", [P, S]), r.sb("lnb", [P, S]), r.sb("wg", [P, S])
        mean, var, root = [r.sb(n, [P, TT * RH]) for n in ("mean", "var", "root")]
        sq = r.sb("sq", [P, TT * RH, RN])
        ps = [r.ps(f"ps{u}") for u in range(8)]
        loaded, gates, vars_, roots, rows, turned, chain = r.sem("loaded", "gates", "vars", "roots", "rows", "turned", "chain")
        with nc.Block() as block:
            @block.sync
            def _(sp):
                sp.dma_start(lnw[:], g["ln_x_w"].to_broadcast([P, S])).then_inc(loaded, 16)
                sp.dma_start(lnb[:], g["ln_x_b"].to_broadcast([P, S])).then_inc(loaded, 16)
                sp.dma_start(wg[:], g["w_gate_up"]).then_inc(loaded, 16)

            @block.tensor
            def _(pe):
                pe.wait_ge(loaded, 48)
                for t in range(TT):
                    pe.matmul(ps[t][:], sgate[:, t * P:(t + 1) * P], wg[:], start=True, stop=True).then_inc(gates, 1)
                for m in range(4):
                    pe.wait_ge(rows, TT)
                    for t in range(TT):
                        last = pe.transpose(ps[4 + m][:, t * P:(t + 1) * P], y[:, t, 2 * m:2 * m + 2, :].rearrange("p h n -> p (h n)"), k.ident[:])
                    last.then_inc(turned, 1)

            @block.scalar
            def _(act):
                act.wait_ge(vars_, 1)
                act.activation(root[:], var[:], ACT.Sqrt).then_inc(roots, 1)
                for m in range(4):
                    act.wait_ge(turned, m + 1)
                    act.activation(oT[:, m, :], ps[4 + m][:], ACT.Copy)

            @block.vector
            def _(dve):
                link = Chain(dve, chain)
                yg = y[:].rearrange("p t h n -> p (t h) n")
                link(dve.reduce_sum(mean[:], yg, AX))
                link(dve.tensor_scalar(mean[:], mean[:], 1.0 / RN, None, ALU.mult))
                link(dve.tensor_tensor(yg, yg, bcast(mean[:], RN, 2), ALU.subtract))
                link(dve.tensor_tensor(sq[:], yg, yg, ALU.mult))
                link(dve.reduce_sum(var[:], sq[:], AX))
                dve.tensor_scalar(var[:], var[:], 1.0 / RN, GN_EPS, ALU.mult, ALU.add).then_inc(vars_, 1)
                dve.wait_ge(roots, 1)
                link(dve.reciprocal(root[:], root[:]))
                link(dve.tensor_tensor(yg, yg, bcast(root[:], RN, 2), ALU.mult))
                dve.wait_ge(loaded, 48)
                yt = y[:].rearrange("p t h n -> p t (h n)")
                link(dve.tensor_tensor(yt, yt, bcast(lnw[:], TT, 1), ALU.mult))
                link(dve.tensor_tensor(yt, yt, bcast(lnb[:], TT, 1), ALU.add))
                v4 = v_tp.rearrange("p m t (o n) -> p m t o n", n=RN)
                s4 = sq[:].rearrange("p (t m o) n -> p t m o n", m=RP, o=2)
                b4 = bonus[:].rearrange("p t (m o) -> p t m o", o=2)
                for t in range(TT):
                    ins = dve.tensor_tensor(s4[:, t], v4[:, :, t], bcast(b4[:, t], RN, 3), ALU.mult)
                link(ins)
                link(dve.tensor_tensor(yg, yg, sq[:], ALU.add))
                for t in range(TT):
                    dve.wait_ge(gates, t + 1)
                    dve.tensor_tensor(yt[:, t], yt[:, t], ps[t][:], ALU.mult).then_inc(rows, 1)


def merge_stage(nc, name, z, gate0, branches, out, kc=4):
    nb = len(branches)
    with ExitStack() as stack:
        r = Room(nc, stack, name)
        w = [[r.sb(f"w{i}_{u}", [P, kc, P]) for u in range(2)] for i in range(nb)]
        part = r.sb("part", [P, nb, S])
        ps = [[r.ps(f"ps{i}_{u}") for u in range(2)] for i in range(nb)]
        made, taken, chain = r.sem("made", "taken", "chain")
        w_ready = [[r.sem(f"w_ready{i}_{u}") for u in range(2)] for i in range(nb)]
        srcs = [w_dram.rearrange("(c p) (m n) -> m p c n", p=P, n=P) for w_dram, _ in branches]
        with nc.Block() as block:
            @block.sync
            def _(sp):
                for m in range(DC):
                    for i in range(nb):
                        if m >= 2:
                            sp.wait_ge(made, nb * (m - 2) + i + 1)
                        sp.dma_start(w[i][m % 2][:], srcs[i][m]).then_inc(w_ready[i][m % 2], 16)

            @block.tensor
            def _(pe):
                for m in range(DC):
                    for i, (_, o) in enumerate(branches):
                        pe.wait_ge(w_ready[i][m % 2], 16 * (m // 2 + 1))
                        if m >= 2:
                            pe.wait_ge(taken, m - 1)
                        for c in range(kc):
                            last = pe.matmul(ps[i][m % 2][:], w[i][m % 2][:, c, :], o[:, c, :], start=c == 0, stop=c == kc - 1)
                        last.then_inc(made, 1)

            @block.vector
            def _(dve):
                link = Chain(dve, chain)
                for m in range(DC):
                    for i in range(nb):
                        dve.wait_ge(made, nb * m + i + 1)
                        ins = dve.tensor_tensor(part[:, i, :], ps[i][m % 2][:], z[:, gate0 + i * DC + m, :], ALU.mult)
                        if i == nb - 1:
                            ins.then_inc(taken, 1)
                            dve.wait_ge(taken, m + 1)
                    for i in range(1, nb):
                        last = i == nb - 1
                        link(dve.tensor_tensor(out[:, m, :] if last else part[:, 0, :], part[:, 0, :], part[:, i, :], ALU.add))


def squash_stage(nc, name, z, c0, n, bias=None):
    with nc.Block() as block:
        @block.scalar
        def _(act):
            for m in range(n):
                extra = {} if bias is None else {"bias": bias[:, m:m + 1]}
                act.activation(z[:, c0 + m, :], z[:, c0 + m, :], ACT.Sigmoid, **extra)

def choose_stage(nc, name, k, g, qT, keys_in, keys_of, e1T, e2T, gT):
    with ExitStack() as stack:
        r = Room(nc, stack, name)
        nkeys = keys_in.shape[1]
        keys = r.sb("keys", [P, nkeys, NK])
        v, idx, left = r.sb("v", [P, 2 * PH, K16]), r.sb("idx", [P, 2 * PH, K16], U32), r.sb("left", [P, 2, NK])
        idf = r.sb("idf", [P, 2 * PH, K16])
        cand, cleft = r.sb("cand", [P, PH, 256]), r.sb("cleft", [P, PH, 256])
        tv, pos = r.sb("tv", [P, PH, K16]), r.sb("pos", [P, PH, K16], U32)
        part, partf = r.sb("part", [P, 2, PH * K16], U32), r.sb("partf", [P, 2, PH * K16])
        iota, hit = r.sb("iota", [P, K16]), r.sb("hit", [P, PH * K16, K16])
        found = r.sb("found", [P, 2, 3, NJ])
        total = r.sb("total", [P, PH])
        ps = [r.ps(f"ps{u}") for u in range(4)]
        pt = r.ps("pt")
        loaded, scored, read, centred, exped, chosen, turned, kept, chain = r.sem(
            "loaded", "scored", "read", "centred", "exped", "chosen", "turned", "kept", "chain")
        scores = lambda c: ps[c // 4][:, (c % 4) * NK:(c % 4 + 1) * NK]
        with nc.Block() as block:
            @block.sync
            def _(sp):
                sp.dma_start(keys[:], keys_in).then_inc(loaded, 16)
                sp.dma_start(iota[:], g["iota16"].to_broadcast([P, K16])).then_inc(loaded, 16)

            @block.tensor
            def _(pe):
                pe.wait_ge(loaded, 32)
                for t in range(TT + 1):
                    if t:
                        pe.wait_ge(read, t)
                    for c in range(2 * PH if t < TT else 0):
                        last = pe.matmul(scores(c), qT[:, c, t * P:(t + 1) * P], keys[:, keys_of(c), :], start=True, stop=True)
                    if t < TT:
                        last.then_inc(scored, 1)
                    if t:
                        pe.wait_ge(chosen, t)
                        if t > 1:
                            pe.wait_ge(kept, t - 1)
                        for j in range(3):
                            last = pe.transpose(pt[:, j * P:(j + 1) * P], found[:, (t - 1) % 2, j, :], k.ident[:])
                        last.then_inc(turned, 1)

            @block.scalar
            def _(act):
                for t in range(TT):
                    act.wait_ge(centred, t + 1)
                    act.activation(tv[:], tv[:], ACT.Exp).then_inc(exped, 1)
                    act.wait_ge(turned, t + 1)
                    for j, dst in enumerate((e1T, e2T, gT)):
                        ins = act.activation(dst[:, t * P:(t + 1) * P], pt[:, j * P:(j + 1) * P], ACT.Copy)
                    ins.then_inc(kept, 1)

            @block.vector
            def _(dve):
                link = Chain(dve, chain)
                dve.wait_ge(loaded, 32)
                for t in range(TT):
                    def top16(vals, index, data, rest):
                        link(dve.max(vals[:, 0:8], data))
                        link(dve.max_index(index[:, 0:8], vals[:, 0:8], data))
                        link(dve.match_replace(rest, vals[:, 0:8], data, -3e38))
                        link(dve.max(vals[:, 8:16], rest))
                        link(dve.max_index(index[:, 8:16], vals[:, 8:16], rest))

                    dve.wait_ge(scored, t + 1)
                    for c in range(2 * PH):
                        top16(v[:, c], idx[:, c], scores(c), left[:, c % 2, :])
                    link.eng.sem_inc(read, 1)
                    v4 = v[:].rearrange("p (h s) n -> p h s n", s=2)
                    link(dve.tensor_tensor(cand[:].rearrange("p h (a b) -> p h a b", b=K16),
                                           bcast(v4[:, :, 0, :], K16, 3), bcast(v4[:, :, 1, :], K16, 2), ALU.add))
                    for h in range(PH):
                        top16(tv[:, h], pos[:, h], cand[:, h], cleft[:, h])
                    posf = pos[:].rearrange("p h n -> p (h n)")
                    link(dve.tensor_single_scalar(part[:, 0], posf, 4, ALU.logical_shift_right))
                    link(dve.tensor_single_scalar(part[:, 1], posf, 15, ALU.bitwise_and))
                    link(dve.tensor_copy(partf[:], part[:]))
                    link(dve.tensor_copy(idf[:], idx[:]))
                    ins = dve.tensor_copy(total[:], tv[:, :, 0])
                    link(ins)
                    id4 = idf[:].rearrange("p (h s) n -> p h s n", s=2)
                    hit4 = hit[:].rearrange("p (h n) a -> p h n a", h=PH)
                    if t >= 2:
                        dve.wait_ge(turned, t - 1)
                    for s in range(2):
                        link(dve.tensor_tensor(hit[:], bcast(partf[:, s], K16, 2), bcast(iota[:], NJ, 1), ALU.is_equal))
                        link(dve.tensor_tensor(hit4, hit4, bcast(id4[:, :, s, :], K16, 2), ALU.mult))
                        link(dve.reduce_sum(found[:, t % 2, s, :], hit[:], AX))
                    dve.tensor_tensor(tv[:], tv[:], bcast(total[:], K16, 2), ALU.subtract).then_inc(centred, 1)
                    dve.wait_ge(exped, t + 1)
                    link(dve.reduce_sum(total[:], tv[:], AX))
                    link(dve.reciprocal(total[:], total[:]))
                    dve.tensor_tensor(found[:, t % 2, 2, :].rearrange("p (h n) -> p h n", h=PH), tv[:], bcast(total[:], K16, 2), ALU.mult).then_inc(chosen, 1)


def spread_stage(nc, name, g, e1T, e2T, gT, gates_dram):
    with ExitStack() as stack:
        r = Room(nc, stack, name)
        iota = r.sb("iota", [P, NK])
        oh1, oh2 = [[r.sb(f"oh{x}_{u}", [P, 4, NK]) for u in range(2)] for x in (1, 2)]
        tile = [r.sb(f"tile{u}", [P, NK, SUB]) for u in range(2)]
        ps = [r.ps(f"ps{u}") for u in range(4)]
        loaded, hot1, hot2, made, kept = r.sem("loaded", "hot1", "hot2", "made", "kept")
        stored = [r.sem(f"stored{u}") for u in range(2)]
        GROUPS = SUB // 4
        with nc.Block() as block:
            @block.sync
            def _(sp):
                sp.dma_start(iota[:], g["iota128"].to_broadcast([P, NK])).then_inc(loaded, 16)
                for u in range(2):
                    sp.sem_inc(stored[u], 16)
                with sp.Fori(0, S // SUB // 2) as i:
                    for u in range(2):
                        sp.wait_ge(kept, 2 * GROUPS * i + GROUPS * (u + 1) + 4)
                        sp.dma_start(gates_dram[ds(2 * i + u, 1)].rearrange("a p e t -> (a p) e t"), tile[u][:]).then_inc(stored[u], 16)
                for u in range(2):
                    sp.wait_ge(stored[u], 16 * (S // SUB // 2) + 16)

            def turns(eng, body):
                with eng.Fori(0, S // SUB // 2) as i:
                    for u in range(2):
                        if eng is acting[0]:
                            eng.wait_ge(stored[u], 16 * i + 16)
                        with eng.Fori(0, GROUPS // 4) as j:
                            for b in range(4):
                                body(2 * GROUPS * i + GROUPS * u + 4 * j + b, u, 4 * j + b, b)

            acting = [None]

            @block.vector
            def _(dve):
                dve.wait_ge(loaded, 16)

                def body(n, u, q, b):
                    dve.wait_ge(made, n + 1)
                    for x in range(4):
                        tok = ds(4 * n + x, 1)
                        ins = dve.tensor_scalar(oh1[b % 2][:, x, :], iota[:], e1T[:, tok], gT[:, tok], ALU.is_equal, ALU.mult)
                    ins.then_inc(hot1, 1)
                    for x in range(4):
                        tok = ds(4 * n + x, 1)
                        ins = dve.tensor_scalar(oh2[b % 2][:, x, :], iota[:], e2T[:, tok], None, ALU.is_equal)
                    ins.then_inc(hot2, 1)

                turns(dve, body)

            @block.tensor
            def _(pe):
                def body(n, u, q, b):
                    pe.wait_ge(hot1, n + 1)
                    pe.wait_ge(hot2, n + 1)
                    pe.wait_ge(kept, n + 1)
                    for x in range(4):
                        last = pe.matmul(ps[b][:, x * NK:(x + 1) * NK], oh2[b % 2][:, x, :], oh1[b % 2][:, x, :], start=True, stop=True)
                    last.then_inc(made, 1)

                pe.sem_inc(made, 2)
                turns(pe, body)

            @block.scalar
            def _(act):
                acting[0] = act

                def body(n, u, q, b):
                    act.wait_ge(made, n + 3)
                    act.activation(tile[u][:, :, ds(q * 4, 4)].rearrange("p e t -> p t e"),
                                   ps[b][:].rearrange("p (t e) -> p t e", e=NK), ACT.Copy).then_inc(kept, 1)

                act.sem_inc(kept, 4)
                turns(act, body)


def wait_above(eng, sem, value):
    if not isinstance(value, int) or value > 0:
        eng.wait_ge(sem, value)


def experts_stage(nc, name, k, hT, downT, up, gates_dram, acc, gelu):
    NB = NK
    IT = NB // 8
    with ExitStack() as stack:
        r = Room(nc, stack, name)
        hhi, hlo = r.sb("hhi", [P, DC, S], F32R), r.sb("hlo", [P, DC, S], F32R)
        uraw, uhi, ulo = [[r.sb(f"{n}{u}", [P, DC, P], dt) for u in range(2)] for n, dt in (("uraw", F32), ("uhi", F32R), ("ulo", F32R))]
        vraw = [r.sb(f"vraw{u}", [P, D]) for u in range(2)]
        vhi, vlo = r.sb("vhi", [P, 4, D], F32R), r.sb("vlo", [P, 4, D], F32R)
        gate = [r.sb(f"gate{u}", [P, S // SUB, 4, SUB]) for u in range(2)]
        actv = [r.sb(f"act{u}", [P, S]) for u in range(2)]
        wfull = [r.sb(f"w{u}", [P, S]) for u in range(2)]
        whi, wlo = [[r.sb(f"{n}{u}", [P, 4, S], F32R) for u in range(2)] for n in ("whi", "wlo")]
        pa = [r.ps(f"pa{u}") for u in range(2)]
        po = [r.ps(f"po{u}") for u in range(4)]
        u_hi, u_lo, v_hi, v_lo, a_made, act_made, w_made, w_hi, w_lo, o_made, o_added, h_hi, h_lo = r.sem(
            "u_hi", "u_lo", "v_hi", "v_lo", "a_made", "act_made", "w_made", "w_hi", "w_lo", "o_made", "o_added", "h_hi", "h_lo")
        u_in, v_in, g_in = [[r.sem(f"{n}{u}") for u in range(2)] for n in ("u_in", "v_in", "g_in")]

        def loop(eng, body):
            body(0)
            with eng.Fori(1, IT - 1) as i:
                body(i)
            body(IT - 1)

        last_turn = lambda i: isinstance(i, int) and i == IT - 1

        with nc.Block() as block:
            @block.sync
            def _(sp):
                def body(i):
                    for j in range(8):
                        n = 8 * i + j
                        if j % 4 == 0:
                            grp, gp = 2 * i + j // 4, j // 4
                            wait_above(sp, w_made, 4 * grp - 4)
                            src = gates_dram[:, :, ds(4 * grp, 4), :] if not isinstance(grp, int) else gates_dram[:, :, 4 * grp:4 * grp + 4, :]
                            sp.dma_start(gate[gp][:], src.rearrange("s p e t -> p s e t")).then_inc(g_in[gp], 16)
                        wait_above(sp, u_lo, n - 1)
                        src = downT[n] if isinstance(n, int) else downT[ds(n, 1)].rearrange("a p c e -> (a p) c e")
                        sp.dma_start(uraw[j % 2][:], src).then_inc(u_in[j % 2], 16)
                        wait_above(sp, v_lo, n - 1)
                        src = up[n] if isinstance(n, int) else up[ds(n, 1)].rearrange("a p d -> (a p) d")
                        sp.dma_start(vraw[j % 2][:], src).then_inc(v_in[j % 2], 16)

                loop(sp, body)

            @block.scalar
            def _(act):
                def split_u(n, j):
                    act.wait_ge(u_in[j % 2], 8 * n + 16 - 8 * (j % 2))
                    wait_above(act, a_made, n - 1)
                    act.activation(uhi[j % 2][:], uraw[j % 2][:], ACT.Copy).then_inc(u_hi, 1)

                def split_v(n, j):
                    act.wait_ge(v_in[j % 2], 8 * n + 16 - 8 * (j % 2))
                    wait_above(act, o_made, 2 * (n - j % 4))
                    act.activation(vhi[:, j % 4, :], vraw[j % 2][:], ACT.Copy).then_inc(v_hi, 1)

                def body(i):
                    for j in range(8):
                        n = 8 * i + j
                        if not (last_turn(i) and j == 7):
                            split_u(n + 1, (j + 1) % 8)
                        act.wait_ge(a_made, n + 1)
                        wait_above(act, w_made, n - 1)
                        act.activation(actv[j % 2][:], pa[j % 2][:], gelu).then_inc(act_made, 1)
                        act.wait_ge(w_made, n + 1)
                        act.activation(whi[j // 4][:, j % 4, :], wfull[j % 2][:], ACT.Copy).then_inc(w_hi, 1)
                        if j % 4 == 1:
                            split_v(n - 1, j - 1)
                        if j % 4:
                            split_v(n, j)

                for c in range(DC):
                    act.activation(hhi[:, c, :], hT[:, c, :], ACT.Copy).then_inc(h_hi, 1)
                split_u(0, 0)
                loop(act, body)

            @block.gpsimd
            def _(pool):
                def body(i):
                    for j in range(8):
                        n = 8 * i + j
                        pool.wait_ge(v_hi, n + 1)
                        pool.tensor_tensor(vlo[:, j % 4, :], vraw[j % 2][:], vhi[:, j % 4, :].bitcast(F32), ALU.subtract).then_inc(v_lo, 1)

                with pool.Fori(0, IT) as i:
                    body(i)

            @block.vector
            def _(dve):
                def split_u(n, j):
                    dve.wait_ge(u_hi, n + 1)
                    dve.tensor_tensor(ulo[j % 2][:], uraw[j % 2][:], uhi[j % 2][:].bitcast(F32), ALU.subtract).then_inc(u_lo, 1)

                def add_group(grp):
                    for d in range(DC):
                        dve.wait_ge(o_made, 8 * grp + d + 1)
                        dve.tensor_tensor(acc[:, d, :], po[d % 4][:], acc[:, d, :], ALU.add).then_inc(o_added, 1)

                def body(i):
                    for j in range(8):
                        n, grp = 8 * i + j, 2 * i + j // 4
                        if not (last_turn(i) and j == 7):
                            split_u(n + 1, (j + 1) % 8)
                        if j % 4 == 0:
                            dve.wait_ge(g_in[j // 4], 16 * i + 16)
                        dve.wait_ge(act_made, n + 1)
                        wait_above(dve, w_lo, n - 1)
                        q3 = lambda ap: ap.rearrange("p (s t) -> p s t", t=SUB)
                        dve.tensor_tensor(q3(wfull[j % 2][:]), q3(actv[j % 2][:]), gate[j // 4][:, :, j % 4, :], ALU.mult).then_inc(w_made, 1)
                        dve.wait_ge(w_hi, n + 1)
                        dve.tensor_tensor(wlo[j // 4][:, j % 4, :], wfull[j % 2][:], whi[j // 4][:, j % 4, :].bitcast(F32), ALU.subtract).then_inc(w_lo, 1)
                        if j % 4 == 0 and not (isinstance(n, int) and n == 0):
                            add_group(grp - 1)

                dve.memset(acc[:], 0.0)
                for c in range(DC):
                    dve.wait_ge(h_hi, c + 1)
                    dve.tensor_tensor(hlo[:, c, :], hT[:, c, :], hhi[:, c, :].bitcast(F32), ALU.subtract).then_inc(h_lo, 1)
                split_u(0, 0)
                loop(dve, body)
                add_group(NB // 4 - 1)

            @block.tensor
            def _(pe):
                def down(n, j):
                    pe.wait_ge(u_lo, n + 1)
                    wait_above(pe, act_made, n - 1)
                    a = pa[j % 2][:]
                    for c in range(DC):
                        hi, lo = uhi[j % 2][:, c, :], ulo[j % 2][:, c, :]
                        pe.matmul(a, hi, hhi[:, c, :], start=c == 0, stop=False)
                        pe.matmul(a, hi, hlo[:, c, :], start=False, stop=False)
                        last = pe.matmul(a, lo, hhi[:, c, :], start=False, stop=c == DC - 1)
                    last.then_inc(a_made, 1)

                def up_group(grp, gp):
                    pe.wait_ge(w_lo, 4 * grp + 4)
                    pe.wait_ge(v_lo, 4 * grp + 4)
                    for d in range(DC):
                        wait_above(pe, o_added, 8 * grp + d - 3)
                        for q in range(4):
                            hi, lo = vhi[:, q, d * P:(d + 1) * P], vlo[:, q, d * P:(d + 1) * P]
                            o = po[d % 4][:]
                            pe.matmul(o, hi, whi[gp][:, q, :], start=q == 0, stop=False)
                            pe.matmul(o, hi, wlo[gp][:, q, :], start=False, stop=False)
                            last = pe.matmul(o, lo, whi[gp][:, q, :], start=False, stop=q == 3)
                        last.then_inc(o_made, 1)

                def body(i):
                    for j in range(8):
                        n, grp = 8 * i + j, 2 * i + j // 4
                        down(n, j)
                        if j % 4 == 0 and not (isinstance(n, int) and n == 0):
                            up_group(grp - 1, 1 - j // 4)

                pe.wait_ge(h_lo, DC)
                loop(pe, body)
                up_group(NB // 4 - 1, 1)


def residual_stage(nc, name, x, acc, gain=None):
    with ExitStack() as stack:
        r = Room(nc, stack, name)
        with nc.Block() as block:
            @block.vector
            def _(dve):
                for c in range(DC):
                    if gain is None:
                        dve.tensor_tensor(x[:, c, :], x[:, c, :], acc[:, c, :], ALU.add)
                    else:
                        dve.scalar_tensor_tensor(x[:, c, :], acc[:, c, :], gain[:, c:c + 1], x[:, c, :], ALU.mult, ALU.add)


def peer(nc, name, k, ins, xT, hT, w_query, keys, keys_of, downT, up, gates_dram, gelu, gain=None):
    with ExitStack() as stack:
        r = Room(nc, stack, name)
        e1T, e2T, gT = r.sb("e1T", [P, S]), r.sb("e2T", [P, S]), r.sb("gT", [P, S])
        with ExitStack() as inner:
            qT = Room(nc, inner, name).sb("qT", [P, 2 * PH, S])
            project_stage(nc, name + "q", w_query, hT, DC, 2 * PH, qT)
            choose_stage(nc, name + "c", k, ins, qT, keys, keys_of, e1T, e2T, gT)
        spread_stage(nc, name + "s", ins, e1T, e2T, gT, gates_dram)
    with ExitStack() as stack:
        acc = Room(nc, stack, name).sb("acc", [P, DC, S])
        experts_stage(nc, name + "e", k, hT, downT, up, gates_dram, acc, gelu)
        residual_stage(nc, name + "r", xT, acc, gain)

def head_norm_stage(nc, name, k, chunks, tokens=S):
    N = len(chunks)
    with ExitStack() as stack:
        r = Room(nc, stack, name)
        sq, mean, root = [[r.sb(f"{n}{u}", [P, tokens]) for u in range(2)] for n in ("sq", "mean", "root")]
        gains = r.sb("gains", [P, N])
        ps = [r.ps(f"ps{u}") for u in range(2)]
        squared, summed, mean_ready, rooted, done, chain = r.sem("squared", "summed", "mean_ready", "rooted", "done", "chain")
        with nc.Block() as block:
            @block.scalar
            def _(act):
                for n in range(N + 1):
                    if n < N:
                        if n >= 2:
                            act.wait_ge(summed, n - 1)
                        act.activation(sq[n % 2][:], chunks[n][0], ACT.Square).then_inc(squared, 1)
                    if n >= 1:
                        act.wait_ge(mean_ready, n)
                        act.activation(root[(n - 1) % 2][:], mean[(n - 1) % 2][:], ACT.Sqrt).then_inc(rooted, 1)

            @block.tensor
            def _(pe):
                for n, (_, _, width, _) in enumerate(chunks):
                    pe.wait_ge(squared, n + 1)
                    if n >= 2:
                        pe.wait_ge(mean_ready, n - 1)
                    ones = k.ones if width == P else k.pair_ones
                    pe.matmul(ps[n % 2][:, 0:tokens], ones[:], sq[n % 2][:], start=True, stop=True).then_inc(summed, 1)

            @block.vector
            def _(dve):
                link = Chain(dve, chain)

                def finish(n):
                    chunk = chunks[n][0]
                    dve.wait_ge(rooted, n + 1)
                    link(dve.reciprocal(root[n % 2][:], root[n % 2][:]))
                    dve.scalar_tensor_tensor(chunk, chunk, gains[:, n:n + 1], root[n % 2][:], ALU.mult, ALU.mult).then_inc(done, 1)

                for n, (_, gain, _, times) in enumerate(chunks):
                    ins = dve.tensor_scalar(gains[:, n:n + 1], gain, times, None, ALU.mult)
                link(ins)
                for n in range(N + 1):
                    if n < N:
                        if n >= 2:
                            dve.wait_ge(done, n - 1)
                        dve.wait_ge(summed, n + 1)
                        dve.tensor_scalar(mean[n % 2][:], ps[n % 2][:, 0:tokens], 1.0 / chunks[n][2], EPS, ALU.mult, ALU.add).then_inc(mean_ready, 1)
                    if n >= 1:
                        finish(n - 1)


def turn_stage(nc, name, k, units):
    with ExitStack() as stack:
        r = Room(nc, stack, name)
        pt = [r.ps(f"pt{u}") for u in range(4)]
        turned, copied = r.sem("turned", "copied")
        with nc.Block() as block:
            @block.tensor
            def _(pe):
                for n, (srcs, _) in enumerate(units):
                    if n >= 4:
                        pe.wait_ge(copied, n - 3)
                    for j, src in enumerate(srcs):
                        last = pe.transpose(pt[n % 4][:, j * P:(j + 1) * P], src, k.ident[:])
                    last.then_inc(turned, 1)

            @block.vector
            def _(dve):
                for n, (srcs, dst) in enumerate(units):
                    dve.wait_ge(turned, n + 1)
                    dve.tensor_copy(dst, pt[n % 4][:, 0:len(srcs) * P].rearrange("p (t n) -> p t n", n=P)).then_inc(copied, 1)


def forget_stage(nc, k, z, bias, fq, fk):
    with ExitStack() as stack:
        r = Room(nc, stack, "forget")
        v, low, mag, c, neg, ones = [r.sb(n, [FH, S]) for n in ("v", "low", "mag", "c", "neg", "ones")]
        raised, absed, logged, summed, filled, moved, chain = r.sem("raised", "absed", "logged", "summed", "filled", "moved", "chain")
        with nc.Block() as block:
            @block.scalar
            def _(act):
                act.wait_ge(raised, 1)
                act.activation(mag[:], v[:], ACT.Abs).then_inc(absed, 1)
                act.wait_ge(absed, 1)
                act.activation(mag[:], mag[:], ACT.Exp, scale=-1.0).then_inc(absed, 1)
                act.wait_ge(absed, 2)
                act.activation(mag[:], mag[:], ACT.Ln, bias=1.0).then_inc(logged, 1)

            @block.vector
            def _(dve):
                link = Chain(dve, chain)
                dve.memset(fq, 1.0)
                dve.memset(fk, 1.0).then_inc(filled, 1)
                dve.memset(ones[:], 1.0)
                link.announce(dve.tensor_scalar(v[:], z[0:FH, Y_FF, :], bias, None, ALU.add), raised, 1)
                link(dve.tensor_scalar(low[:], v[:], 0.0, None, ALU.min))
                dve.wait_ge(logged, 1)
                link(dve.tensor_tensor(low[:], low[:], mag[:], ALU.subtract))
                link(dve.tensor_tensor_scan(c[:], ones[:], low[:], 0.0, ALU.mult, ALU.add))
                dve.tensor_scalar(neg[:], c[:], -1.0, None, ALU.mult).then_inc(summed, 1)

            @block.sync
            def _(sp):
                sp.wait_ge(summed, 1)
                sp.wait_ge(filled, 1)
                for h in range(FH):
                    sp.dma_start(fq[0:1, h, :], c[h:h + 1, :]).then_inc(moved, 16)
                    sp.dma_start(fk[1:2, h, :], neg[h:h + 1, :]).then_inc(moved, 16)
                sp.wait_ge(moved, 2 * 16 * FH)


def second_mixer(nc, k, ins, cols, xT, hT):
    with ExitStack() as mixer:
        m = Room(nc, mixer, "mix2")
        z = m.sb("z", [P, Y_N, S])
        project_stage(nc, "p2", ins["w_in_2"], hT, DC, Y_N, z)
        foxT, swaT, memT = m.sb("foxT", [P, 4, S]), m.sb("swaT", [P, 4, S]), m.sb("memT", [P, 4, S])
        heads = [(z[:, Y_FQ + i, :], cols("fox_q_g"), FD, FD ** -0.5) for i in range(4)]
        heads += [(z[:, Y_FK + i, :], cols("fox_k_g"), FD, 1.0) for i in range(4)]
        heads += [(z[:, Y_SQ + i, :], cols("swa_q_g"), SD, SD ** -0.5) for i in range(4)]
        heads += [(z[:, Y_SKV, :], cols("swa_k_g"), SD, 1.0)]
        heads += [(z[:, Y_MQ + i, :], cols("mem_q_g"), GD, GD ** -0.5) for i in range(4)]
        head_norm_stage(nc, "hn", k, heads)
        tiles = lambda chunk: [chunk[:, t * P:(t + 1) * P] for t in range(chunk.shape[-1] // P)]
        with ExitStack() as local, ExitStack() as fox:
            vs, a = Room(nc, local, "local"), Room(nc, fox, "fox")
            v_tp = vs.sb("v", [P, 5, TT, P])
            fq, fk = hT[0:2], a.sb("fk", [2, FH, S])[:]
            forget_stage(nc, k, z, cols("b_forget")[0:FH], fq, fk)
            turn_stage(nc, "vt", k, [(tiles(z[:, Y_FV + i, :]), v_tp[:, i]) for i in range(4)] + [(tiles(z[:, Y_SKV + 1, :]), v_tp[:, 4])])
            items = []
            for h in range(FH):
                c, half = h // 2, slice(h % 2 * FD, h % 2 * FD + FD)
                for t in range(TT):
                    items.append((z[half, Y_FQ + c, t * P:(t + 1) * P], z[half, Y_FK + c, 0:(t + 1) * P], k.causal[:],
                                  [v_tp[:, c, j, half] for j in range(t + 1)], h, t,
                                  (fq[:, h, t * P:(t + 1) * P], fk[:, h, 0:(t + 1) * P])))
            attention_stage(nc, "foxa", k, items, FH, FD, foxT)
            fox.close()
            alibi, sinks = vs.sb("alibi", [P, SH, 2 * P]), a.sb("sinks", [P, SH])
            load_stage(nc, "swal", [(alibi[:], ins["alibi"]), (sinks[:], ins["swa_sinks"].to_broadcast([P, SH]))])
            items = []
            for h in range(SH):
                grp = h // (SH // SG)
                half = slice(grp * SD, grp * SD + SD)
                for t in range(TT):
                    k0 = max(t - 1, 0)
                    items.append((z[half, Y_SQ + h % 4, t * P:(t + 1) * P], z[half, Y_SKV, k0 * P:(t + 1) * P],
                                  alibi[:, h, (0 if t else P):2 * P], [v_tp[:, 4, j, half] for j in range(k0, t + 1)], h, t, None))
            attention_stage(nc, "swaa", k, items, SH, SD, swaT, sinks=sinks)
        with ExitStack() as memory:
            a = Room(nc, memory, "mem")
            mT, mkv, mv = a.sb("mT", [P, DC, NMEM]), a.sb("mkv", [P, DC, NMEM]), a.sb("mv", [P, 4, 2, P])
            load_stage(nc, "meml", [(mT[:], ins["memT"].rearrange("(c p) t -> p c t", p=P))])
            norm_stage(nc, "mn", k, mT, DC, D, cols("mem_norm_g_2"), mT, tokens=NMEM)
            project_stage(nc, "mp", ins["w_mem_kv"], mT, DC, DC, mkv, tokens=NMEM)
            head_norm_stage(nc, "mh", k, [(mkv[:, i, :], cols("mem_k_g"), GD, 1.0) for i in range(4)], tokens=NMEM)
            turn_stage(nc, "mt", k, [(tiles(mkv[:, 4 + i, :]), mv[:, i]) for i in range(4)])
            items = [(z[:, Y_MQ + h, t * P:(t + 1) * P], mkv[:, h, :], None, [mv[:, h, j, :] for j in range(2)], h, t, None)
                     for h in range(GH) for t in range(TT)]
            attention_stage(nc, "mema", k, items, GH, GD, memT)
        squash_stage(nc, "sg2", z, Y_GATE, 3 * DC, bias=cols("b_gate_2"))
        merge_stage(nc, "mg2", z, Y_GATE, [(ins["w_fox_o"], foxT), (ins["w_swa_o"], swaT), (ins["w_mem_o"], memT)], hT)
    project_stage(nc, "po2", ins["w_out_2"], hT, DC, DC, xT, add=(k.ones, xT))

def y_of(t):
    return t[:].rearrange("p t (h n) -> p t h n", n=RN)


class Held:
    pass


def build(nc, ins, where, out):
    with ExitStack() as whole:
        r = Room(nc, whole, "held")
        k = Held()
        k.ident, k.ones = r.sb("ident", [P, P]), r.sb("ones", [P, P])
        k.columns = r.sb("columns", [P, ins["columns"].shape[1]])
        k.causal, k.pair_ones = r.sb("causal", [P, P]), r.sb("pair_ones", [P, P])
        xT, hT, mod = r.sb("xT", [P, DC, S]), r.sb("hT", [P, DC, S]), r.sb("mod", [P, 48])
        gain = r.sb("gain", [P, DC])
        cols = lambda n: k.columns[:, where[n][0]:where[n][1]]
        load_stage(nc, "first", [(k.ident[:], ins["ident"]), (k.columns[:], ins["columns"]), (k.causal[:], ins["causal"]), (k.pair_ones[:], ins["pair_ones"]),
                                 (xT[:], ins["xT"].rearrange("(c p) t -> p c t", p=P))])
        ada_stage(nc, cols("c"), ins["w_ada"], cols("b_ada"), mod)
        gain_stage(nc, "g1", gain, cols("norm_mix"), mod[:, DC:2 * DC], ones=k.ones)
        norm_stage(nc, "n1", k, xT, DC, D, gain, hT, shift=mod[:, 0:DC])
        with ExitStack() as mixer:
            m = Room(nc, mixer, "mix")
            z = m.sb("z", [P, Z_N, S])
            project_stage(nc, "p1", ins["w_in"], hT, DC, Z_N, z)
            oT = m.sb("oT", [P, 4, S])
            with ExitStack() as mla:
                a = Room(nc, mla, "mla")
                qT, kT, v_tp = a.sb("qT", [QH, MH, S]), a.sb("kT", [QH, MH, S]), a.sb("v", [P, TT, MH, VH])
                norm_stage(nc, "nq", k, z[:, Z_QA:Z_KV], 2, 256, cols("q_a_norm"), z[:, Z_QA:Z_KV])
                norm_stage(nc, "nk", k, z[:, Z_KV:Z_R], 1, 128, cols("kv_a_norm"), z[:, Z_KV:Z_R])
                mla_heads_stage(nc, k, z, ins, z[:, Z_QA:Z_KV], z[:, Z_KV:Z_R], ins["w_uq"], ins["w_ukv"], qT, kT, v_tp, hT)
                items = [(qT[:, h, t * P:(t + 1) * P], kT[:, h, 0:(t + 1) * P], k.causal[:],
                          [v_tp[:, j, h, :] for j in range(t + 1)], h, t, None) for h in range(MH) for t in range(TT)]
                attention_stage(nc, "mlaa", k, items, MH, VH, oT)
            with ExitStack() as rwkv:
                a = Room(nc, rwkv, "rwkv")
                KR, sgate = a.sb("KR", [P, RP, TT, 2, P]), a.sb("sgate", [P, S])
                mid_e, end_e, bonus = a.sb("mid_e", [P, RP * TT]), a.sb("end_e", [P, RP * TT]), a.sb("bonus", [P, TT, RH])
                tile4 = lambda ap: ap.rearrange("p m (t n) -> p m t n", n=P)
                vT = a.sb("vT", [P, RP, TT, P])
                with ExitStack() as early:
                    rk = Room(nc, early, "early").sb("rk", [P, RP, S])
                    rwkv_prepare_stage(nc, k, z, ins, cols, hT, KR, rk, sgate, mid_e, end_e)
                    kkT, bT, kdT = tile4(hT[:, 0:4, :]), tile4(hT[:, 4:8, :]), tile4(z[:, Z_V:Z_WA, :])
                    rwkv_turn_stage(nc, k, z, ins, KR, rk, kkT, bT, kdT, vT, bonus)
                rT = a.sb("rT", [P, 4, S])
                rwkv_solve_stage(nc, k, ins, KR, z[:, Z_R:Z_K, :], z[:, Z_K:Z_V, :], kkT, bT, kdT, vT, mid_e, end_e, y_of(rT))
                yT = a.sb("yT", [P, 4, S])
                rwkv_finish_stage(nc, k, ins, y_of(rT), vT[:], bonus, sgate, yT, None)
                squash_stage(nc, "sg1", z, Z_GATE, 2 * DC)
                merge_stage(nc, "mg1", z, Z_GATE, [(ins["w_o_mla"], oT), (ins["w_o_rwkv"], yT)], hT)
            project_stage(nc, "po1", ins["w_out"], hT, DC, DC, xT, add=(mod[:, 2 * DC:3 * DC], xT))
        gates_dram = nc.dram_tensor("gates_scratch", [S // SUB, P, NK, SUB], F32, kind="Internal").ap()
        gain_stage(nc, "g2", gain, cols("norm_ffn"), mod[:, 4 * DC:5 * DC])
        norm_stage(nc, "n2", k, xT, DC, D, gain, hT, shift=mod[:, 3 * DC:4 * DC])
        peer(nc, "e1", k, ins, xT, hT, ins["w_query"], ins["keys1"], lambda c: c % 2, ins["down1"], ins["up1"],
             gates_dram, ACT.Gelu_apprx_tanh, gain=mod[:, 5 * DC:6 * DC])
        norm_stage(nc, "n3", k, xT, DC, D, cols("norm1_g_2"), hT)
        second_mixer(nc, k, ins, cols, xT, hT)
        norm_stage(nc, "n4", k, xT, DC, D, cols("norm2_g_2"), hT)
        peer(nc, "e2", k, ins, xT, hT, ins["w_peer_q"], ins["keys2"], lambda c: c, ins["down2"], ins["up2"],
             gates_dram, ACT.Gelu)
        with ExitStack() as stack:
            stored = Room(nc, stack, "end").sem("stored")
            with nc.Block() as block:
                @block.sync
                def _(sp):
                    sp.dma_start(out.rearrange("(c p) t -> p c t", p=P), xT[:]).then_inc(stored, 16)
                    sp.wait_ge(stored, 16)


def gain_stage(nc, name, gain, g, scale, ones=None):
    with ExitStack() as stack:
        r = Room(nc, stack, name)
        chain = r.sem("chain")
        with nc.Block() as block:
            @block.vector
            def _(dve):
                link = Chain(dve, chain)
                if ones is not None:
                    dve.memset(ones[:], 1.0)
                link(dve.tensor_scalar(gain[:], scale, 1.0, None, ALU.add))
                dve.tensor_tensor(gain[:], gain[:], g, ALU.mult)

def _cols(v):
    return np.ascontiguousarray(np.asarray(v).reshape(-1, P).T)


def _layout(inp):
    f = {n: np.asarray(v) for n, v in inp.items()}
    first = lambda n: f[n][0]
    zeros = lambda *s: np.zeros(s, np.float32)
    a = {}
    a["xT"] = f["x"][0].T
    a["positions"] = _cols(f["positions"][0])
    a["w_ada"] = first("w_ada")
    w = first("w_in")
    a["w_in"] = np.concatenate([w[:, 0:384], w[:, 416:], w[:, 384:416], zeros(D, 96)], axis=1)
    a["w_uq"], a["w_ukv"] = first("w_uq"), first("w_ukv")
    a["q_norm"], a["k_norm"] = f["q_norm"], f["k_norm"]
    a["inv_freq"] = (np.float32(10000.0) ** (-np.arange(16, dtype=np.float32) / np.float32(16))).astype(np.float32)[None]
    a["ident"] = np.eye(P, dtype=np.float32)
    q = np.arange(P)
    a["causal"] = np.where(q[None, :] <= q[:, None], 0.0, NEG).astype(np.float32)
    b16 = q[:, None] // 16 == q[None, :] // 16
    lower, upper = q[None, :] < q[:, None], q[None, :] > q[:, None]
    up_incl = q[None, :] >= q[:, None]
    a["masks"] = np.stack([np.where(upper & b16, -1.0, 0.0), np.where(lower & b16, -1.0, 0.0), np.where(lower & ~b16, -1.0, 0.0),
                           np.where(upper, 1.0, 0.0), np.where(up_incl, 1.0, 0.0)]).astype(np.float32)
    a["pair_ones"] = (q[:, None] // RN == q[None, :] // RN).astype(np.float32)
    a["pair_sel"] = (q[:, None] // RN == np.arange(2)[None, :]).astype(np.float32)
    a["id64"] = (q[:, None] % RN == np.arange(RN)[None, :]).astype(np.float32)
    for n in ("w_decay_up", "w_aaa_up", "w_gate_up", "w_o_mla", "w_o_rwkv", "w_out"):
        a[n] = first(n)
    w = first("w_in_2")
    sq = w[:, 1544:2056].reshape(D, 2, 4, SD).transpose(0, 2, 1, 3).reshape(D, 512)
    a["w_in_2"] = np.concatenate([w[:, 0:1536], sq, w[:, 2056:2312], w[:, 2312:2824], w[:, 2824:], w[:, 1536:1544], zeros(D, 120)], axis=1)
    dist = q[:, None] + P - np.arange(2 * P)[None, :]
    slopes = 2.0 ** -(np.arange(SH) + 1.0)
    a["alibi"] = np.where(((dist >= 0) & (dist < P))[:, None, :], -slopes[None, :, None] * dist[:, None, :], NEG).astype(np.float32)
    a["swa_sinks"] = f["swa_sinks_2"]
    a["memT"] = f["mem_2"][0].T
    for n in ("w_mem_kv", "w_fox_o", "w_swa_o", "w_mem_o"):
        a[n] = first(n + "_2")
    a["w_out_2"], a["w_peer_q"] = first("w_out_2"), first("w_peer_q_2")
    a["keys2"] = np.stack([first("peer_keys1_2"), first("peer_keys2_2")], axis=1).reshape(2 * PH, NK, P).transpose(2, 0, 1)
    a["down2"] = first("peer_u_2").reshape(NK, NK, DC, P).transpose(0, 3, 2, 1)
    a["up2"] = first("peer_v_2").reshape(NK, NK, D)
    a["w_query"] = first("w_query")
    a["keys1"] = np.stack([first("sub_keys1").T, first("sub_keys2").T], axis=1)
    a["down1"] = first("expert_down").reshape(NK, NK, DC, P).transpose(0, 3, 2, 1)
    a["up1"] = first("expert_up").reshape(NK, NK, D)
    a["iota16"], a["iota128"] = np.arange(K16, dtype=np.float32)[None], np.arange(NK, dtype=np.float32)[None]
    a["ln_x_w"], a["ln_x_b"] = f["ln_x_w"], f["ln_x_b"]
    vecs = [("c", f["c"][0]), ("b_ada", first("b_ada")), ("norm_mix", first("norm_mix")), ("q_a_norm", first("q_a_norm")), ("kv_a_norm", first("kv_a_norm"))]
    vecs += [(n, first(n)) for n in ("mu_shift", "decay_base", "aaa_base", "k_k", "k_a")]
    vecs += [("r_k", first("r_k").reshape(-1)), ("norm_ffn", first("norm_ffn"))]
    vecs += [("norm1_g_2", first("norm1_g_2")), ("mem_norm_g_2", first("mem_norm_g_2")), ("norm2_g_2", first("norm2_g_2")),
             ("b_gate_2", first("b_gate_2"))]
    twice = lambda v: np.concatenate([v, v])
    vecs += [(n, twice(first(n + "_2"))) for n in ("fox_q_g", "fox_k_g", "swa_q_g", "swa_k_g")]
    vecs += [(n, first(n + "_2")) for n in ("mem_q_g", "mem_k_g")]
    vecs += [("b_forget", np.concatenate([first("b_forget_2"), zeros(P - FH)]))]
    at, parts, where = 0, [], {}
    for n, v in vecs:
        m = _cols(v)
        where[n] = (at, at + m.shape[1])
        at += m.shape[1]
        parts.append(m)
    a["columns"] = np.concatenate(parts, axis=1)
    return {n: np.ascontiguousarray(v) for n, v in a.items()}, where


def kernel(**inputs):
    import concourse.bacc as _bacc
    from concourse.bass_utils import run_bass_kernel_spmd as _run

    nc = _bacc.Bacc("TRN2", target_bir_lowering=False, num_devices=1)
    arrays, where = _layout(inputs)
    ins = {n: nc.dram_tensor(f"in_{n}", list(v.shape), mybir.dt.from_np(v.dtype), kind="ExternalInput").ap()
           for n, v in arrays.items()}
    out = nc.dram_tensor("out_xT", [D, S], F32, kind="ExternalOutput").ap()
    build(nc, ins, where, out)
    res = _run(nc, [{f"in_{n}": v for n, v in arrays.items()}], core_ids=[0])
    return np.ascontiguousarray(res.results[0]["out_xT"].T)[None]
```

```python
import numpy as np
import concourse.bass as bass
from concourse import mybir
from contextlib import ExitStack

F32 = mybir.dt.float32
F32R = mybir.dt.float32r
U32 = mybir.dt.uint32
I32 = mybir.dt.int32
ALU = mybir.AluOpType
ACT = mybir.ActivationFunctionType
AX = mybir.AxisListType.X
ds = bass.ds

P = 128
S = 512
D = 1024
TT = S // P
DC = D // P
EPS = 1e-6
NEG = -1e30
MH, NOPE, ROPE, VH = 8, 64, 32, 64
QH = NOPE + ROPE
RH, RN = 8, 64
RP = RH // 2
GN_EPS = 64e-5
Z_QA, Z_KV, Z_R, Z_K, Z_V, Z_WA, Z_GD, Z_GATE, Z_ROPE, Z_N = 0, 2, 3, 7, 11, 15, 16, 17, 33, 34
FH, FD = 8, 64
SH, SG, SD = 8, 2, 64
GH, GD = 4, 128
NMEM = 256
Y_FQ, Y_FK, Y_FV, Y_SQ, Y_SKV, Y_MQ, Y_GATE, Y_FF, Y_N = 0, 4, 8, 12, 16, 18, 22, 46, 47
PH, NK, K16 = 8, 128, 16
NJ = PH * K16
SUB = 64


class Chain:

    def __init__(self, eng, sem):
        self.eng, self.sem, self.n = eng, sem, 0

    def __call__(self, ins):
        self.n += 1
        ins.then_inc(self.sem, 1)
        self.eng.wait_ge(self.sem, self.n)

    def announce(self, ins, sem, count):
        ins.then_inc(sem, 1)
        self.eng.wait_ge(sem, count)


class Room:

    def __init__(self, nc, stack, name):
        self.nc, self.stack, self.name, self.sems = nc, stack, name, []
        stack.callback(lambda: [nc.gpsimd.sem_clear(s) for s in self.sems])

    def sb(self, name, shape, dt=F32):
        return self.stack.enter_context(self.nc.sbuf_tensor(f"{self.name}_{name}", shape, dt))

    def ps(self, name, shape=(P, 512), dt=F32):
        return self.stack.enter_context(self.nc.psum_tensor(f"{self.name}_{name}", list(shape), dt))

    def sem(self, *names):
        got = [self.stack.enter_context(self.nc.semaphore(f"{self.name}_{n}")) for n in names]
        self.sems += got
        return got[0] if len(got) == 1 else got


def bcast(ap, n, axis):
    shape = list(ap.shape)
    a = ap.unsqueeze(axis)
    shape.insert(axis, n)
    return a.to_broadcast(shape)


def row(t, m):
    return t[:, m, :] if isinstance(m, int) else t[:, ds(m, 1), :].rearrange("p a t -> p (a t)")


def col(t, m):
    return t[:, m:m + 1] if isinstance(m, int) else t[:, ds(m, 1)]


def load_stage(nc, name, pairs):
    with ExitStack() as stack:
        r = Room(nc, stack, name)
        loaded = r.sem("loaded")
        with nc.Block() as block:
            @block.sync
            def _(sp):
                for dst, src in pairs:
                    sp.dma_start(dst, src).then_inc(loaded, 16)
                sp.wait_ge(loaded, 16 * len(pairs))


def ada_stage(nc, k, ccol, w_ada, bcol, mod):
    groups = w_ada.shape[0]
    with ExitStack() as stack:
        r = Room(nc, stack, "ada")
        sig, sc = r.sb("sig", [P, DC]), r.sb("silu", [P, DC])
        w = [r.sb(f"w{u}", [P, DC, 512]) for u in range(3)]
        acc = [[r.sb(f"acc{u}{v}", [P, 512]) for v in range(2)] for u in range(2)]
        ps = r.ps("ps")
        sig_ready, silu_ready, summed, product_ready, chain = r.sem("sig_ready", "silu_ready", "summed", "product_ready", "chain")
        w_ready = [r.sem(f"w_ready{u}") for u in range(3)]
        with nc.Block() as block:
            @block.sync
            def _(sp):
                for n in range(groups):
                    if n >= 3:
                        sp.wait_ge(summed, n - 2)
                    sp.dma_start(w[n % 3][:], w_ada[n]).then_inc(w_ready[n % 3], 16)

            @block.scalar
            def _(act):
                act.activation(sig[:], ccol, ACT.Sigmoid).then_inc(sig_ready, 1)

            @block.tensor
            def _(pe):
                for n in range(groups):
                    pe.wait_ge(summed, n + 1)
                    for j in range(4):
                        last = pe.matmul(ps[:, 4 * n + j:4 * n + j + 1], acc[n % 2][1][:, j * P:(j + 1) * P], k.ones[:, 0:1],
                                         start=True, stop=True)
                    last.then_inc(product_ready, 1)

            @block.vector
            def _(dve):
                link = Chain(dve, chain)
                dve.memset(k.ones[:], 1.0)
                dve.wait_ge(sig_ready, 1)
                link(dve.tensor_tensor(sc[:], ccol, sig[:], ALU.mult))
                for n in range(groups):
                    dve.wait_ge(w_ready[n % 3], 16 * (n // 3) + 16)
                    if n >= 2:
                        dve.wait_ge(product_ready, n - 1)
                    link(dve.tensor_scalar(acc[n % 2][0][:], w[n % 3][:, 0, :], sc[:, 0:1], None, ALU.mult))
                    for c in range(1, DC):
                        ins = dve.scalar_tensor_tensor(acc[n % 2][c % 2][:], w[n % 3][:, c, :], sc[:, c:c + 1],
                                                       acc[n % 2][1 - c % 2][:], ALU.mult, ALU.add)
                        if c < DC - 1:
                            link(ins)
                    ins.then_inc(summed, 1)
                dve.wait_ge(product_ready, groups)
                dve.tensor_tensor(mod[:], ps[:, 0:4 * groups], bcol, ALU.add)


def norm_stage(nc, name, k, src, chunks, width, gain, dst, shift=None, tokens=S):
    with ExitStack() as stack:
        r = Room(nc, stack, name)
        sq, mean, root, rstd = r.sb("sq", [P, chunks, tokens]), r.sb("mean", [P, tokens]), r.sb("root", [P, tokens]), r.sb("rstd", [P, tokens])
        ss = r.ps("ss")
        sq_ready, ss_ready, mean_ready, root_ready, chain = r.sem("sq_ready", "ss_ready", "mean_ready", "root_ready", "chain")
        with nc.Block() as block:
            @block.scalar
            def _(act):
                for c in range(chunks):
                    act.activation(sq[:, c, :], src[:, c, :], ACT.Square).then_inc(sq_ready, 1)
                act.wait_ge(mean_ready, 1)
                act.activation(root[:], mean[:], ACT.Sqrt).then_inc(root_ready, 1)

            @block.tensor
            def _(pe):
                for c in range(chunks):
                    pe.wait_ge(sq_ready, c + 1)
                    last = pe.matmul(ss[:, 0:tokens], k.ones[:], sq[:, c, :], start=c == 0, stop=c == chunks - 1)
                last.then_inc(ss_ready, 1)

            @block.vector
            def _(dve):
                link = Chain(dve, chain)
                dve.wait_ge(ss_ready, 1)
                dve.tensor_scalar(mean[:], ss[:, 0:tokens], 1.0 / width, EPS, ALU.mult, ALU.add).then_inc(mean_ready, 1)
                dve.wait_ge(root_ready, 1)
                link(dve.reciprocal(rstd[:], root[:]))
                for c in range(chunks):
                    ins = dve.scalar_tensor_tensor(dst[:, c, :], src[:, c, :], gain[:, c:c + 1], rstd[:], ALU.mult, ALU.mult)
                    if shift is not None:
                        link(ins)
                        dve.tensor_scalar(dst[:, c, :], dst[:, c, :], shift[:, c:c + 1], None, ALU.add)


def project_stage(nc, name, w_dram, act_in, kc, chunks, dst, tokens=S, add=None):
    with ExitStack() as stack:
        r = Room(nc, stack, name)
        hhi, hlo = r.sb("hhi", [P, kc, tokens], F32R), r.sb("hlo", [P, kc, tokens], F32R)
        raw, whi, wlo = [[r.sb(f"{n}{u}", [P, kc, P], dt) for u in range(2)] for n, dt in (("raw", F32), ("whi", F32R), ("wlo", F32R))]
        ps = [r.ps(f"ps{u}") for u in range(4)]
        h_hi, h_lo, w_hi, split, made, used = r.sem("h_hi", "h_lo", "w_hi", "split", "made", "used")
        w_ready = [r.sem(f"w_ready{u}") for u in range(2)]
        turns = (chunks - 1) // 4

        def loop(eng, body):
            if turns:
                with eng.Fori(0, turns) as i:
                    for q in range(4):
                        body(4 * i + q, q)
            for n in range(4 * turns, chunks):
                body(n, n % 4)

        with nc.Block() as block:
            @block.sync
            def _(sp):
                def body(n, q):
                    sp.wait_ge(split, n + 1)
                    src = w_dram[n] if isinstance(n, int) else w_dram[ds(n, 1)].rearrange("a p c e -> (a p) c e")
                    sp.dma_start(raw[q % 2][:], src).then_inc(w_ready[q % 2], 16)

                loop(sp, body)

            @block.scalar
            def _(act):
                def body(n, q):
                    act.wait_ge(w_ready[q % 2], 8 * n + 16 - 8 * (q % 2))
                    act.wait_ge(made, n + 1)
                    act.activation(whi[q % 2][:], raw[q % 2][:], ACT.Copy).then_inc(w_hi, 1)

                for c in range(kc):
                    act.activation(hhi[:, c, :], act_in[:, c, :], ACT.Copy).then_inc(h_hi, 1)
                loop(act, body)

            @block.tensor
            def _(pe):
                def body(n, q):
                    pe.wait_ge(split, n + 3)
                    pe.wait_ge(used, n + 1)
                    out = ps[q][:, 0:tokens]
                    for c in range(kc):
                        hi, lo = whi[q % 2][:, c, :], wlo[q % 2][:, c, :]
                        pe.matmul(out, hi, hhi[:, c, :], start=c == 0, stop=False)
                        pe.matmul(out, hi, hlo[:, c, :], start=False, stop=False)
                        last = pe.matmul(out, lo, hhi[:, c, :], start=False, stop=c == kc - 1)
                    last.then_inc(made, 1)

                pe.sem_inc(made, 2)
                pe.wait_ge(h_lo, kc)
                loop(pe, body)

            @block.vector
            def _(dve):
                def split_w(n, q):
                    dve.wait_ge(w_hi, n + 1)
                    dve.tensor_tensor(wlo[q % 2][:], raw[q % 2][:], whi[q % 2][:].bitcast(F32), ALU.subtract).then_inc(split, 1)

                def body(n, q):
                    if not (isinstance(n, int) and n == chunks - 1):
                        split_w(n + 1, q + 1)
                    dve.wait_ge(made, n + 3)
                    got = ps[q][:, 0:tokens]
                    if add is None:
                        ins = dve.tensor_copy(row(dst, n), got)
                    else:
                        gain, base = add
                        ins = dve.scalar_tensor_tensor(row(dst, n), got, col(gain, n), row(base, n), ALU.mult, ALU.add)
                    ins.then_inc(used, 1)

                dve.sem_inc(split, 2)
                dve.sem_inc(used, 4)
                for c in range(kc):
                    dve.wait_ge(h_hi, c + 1)
                    dve.tensor_tensor(hlo[:, c, :], act_in[:, c, :], hhi[:, c, :].bitcast(F32), ALU.subtract).then_inc(h_lo, 1)
                split_w(0, 0)
                loop(dve, body)

def mla_heads_stage(nc, k, z, g, cq, ckv, w_uq_in, w_ukv_in, qT, kT, v_tp, spare):
    with ExitStack() as stack:
        r = Room(nc, stack, "mlah")
        w_uq, w_ukv = r.sb("w_uq", [P, 2, MH * QH]), r.sb("w_ukv", [P, MH * (NOPE + VH)])
        gq, gk = r.sb("gq", [P, QH]), r.sb("gk", [P, QH])
        pos_i, pos = r.sb("pos_i", [P, TT], I32), r.sb("pos", [P, TT])
        freq = r.sb("freq", [P, 16])
        ang, turns, trig = r.sb("ang", [P, TT, 16]), r.sb("turns", [P, TT, 16]), r.sb("trig", [P, 2, TT, 16])
        q, kk = r.sb("q", [P, TT, MH, QH]), r.sb("kk", [P, TT, MH, QH])
        kr = r.sb("kr", [P, TT, ROPE])
        sq = r.sb("sq", [P, TT * MH, QH])
        ss, root = r.sb("ss", [P, 4, TT * MH]), r.sb("root", [P, 4, TT * MH])
        rot = spare[:, 0:4, :].rearrange("p a (g n) -> p a g n", n=16)
        ps = [r.ps(f"ps{u}") for u in range(4)]
        pt = [r.ps(f"pt{u}") for u in range(2)]
        loaded, made, taken, sums, roots, heads, turned, turned_used, reduced, sines, chain = r.sem(
            "loaded", "made", "taken", "sums", "roots", "heads", "turned", "turned_used", "reduced", "sines", "chain")
        TWO_PI = 2 * np.pi
        C1 = float(np.float32(6.28125))
        C2 = float(np.float32(np.float32((TWO_PI - C1) * 4096) // 1 / 4096))
        C3 = float(np.float32(TWO_PI - C1 - C2))
        MAGIC = 12582912.0
        with nc.Block() as block:
            @block.sync
            def _(sp):
                sp.dma_start(w_uq[:], w_uq_in.rearrange("(c p) n -> p c n", p=P)).then_inc(loaded, 16)
                sp.dma_start(w_ukv[:], w_ukv_in).then_inc(loaded, 16)
                sp.dma_start(gq[:], g["q_norm"].to_broadcast([P, QH])).then_inc(loaded, 16)
                sp.dma_start(gk[:], g["k_norm"].to_broadcast([P, QH])).then_inc(loaded, 16)
                sp.dma_start(pos_i[:], g["positions"]).then_inc(loaded, 16)
                sp.dma_start(freq[:], g["inv_freq"].to_broadcast([P, 16])).then_inc(loaded, 16)

            @block.tensor
            def _(pe):
                pe.wait_ge(loaded, 96)
                for t in range(TT):
                    tok = slice(t * P, t * P + P)
                    if t:
                        pe.wait_ge(taken, t)
                    for u, n0, n1 in ((0, 0, 384), (1, 384, 768)):
                        for c in range(2):
                            pe.matmul(ps[u][:, 0:384], cq[:, c, tok], w_uq[:, c, n0:n1], start=c == 0, stop=c == 1)
                    for u in range(2):
                        pe.matmul(ps[2 + u][:], ckv[:, 0, tok], w_ukv[:, u * 512:(u + 1) * 512], start=True, stop=True)
                    pe.transpose(pt[0][:, 0:P], z[:, Z_ROPE, tok], k.ident[:]).then_inc(made, 1)
                pe.wait_ge(taken, TT)
                for n in range(2 * MH):
                    src, h = (q, n) if n < MH else (kk, n - MH)
                    pe.wait_ge(heads, TT if n < MH else TT + 1)
                    if n >= 2:
                        pe.wait_ge(turned_used, n - 1)
                    for t in range(TT):
                        last = pe.transpose(pt[n % 2][0:QH, t * P:(t + 1) * P], src[:, t, h, :], k.ident[:])
                    last.then_inc(turned, 1)

            @block.scalar
            def _(act):
                act.wait_ge(sines, 2)
                act.activation(trig[:], trig[:], ACT.Sin).then_inc(sines, 1)
                act.wait_ge(sums, 4)
                act.activation(root[:], ss[:], ACT.Sqrt).then_inc(roots, 1)
                for n in range(2 * MH):
                    dst, h = (qT, n) if n < MH else (kT, n - MH)
                    act.wait_ge(turned, n + 1)
                    act.activation(dst[:, h, :], pt[n % 2][0:QH, :], ACT.Copy).then_inc(turned_used, 1)

            @block.vector
            def _(dve):
                link = Chain(dve, chain)
                dve.wait_ge(loaded, 96)
                link(dve.tensor_scalar(gq[:], gq[:], QH ** -0.5, None, ALU.mult))
                link(dve.tensor_copy(pos[:], pos_i[:]))
                link(dve.tensor_tensor(ang[:], bcast(pos[:], 16, 2), bcast(freq[:], TT, 1), ALU.mult))
                for j in range(2):
                    link(dve.tensor_scalar(turns[:], ang[:], 1 / TWO_PI, 0.25 * j, ALU.mult, ALU.add))
                    link(dve.tensor_scalar(turns[:], turns[:], MAGIC, None, ALU.add))
                    link(dve.tensor_scalar(turns[:], turns[:], MAGIC, None, ALU.subtract))
                    link(dve.scalar_tensor_tensor(trig[:, j], turns[:], -C1, ang[:], ALU.mult, ALU.add))
                    link(dve.scalar_tensor_tensor(trig[:, j], turns[:], -C2, trig[:, j], ALU.mult, ALU.add))
                    link(dve.scalar_tensor_tensor(trig[:, j], turns[:], -C3, trig[:, j], ALU.mult, ALU.add))
                    if j:
                        link(dve.tensor_scalar(trig[:, j], trig[:, j], np.pi / 2, None, ALU.add))
                    link.announce(dve.tensor_scalar(trig[:, j], trig[:, j], 3.1415925, -3.1415925, ALU.min, ALU.max), sines, j + 1)
                for t in range(TT):
                    dve.wait_ge(made, t + 1)
                    dve.tensor_copy(q[:, t, 0:4, :], ps[0][:, 0:384].rearrange("p (h d) -> p h d", h=4))
                    dve.tensor_copy(q[:, t, 4:8, :], ps[1][:, 0:384].rearrange("p (h d) -> p h d", h=4))
                    for u in range(2):
                        both = ps[2 + u][:].rearrange("p (h d) -> p h d", h=4)
                        dve.tensor_copy(kk[:, t, 4 * u:4 * u + 4, 0:NOPE], both[:, :, 0:NOPE])
                        dve.tensor_copy(v_tp[:, t, 4 * u:4 * u + 4, :], both[:, :, NOPE:NOPE + VH])
                    link.announce(dve.tensor_copy(kr[:, t, :], pt[0][:, 0:ROPE]), taken, t + 1)
                qg, kg = q[:].rearrange("p t h d -> p (t h) d"), kk[:].rearrange("p t h d -> p (t h) d")
                link(dve.tensor_tensor(sq[:], qg, qg, ALU.mult))
                link(dve.reduce_sum(ss[:, 0], sq[:, :, 0:NOPE], AX))
                link(dve.reduce_sum(ss[:, 1], sq[:, :, NOPE:QH], AX))
                link(dve.tensor_tensor(sq[:, :, 0:NOPE], kg[:, :, 0:NOPE], kg[:, :, 0:NOPE], ALU.mult))
                link(dve.reduce_sum(ss[:, 2], sq[:, :, 0:NOPE], AX))
                link(dve.tensor_tensor(sq[:, 0:TT, 0:ROPE], kr[:], kr[:], ALU.mult))
                link(dve.memset(ss[:, 3], 1.0))
                link(dve.reduce_sum(ss[:, 3, 0:TT], sq[:, 0:TT, 0:ROPE], AX))
                for j, n in enumerate((NOPE, ROPE, NOPE, ROPE)):
                    link.announce(dve.tensor_scalar(ss[:, j], ss[:, j], 1.0 / n, EPS, ALU.mult, ALU.add), sums, j + 1)
                dve.wait_ge(roots, 1)
                link(dve.reciprocal(ss[:], root[:]))
                TH = TT * MH
                link(dve.tensor_tensor(qg[:, :, 0:NOPE], qg[:, :, 0:NOPE], bcast(ss[:, 0], NOPE, 2), ALU.mult))
                link(dve.tensor_tensor(qg[:, :, NOPE:QH], qg[:, :, NOPE:QH], bcast(ss[:, 1], ROPE, 2), ALU.mult))
                link(dve.tensor_tensor(kg[:, :, 0:NOPE], kg[:, :, 0:NOPE], bcast(ss[:, 2], NOPE, 2), ALU.mult))
                link(dve.tensor_tensor(kr[:], kr[:], bcast(ss[:, 3, 0:TT], ROPE, 2), ALU.mult))
                link(dve.tensor_tensor(qg, qg, bcast(gq[:], TH, 1), ALU.mult))
                link(dve.tensor_tensor(kg[:, :, 0:NOPE], kg[:, :, 0:NOPE], bcast(gk[:, 0:NOPE], TH, 1), ALU.mult))
                link(dve.tensor_tensor(kr[:], kr[:], bcast(gk[:, NOPE:QH], TT, 1), ALU.mult))
                dve.wait_ge(sines, 3)
                r4 = rot.rearrange("p a (t h) n -> p a t h n", t=TT)
                for t in range(TT):
                    x1, x2 = q[:, t, :, NOPE:NOPE + 16], q[:, t, :, NOPE + 16:QH]
                    sin, cos = bcast(trig[:, 0, t], MH, 1), bcast(trig[:, 1, t], MH, 1)
                    dve.tensor_tensor(r4[:, 0, t], x1, cos, ALU.mult)
                    dve.tensor_tensor(r4[:, 1, t], x2, sin, ALU.mult)
                    dve.tensor_tensor(r4[:, 2, t], x1, sin, ALU.mult)
                    link(dve.tensor_tensor(r4[:, 3, t], x2, cos, ALU.mult))
                    dve.tensor_tensor(x1, r4[:, 0, t], r4[:, 1, t], ALU.subtract)
                    link.announce(dve.tensor_tensor(x2, r4[:, 2, t], r4[:, 3, t], ALU.add), heads, t + 1)
                x1, x2 = kr[:, :, 0:16], kr[:, :, 16:32]
                sin, cos = trig[:, 0], trig[:, 1]
                dve.tensor_tensor(rot[:, 0, 0:TT], x1, cos, ALU.mult)
                dve.tensor_tensor(rot[:, 1, 0:TT], x2, sin, ALU.mult)
                dve.tensor_tensor(rot[:, 2, 0:TT], x1, sin, ALU.mult)
                link(dve.tensor_tensor(rot[:, 3, 0:TT], x2, cos, ALU.mult))
                dve.tensor_tensor(x1, rot[:, 0, 0:TT], rot[:, 1, 0:TT], ALU.subtract)
                link(dve.tensor_tensor(x2, rot[:, 2, 0:TT], rot[:, 3, 0:TT], ALU.add))
                dve.tensor_copy(kk[:, :, :, NOPE:QH], bcast(kr[:], MH, 2)).then_inc(heads, 1)


def attention_stage(nc, name, k, items, heads, vdim, oT, sinks=None):
    per = P // vdim
    N = len(items)
    with ExitStack() as stack:
        r = Room(nc, stack, name)
        p = [r.sb(f"p{u}", [P, 512]) for u in range(3)]
        pT = [r.sb(f"pT{u}", [P, 512]) for u in range(2)]
        nmax, total, inv = r.sb("nmax", [P, N]), r.sb("total", [P, N]), r.sb("inv", [P, N])
        esink = r.sb("esink", [P, N])
        ps = [r.ps(f"ps{u}") for u in range(3)]
        pt = [r.ps(f"pt{u}") for u in range(2)]
        po = [r.ps(f"po{u}") for u in range(2)]
        scored, biased, maxed, exped, sunk, weighed, turned, copied, summed, taken, chain = r.sem(
            "scored", "biased", "maxed", "exped", "sunk", "weighed", "turned", "copied", "summed", "taken", "chain")
        width = [it[1].shape[-1] for it in items]
        with nc.Block() as block:
            @block.tensor
            def _(pe):
                def score(n):
                    q_ap, k_ap, more = items[n][0], items[n][1], items[n][6]
                    if n >= 3:
                        pe.wait_ge(exped, n - 2)
                    out = ps[n % 3][:, 0:width[n]]
                    last = pe.matmul(out, q_ap, k_ap, start=True, stop=more is None)
                    if more is not None:
                        last = pe.matmul(out, more[0], more[1], start=False, stop=True)
                    last.then_inc(scored, 1)

                def turn(n):
                    pe.wait_ge(weighed, n + 1)
                    if n >= 2:
                        pe.wait_ge(copied, n - 1)
                    for j in range(width[n] // P):
                        last = pe.transpose(pt[n % 2][:, j * P:(j + 1) * P], p[n % 3][:, j * P:(j + 1) * P], k.ident[:])
                    last.then_inc(turned, 1)

                def weigh_values(n):
                    vs, at = items[n][3], (items[n][4] % per) * vdim
                    pe.wait_ge(copied, n + 1)
                    if n >= 2:
                        pe.wait_ge(taken, n - 1)
                    for j, v in enumerate(vs):
                        last = pe.matmul(po[n % 2][at:at + vdim, 0:P], v, pT[n % 2][:, j * P:(j + 1) * P],
                                         start=j == 0, stop=j == len(vs) - 1)
                    last.then_inc(summed, 1)

                for step in range(N + 3):
                    if step < N:
                        score(step)
                    if 2 <= step < N + 2:
                        turn(step - 2)
                    if 3 <= step:
                        weigh_values(step - 3)

            @block.scalar
            def _(act):
                for step in range(N + 2):
                    if step < N:
                        n = step
                        act.wait_ge(maxed, n + 1)
                        if n >= 3:
                            act.wait_ge(turned, n - 2)
                        act.activation(p[n % 3][:, 0:width[n]], ps[n % 3][:, 0:width[n]], ACT.Exp, bias=nmax[:, n:n + 1],
                                       accum_out=total[:, n:n + 1]).then_inc(exped, 1)
                        if sinks is not None:
                            h = items[n][4]
                            act.activation(esink[:, n:n + 1], sinks[:, h:h + 1], ACT.Exp,
                                           bias=nmax[:, n:n + 1]).then_inc(sunk, 1)
                    if step >= 2:
                        n = step - 2
                        act.wait_ge(turned, n + 1)
                        if n >= 2:
                            act.wait_ge(summed, n - 1)
                        act.activation(pT[n % 2][:, 0:width[n]], pt[n % 2][:, 0:width[n]], ACT.Copy).then_inc(copied, 1)

            @block.vector
            def _(dve):
                link = Chain(dve, chain)
                masked = [0]

                def peak(n):
                    bias, w, h = items[n][2], width[n], items[n][4]
                    dve.wait_ge(scored, n + 1)
                    if bias is not None:
                        part = ps[n % 3][:, w - bias.shape[-1]:w]
                        masked[0] += 1
                        link.announce(dve.tensor_tensor(part, part, bias, ALU.add), biased, masked[0])
                    link(dve.reduce_max(nmax[:, n:n + 1], ps[n % 3][:, 0:w], AX))
                    if sinks is not None:
                        link(dve.tensor_tensor(nmax[:, n:n + 1], nmax[:, n:n + 1], sinks[:, h:h + 1], ALU.max))
                    dve.tensor_scalar(nmax[:, n:n + 1], nmax[:, n:n + 1], -1.0, None, ALU.mult).then_inc(maxed, 1)

                def weigh(n):
                    dve.wait_ge(exped, n + 1)
                    if sinks is not None:
                        dve.wait_ge(sunk, n + 1)
                        link(dve.tensor_tensor(total[:, n:n + 1], total[:, n:n + 1], esink[:, n:n + 1], ALU.add))
                    link(dve.reciprocal(inv[:, n:n + 1], total[:, n:n + 1]))
                    dve.tensor_scalar(p[n % 3][:, 0:width[n]], p[n % 3][:, 0:width[n]], inv[:, n:n + 1], None, ALU.mult).then_inc(weighed, 1)

                def take(n):
                    h, t = items[n][4], items[n][5]
                    at = (h % per) * vdim
                    dve.wait_ge(summed, n + 1)
                    dve.tensor_copy(oT[at:at + vdim, h // per, t * P:(t + 1) * P], po[n % 2][at:at + vdim, 0:P]).then_inc(taken, 1)

                for step in range(N + 4):
                    if step < N:
                        peak(step)
                    if 1 <= step <= N:
                        weigh(step - 1)
                    if 4 <= step:
                        take(step - 4)

def rwkv_prepare_stage(nc, k, z, g, cols, hT, KR, rk, sgate, mid_e, end_e):
    with ExitStack() as stack:
        r = Room(nc, stack, "rprep")
        d = r.sb("d", [P, 14, S])
        kk, kh, b = d[:, 0:4, :], d[:, 4:8, :], d[:, 8:12, :]
        ld, a, c, eprev = [r.sb(n, [P, RP, S]) for n in ("ld", "a", "c", "eprev")]
        einc, eneg = hT[:, 0:4, :], hT[:, 4:8, :]
        pair_ones, ones = k.pair_ones, k.ones
        lora, tw = rk[:, 0, :], rk[0:64, 1, :]
        ps = [r.ps(f"ps{u}") for u in range(8)]
        loaded, shifted, squashed, products, gated, used, squares, norms, roots, cums, exps, chain = r.sem(
            "loaded", "shifted", "squashed", "products", "gated", "used", "squares", "norms", "roots", "cums", "exps", "chain")
        with nc.Block() as block:
            @block.sync
            def _(sp):
                sp.dma_start(lora[0:64, :], g["w_decay_up"]).then_inc(loaded, 16)
                sp.dma_start(lora[64:128, :], g["w_aaa_up"]).then_inc(loaded, 16)

            @block.tensor
            def _(pe):
                pe.wait_ge(loaded, 32)
                pe.wait_ge(squashed, 1)
                for m in range(4):
                    pe.matmul(ps[m][:], lora[0:64, m * P:(m + 1) * P], tw, start=True, stop=True).then_inc(products, 1)
                for m in range(4):
                    pe.matmul(ps[4 + m][:], lora[64:128, m * P:(m + 1) * P], z[64:128, Z_WA, :], start=True, stop=True).then_inc(products, 1)
                pe.wait_ge(gated, 8)
                pe.wait_ge(squares, 1)
                for m in range(4):
                    pe.matmul(ps[m][:], pair_ones[:], c[:, m, :], start=True, stop=True).then_inc(norms, 1)

            @block.scalar
            def _(act):
                act.wait_ge(shifted, 1)
                act.activation(tw, z[0:64, Z_WA, :], ACT.Tanh).then_inc(squashed, 1)
                act.activation(sgate[:], z[:, Z_GD, :], ACT.Sigmoid)
                for m in range(8):
                    act.wait_ge(products, m + 1)
                    dst, base = (ld, cols("decay_base")) if m < 4 else (a, cols("aaa_base"))
                    act.activation(dst[:, m % 4, :], ps[m][:], ACT.Sigmoid, bias=base[:, m % 4:m % 4 + 1]).then_inc(gated, 1)
                for m in range(4):
                    act.wait_ge(norms, m + 1)
                    act.activation(eprev[:, m, :], ps[m][:], ACT.Sqrt).then_inc(roots, 1)
                act.wait_ge(cums, 1)
                act.activation(einc, c[:], ACT.Exp).then_inc(exps, 1)
                act.activation(eneg, c[:], ACT.Exp, scale=-1.0).then_inc(exps, 1)
                act.wait_ge(cums, 2)
                act.activation(eprev[:], ld[:], ACT.Exp).then_inc(exps, 1)
                act.activation(mid_e[:], mid_e[:], ACT.Exp).then_inc(exps, 1)

            @block.vector
            def _(dve):
                link = Chain(dve, chain)
                zs = z[:, Z_R:Z_GATE, :]
                link(dve.tensor_tensor(d[:, :, 1:S], zs[:, :, 0:S - 1], zs[:, :, 1:S], ALU.subtract))
                link(dve.tensor_scalar(d[:, :, 0:1], zs[:, :, 0:1], -1.0, None, ALU.mult))
                mu = cols("mu_shift")
                for m in range(14):
                    ins = dve.scalar_tensor_tensor(zs[:, m, :], d[:, m, :], mu[:, m:m + 1], zs[:, m, :], ALU.mult, ALU.add)
                link.announce(ins, shifted, 1)
                rr, kz = z[:, Z_R:Z_K, :], z[:, Z_K:Z_V, :]
                for m in range(4):
                    ins = dve.tensor_scalar(kk[:, m, :], kz[:, m, :], cols("k_k")[:, m:m + 1], None, ALU.mult)
                link(ins)
                dve.tensor_tensor(c[:], kk, kk, ALU.mult).then_inc(squares, 1)
                dve.wait_ge(gated, 8)
                for m in range(4):
                    ins = dve.tensor_scalar(kh[:, m, :], a[:, m, :], 1.0, cols("k_a")[:, m:m + 1], ALU.subtract, ALU.mult)
                link(ins)
                link(dve.scalar_tensor_tensor(kh, kh, 1.0, kz, ALU.add, ALU.mult))
                for m in range(4):
                    ins = dve.scalar_tensor_tensor(rk[:, m, :], rr[:, m, :], cols("r_k")[:, m:m + 1], kh[:, m, :], ALU.mult, ALU.mult)
                link(ins)
                dve.wait_ge(roots, 4)
                link(dve.tensor_scalar(eprev[:], eprev[:], 1e-12, None, ALU.max))
                link(dve.reciprocal(eprev[:], eprev[:]))
                link(dve.tensor_tensor(kk, kk, eprev[:], ALU.mult))
                link(dve.tensor_tensor(b, kk, a[:], ALU.mult))
                link(dve.tensor_scalar(ld[:], ld[:], -float(np.exp(-0.5)), None, ALU.mult))
                for m in range(RP):
                    for t in range(TT):
                        seg = slice(t * P, t * P + P)
                        ins = dve.tensor_tensor_scan(c[:, m, seg], ones[:], ld[:, m, seg], 0.0, ALU.mult, ALU.add)
                link(ins)
                c3, ld3 = c[:].rearrange("p m (t n) -> p (m t) n", n=P), ld[:].rearrange("p m (t n) -> p (m t) n", n=P)
                link(dve.tensor_copy(mid_e[:], c3[:, :, P // 2 - 1]))
                ins = dve.tensor_tensor(c3, c3, bcast(mid_e[:], P, 2), ALU.subtract)
                link.announce(ins, cums, 1)
                link.announce(dve.tensor_tensor(ld[:], c[:], ld[:], ALU.subtract), cums, 2)
                dve.wait_ge(exps, 1)
                cut = lambda ap: ap.rearrange("p m (t n) -> p m t n", n=P)
                link(dve.tensor_tensor(KR[:, :, :, 1, :], cut(rr), cut(einc), ALU.mult))
                dve.tensor_copy(end_e[:], einc.rearrange("p m (t n) -> p (m t) n", n=P)[:, :, P - 1])
                dve.wait_ge(exps, 2)
                dve.tensor_tensor(rr, b, eneg, ALU.mult)
                dve.tensor_tensor(kz, kh, eneg, ALU.mult)
                dve.wait_ge(exps, 3)
                dve.tensor_tensor(KR[:, :, :, 0, :], cut(kk), cut(eprev[:]), ALU.mult)


def rwkv_turn_stage(nc, k, z, g, KR, rk, kkT, bT, kdT, vT, bonus):
    with ExitStack() as stack:
        r = Room(nc, stack, "rturn")
        pt = [r.ps(f"pt{u}") for u in range(4)]
        pb = r.ps("pb")
        sel = r.sb("sel", [P, 2])
        loaded, turned, copied, summed = r.sem("loaded", "turned", "copied", "summed")
        kz, rr, vz = z[:, Z_K:Z_V, :], z[:, Z_R:Z_K, :], z[:, Z_V:Z_WA, :]
        units = [(src, dst, m) for src, dst in ((vz, vT), (rr, bT), (None, kkT), (kz, kdT)) for m in range(RP)]
        with nc.Block() as block:
            @block.sync
            def _(sp):
                sp.dma_start(sel[:], g["pair_sel"]).then_inc(loaded, 16)

            @block.tensor
            def _(pe):
                for n, (src, _, m) in enumerate(units):
                    if n >= 4:
                        pe.wait_ge(copied, n - 3)
                    for t in range(TT):
                        data = KR[:, m, t, 0, :] if src is None else src[:, m, t * P:(t + 1) * P]
                        last = pe.transpose(pt[n % 4][:, t * P:(t + 1) * P], data, k.ident[:])
                    last.then_inc(turned, 1)
                pe.wait_ge(loaded, 16)
                for t in range(TT):
                    for m in range(RP):
                        last = pe.matmul(pb[:, t * 8 + 2 * m:t * 8 + 2 * m + 2], rk[:, m, t * P:(t + 1) * P], sel[:], start=True, stop=True)
                last.then_inc(summed, 1)

            @block.vector
            def _(dve):
                for n, (_, dst, m) in enumerate(units):
                    dve.wait_ge(turned, max(n + 1, RP + 1 if n >= 3 * RP else 0))
                    dve.tensor_copy(dst[:, m, :, :], pt[n % 4][:].rearrange("p (t n) -> p t n", n=P)).then_inc(copied, 1)
                dve.wait_ge(summed, 1)
                dve.tensor_copy(bonus[:], pb[:, 0:TT * RH].rearrange("p (t h) -> p t h", h=RH))


def rwkv_solve_stage(nc, k, g, KR, Bd, Kd, kkT, bT, kdT, vT, mid_e, end_e, y):
    with ExitStack() as stack:
        r = Room(nc, stack, "rsolve")
        masks = r.sb("masks", [P, 5, P])
        MdT, Md, Moff, T, A2T, A3T, A4T, Pa, Pb, Pc, Pd = [
            r.sb(n, [P, RH, P]) for n in ("MdT", "Md", "Moff", "T", "A2T", "A3T", "A4T", "Pa", "Pb", "Pc", "Pd")]
        state = r.sb("state", [P, RP, RN])
        id64 = r.sb("id64", [P, RN])
        escale = r.sb("escale", [P, RP, TT])
        bank = [r.ps(f"bank{u}") for u in range(8)]
        loaded, made, taken, ready = r.sem("loaded", "made", "taken", "ready")
        STEPS = 27
        N, NT, X, X1, WU, RtT, PTI, Z = Md, MdT, Moff, Md, MdT, Pa, Pb, Pd

        def products(pe, c, step, h, out):
            o, m = divmod(h, 4)
            half = slice(o * RN, o * RN + RN)
            seg = slice(c * P, c * P + P)
            KKd, Rd = KR[half, m, c, 0, :], KR[half, m, c, 1, :]
            bd, kd = Bd[half, m, seg], Kd[half, m, seg]
            V, bt, kt = [x[:, m, c, half] for x in (vT, bT, kdT)]
            U0, W = WU[:, h, RN:P], WU[:, h, 0:RN]
            s0 = state[half, m, :]
            table = {
                0: [(bd, KKd)], 1: [(KKd, bd)], 2: [(kd, KKd)], 3: [(bd, Rd)], 4: [(kd, Rd)],
                5: [(MdT[:, h], Md[:, h])], 6: [(Md[:, h], MdT[:, h])], 7: [(Pa[:, h], T[:, h])],
                8: [(Pb[:, h], Pa[:, h])], 9: [(Pa[:, h], Pb[:, h])], 10: [(Pc[:, h], T[:, h])],
                11: [(Pd[:, h], Pc[:, h])], 12: [(Pa[:, h], T[:, h])],
                13: [(T[:, h], Moff[:, h])], 14: [(Moff[:, h], T[:, h])],
                15: [(NT[:, h], N[:, h])], 16: [(N[:, h], NT[:, h])], 17: [(Pa[:, h], Z[:, h])],
                18: [(Pb[:, h], Pa[:, h])], 19: [(Pc[:, h], Z[:, h])],
                20: [(A2T[:, h], V)], 21: [(T[:, h], X[:, h])], 22: [(Z[:, h], X1[:, h])],
                23: [(W, A3T[:, h])], 24: [(W, bt)],
                25: [(A3T[:, h], U0), (A4T[:, h], V), (RtT[half, m, :], s0)],
                26: [(bt, U0), (kt, V), (PTI[half, m, 0:RN], s0)],
            }[step]
            for n, (lhs, rhs) in enumerate(table):
                last = pe.matmul(out, lhs, rhs, start=n == 0, stop=n == len(table) - 1)
            return last

        def out_of(step, h, ps):
            o, m = divmod(h, 4)
            rows = slice(o * RN, o * RN + RN) if step in (23, 24, 26) else slice(0, P)
            return ps[rows, m * P:m * P + (RN if step in (20, 24, 25, 26) else P)]

        with nc.Block() as block:
            @block.sync
            def _(sp):
                sp.dma_start(masks[:], g["masks"].rearrange("m p n -> p m n")).then_inc(loaded, 16)
                sp.dma_start(id64[:], g["id64"]).then_inc(loaded, 16)

            @block.tensor
            def _(pe):
                pe.wait_ge(ready, 1)
                n = 0
                for c in range(TT):
                    for step in range(STEPS):
                        for hf in range(2):
                            if n >= 2:
                                pe.wait_ge(taken, n - 1)
                            for h in range(4 * hf, 4 * hf + 4):
                                last = products(pe, c, step, h, out_of(step, h, bank[n % 8]))
                            last.then_inc(made, 1)
                            n += 1

            @block.vector
            def _(dve):
                dve.wait_ge(loaded, 32)
                dve.memset(state[:], 0.0)
                dve.tensor_copy(escale[:, :, TT - 1:TT], end_e[:].rearrange("p (m t) -> p m t", t=TT)[:, :, TT - 1:TT])
                dve.tensor_tensor(escale[:, :, 0:TT - 1], end_e[:].rearrange("p (m t) -> p m t", t=TT)[:, :, 0:TT - 1],
                                  mid_e[:].rearrange("p (m t) -> p m t", t=TT)[:, :, 1:TT], ALU.mult).then_inc(ready, 1)
                dve.wait_ge(ready, 1)
                mask = lambda j: bcast(masks[:, j, :], 4, 1)
                ident = bcast(k.ident[:], 4, 1)
                n = 0
                for c in range(TT):
                    for step in range(STEPS):
                        for hf in range(2):
                            hs, half = slice(4 * hf, 4 * hf + 4), slice(RN * hf, RN * hf + RN)
                            full = bank[n % 8][:].rearrange("p (h n) -> p h n", n=P)
                            dve.wait_ge(made, n + 1)
                            tt, cp = dve.tensor_tensor, dve.tensor_copy
                            if step == 0:
                                tt(MdT[:, hs], full, mask(0), ALU.mult).then_inc(ready, 1)
                                dve.wait_ge(ready, 2 + 2 * c + hf)
                                ins = tt(T[:, hs], MdT[:, hs], ident, ALU.add)
                            elif step == 1:
                                tt(Md[:, hs], full, mask(1), ALU.mult)
                                ins = tt(Moff[:, hs], full, mask(2), ALU.mult)
                            elif step == 2:
                                ins = tt(A2T[:, hs], full, mask(3), ALU.mult)
                            elif step in (3, 4):
                                ins = tt((A3T if step == 3 else A4T)[:, hs], full, mask(4), ALU.mult)
                            elif step in (7, 10, 12):
                                ins = tt(T[:, hs], full, T[:, hs], ALU.add)
                            elif step in (17, 19):
                                ins = tt(Z[:, hs], full, Z[:, hs], ALU.add)
                            elif step in (5, 6, 8, 9, 11, 13, 15, 16, 18, 21):
                                dst = {5: Pa, 6: Pb, 8: Pc, 9: Pd, 11: Pa, 13: N, 15: Pa, 16: Pb, 18: Pc, 21: X1}[step]
                                ins = cp(dst[:, hs], full)
                            elif step == 14:
                                cp(NT[:, hs], full)
                                ins = tt(Z[:, hs], full, ident, ALU.add)
                            elif step == 20:
                                cp(X[:, hs, 0:RN], kkT[:, :, c, half])
                                ins = cp(X[:, hs, RN:P], full[:, :, 0:RN])
                            elif step == 22:
                                ins = dve.tensor_scalar(WU[:, hs], full, -1.0, None, ALU.mult)
                            elif step == 23:
                                ins = tt(RtT[half, 0:4], full[half], KR[half, :, c, 1, :], ALU.add)
                            elif step == 24:
                                ins = tt(PTI[half, 0:4, 0:RN], full[half, :, 0:RN], bcast(id64[half], 4, 1), ALU.add)
                            elif step == 25:
                                ins = cp(y[:, c].rearrange("p (m o) n -> p m o n", o=2)[:, :, hf, :], full[:, :, 0:RN])
                            else:
                                for m in range(RP):
                                    ins = dve.tensor_scalar(state[half, m, :], full[half, m, 0:RN], escale[half, m, c:c + 1], None, ALU.mult)
                            ins.then_inc(taken, 1)
                            n += 1


def rwkv_finish_stage(nc, k, g, y, v_tp, bonus, sgate, oT, bufs):
    with ExitStack() as stack:
        r = Room(nc, stack, "rfin")
        lnw, lnb, wg = r.sb("lnw", [P, S]), r.sb("lnb", [P, S]), r.sb("wg", [P, S])
        mean, var, root = [r.sb(n, [P, TT * RH]) for n in ("mean", "var", "root")]
        sq = r.sb("sq", [P, TT * RH, RN])
        ps = [r.ps(f"ps{u}") for u in range(8)]
        loaded, gates, vars_, roots, rows, turned, chain = r.sem("loaded", "gates", "vars", "roots", "rows", "turned", "chain")
        with nc.Block() as block:
            @block.sync
            def _(sp):
                sp.dma_start(lnw[:], g["ln_x_w"].to_broadcast([P, S])).then_inc(loaded, 16)
                sp.dma_start(lnb[:], g["ln_x_b"].to_broadcast([P, S])).then_inc(loaded, 16)
                sp.dma_start(wg[:], g["w_gate_up"]).then_inc(loaded, 16)

            @block.tensor
            def _(pe):
                pe.wait_ge(loaded, 48)
                for t in range(TT):
                    pe.matmul(ps[t][:], sgate[:, t * P:(t + 1) * P], wg[:], start=True, stop=True).then_inc(gates, 1)
                for m in range(4):
                    pe.wait_ge(rows, TT)
                    for t in range(TT):
                        last = pe.transpose(ps[4 + m][:, t * P:(t + 1) * P], y[:, t, 2 * m:2 * m + 2, :].rearrange("p h n -> p (h n)"), k.ident[:])
                    last.then_inc(turned, 1)

            @block.scalar
            def _(act):
                act.wait_ge(vars_, 1)
                act.activation(root[:], var[:], ACT.Sqrt).then_inc(roots, 1)
                for m in range(4):
                    act.wait_ge(turned, m + 1)
                    act.activation(oT[:, m, :], ps[4 + m][:], ACT.Copy)

            @block.vector
            def _(dve):
                link = Chain(dve, chain)
                yg = y[:].rearrange("p t h n -> p (t h) n")
                link(dve.reduce_sum(mean[:], yg, AX))
                link(dve.tensor_scalar(mean[:], mean[:], 1.0 / RN, None, ALU.mult))
                link(dve.tensor_tensor(yg, yg, bcast(mean[:], RN, 2), ALU.subtract))
                link(dve.tensor_tensor(sq[:], yg, yg, ALU.mult))
                link(dve.reduce_sum(var[:], sq[:], AX))
                dve.tensor_scalar(var[:], var[:], 1.0 / RN, GN_EPS, ALU.mult, ALU.add).then_inc(vars_, 1)
                dve.wait_ge(roots, 1)
                link(dve.reciprocal(root[:], root[:]))
                link(dve.tensor_tensor(yg, yg, bcast(root[:], RN, 2), ALU.mult))
                dve.wait_ge(loaded, 48)
                yt = y[:].rearrange("p t h n -> p t (h n)")
                link(dve.tensor_tensor(yt, yt, bcast(lnw[:], TT, 1), ALU.mult))
                link(dve.tensor_tensor(yt, yt, bcast(lnb[:], TT, 1), ALU.add))
                v4 = v_tp.rearrange("p m t (o n) -> p m t o n", n=RN)
                s4 = sq[:].rearrange("p (t m o) n -> p t m o n", m=RP, o=2)
                b4 = bonus[:].rearrange("p t (m o) -> p t m o", o=2)
                for t in range(TT):
                    ins = dve.tensor_tensor(s4[:, t], v4[:, :, t], bcast(b4[:, t], RN, 3), ALU.mult)
                link(ins)
                link(dve.tensor_tensor(yg, yg, sq[:], ALU.add))
                for t in range(TT):
                    dve.wait_ge(gates, t + 1)
                    dve.tensor_tensor(yt[:, t], yt[:, t], ps[t][:], ALU.mult).then_inc(rows, 1)


def merge_stage(nc, name, z, gate0, branches, out, kc=4):
    nb = len(branches)
    with ExitStack() as stack:
        r = Room(nc, stack, name)
        w = [[r.sb(f"w{i}_{u}", [P, kc, P]) for u in range(2)] for i in range(nb)]
        part = r.sb("part", [P, nb, S])
        ps = [[r.ps(f"ps{i}_{u}") for u in range(2)] for i in range(nb)]
        made, taken, chain = r.sem("made", "taken", "chain")
        w_ready = [[r.sem(f"w_ready{i}_{u}") for u in range(2)] for i in range(nb)]
        srcs = [w_dram.rearrange("(c p) (m n) -> m p c n", p=P, n=P) for w_dram, _ in branches]
        with nc.Block() as block:
            @block.sync
            def _(sp):
                for m in range(DC):
                    for i in range(nb):
                        if m >= 2:
                            sp.wait_ge(made, nb * (m - 2) + i + 1)
                        sp.dma_start(w[i][m % 2][:], srcs[i][m]).then_inc(w_ready[i][m % 2], 16)

            @block.tensor
            def _(pe):
                for m in range(DC):
                    for i, (_, o) in enumerate(branches):
                        pe.wait_ge(w_ready[i][m % 2], 16 * (m // 2 + 1))
                        if m >= 2:
                            pe.wait_ge(taken, m - 1)
                        for c in range(kc):
                            last = pe.matmul(ps[i][m % 2][:], w[i][m % 2][:, c, :], o[:, c, :], start=c == 0, stop=c == kc - 1)
                        last.then_inc(made, 1)

            @block.vector
            def _(dve):
                link = Chain(dve, chain)
                for m in range(DC):
                    for i in range(nb):
                        dve.wait_ge(made, nb * m + i + 1)
                        ins = dve.tensor_tensor(part[:, i, :], ps[i][m % 2][:], z[:, gate0 + i * DC + m, :], ALU.mult)
                        if i == nb - 1:
                            ins.then_inc(taken, 1)
                            dve.wait_ge(taken, m + 1)
                    for i in range(1, nb):
                        last = i == nb - 1
                        link(dve.tensor_tensor(out[:, m, :] if last else part[:, 0, :], part[:, 0, :], part[:, i, :], ALU.add))


def squash_stage(nc, name, z, c0, n, bias=None):
    with nc.Block() as block:
        @block.scalar
        def _(act):
            for m in range(n):
                extra = {} if bias is None else {"bias": bias[:, m:m + 1]}
                act.activation(z[:, c0 + m, :], z[:, c0 + m, :], ACT.Sigmoid, **extra)

def choose_stage(nc, name, k, g, qT, keys_in, keys_of, e1T, e2T, gT):
    with ExitStack() as stack:
        r = Room(nc, stack, name)
        nkeys = keys_in.shape[1]
        keys = r.sb("keys", [P, nkeys, NK])
        v, idx, left = r.sb("v", [P, 2 * PH, K16]), r.sb("idx", [P, 2 * PH, K16], U32), r.sb("left", [P, 2, NK])
        idf = r.sb("idf", [P, 2 * PH, K16])
        cand, cleft = r.sb("cand", [P, PH, 256]), r.sb("cleft", [P, PH, 256])
        tv, pos = r.sb("tv", [P, PH, K16]), r.sb("pos", [P, PH, K16], U32)
        part, partf = r.sb("part", [P, 2, PH * K16], U32), r.sb("partf", [P, 2, PH * K16])
        iota, hit = r.sb("iota", [P, K16]), r.sb("hit", [P, PH * K16, K16])
        found = r.sb("found", [P, 2, 3, NJ])
        total = r.sb("total", [P, PH])
        ps = [r.ps(f"ps{u}") for u in range(4)]
        pt = r.ps("pt")
        loaded, scored, read, centred, exped, chosen, turned, kept, chain = r.sem(
            "loaded", "scored", "read", "centred", "exped", "chosen", "turned", "kept", "chain")
        scores = lambda c: ps[c // 4][:, (c % 4) * NK:(c % 4 + 1) * NK]
        with nc.Block() as block:
            @block.sync
            def _(sp):
                sp.dma_start(keys[:], keys_in).then_inc(loaded, 16)
                sp.dma_start(iota[:], g["iota16"].to_broadcast([P, K16])).then_inc(loaded, 16)

            @block.tensor
            def _(pe):
                pe.wait_ge(loaded, 32)
                for t in range(TT + 1):
                    if t:
                        pe.wait_ge(read, t)
                    for c in range(2 * PH if t < TT else 0):
                        last = pe.matmul(scores(c), qT[:, c, t * P:(t + 1) * P], keys[:, keys_of(c), :], start=True, stop=True)
                    if t < TT:
                        last.then_inc(scored, 1)
                    if t:
                        pe.wait_ge(chosen, t)
                        if t > 1:
                            pe.wait_ge(kept, t - 1)
                        for j in range(3):
                            last = pe.transpose(pt[:, j * P:(j + 1) * P], found[:, (t - 1) % 2, j, :], k.ident[:])
                        last.then_inc(turned, 1)

            @block.scalar
            def _(act):
                for t in range(TT):
                    act.wait_ge(centred, t + 1)
                    act.activation(tv[:], tv[:], ACT.Exp).then_inc(exped, 1)
                    act.wait_ge(turned, t + 1)
                    for j, dst in enumerate((e1T, e2T, gT)):
                        ins = act.activation(dst[:, t * P:(t + 1) * P], pt[:, j * P:(j + 1) * P], ACT.Copy)
                    ins.then_inc(kept, 1)

            @block.vector
            def _(dve):
                link = Chain(dve, chain)
                dve.wait_ge(loaded, 32)
                for t in range(TT):
                    def top16(vals, index, data, rest):
                        link(dve.max(vals[:, 0:8], data))
                        link(dve.max_index(index[:, 0:8], vals[:, 0:8], data))
                        link(dve.match_replace(rest, vals[:, 0:8], data, -3e38))
                        link(dve.max(vals[:, 8:16], rest))
                        link(dve.max_index(index[:, 8:16], vals[:, 8:16], rest))

                    dve.wait_ge(scored, t + 1)
                    for c in range(2 * PH):
                        top16(v[:, c], idx[:, c], scores(c), left[:, c % 2, :])
                    link.eng.sem_inc(read, 1)
                    v4 = v[:].rearrange("p (h s) n -> p h s n", s=2)
                    link(dve.tensor_tensor(cand[:].rearrange("p h (a b) -> p h a b", b=K16),
                                           bcast(v4[:, :, 0, :], K16, 3), bcast(v4[:, :, 1, :], K16, 2), ALU.add))
                    for h in range(PH):
                        top16(tv[:, h], pos[:, h], cand[:, h], cleft[:, h])
                    posf = pos[:].rearrange("p h n -> p (h n)")
                    link(dve.tensor_single_scalar(part[:, 0], posf, 4, ALU.logical_shift_right))
                    link(dve.tensor_single_scalar(part[:, 1], posf, 15, ALU.bitwise_and))
                    link(dve.tensor_copy(partf[:], part[:]))
                    link(dve.tensor_copy(idf[:], idx[:]))
                    ins = dve.tensor_copy(total[:], tv[:, :, 0])
                    link(ins)
                    id4 = idf[:].rearrange("p (h s) n -> p h s n", s=2)
                    hit4 = hit[:].rearrange("p (h n) a -> p h n a", h=PH)
                    if t >= 2:
                        dve.wait_ge(turned, t - 1)
                    for s in range(2):
                        link(dve.tensor_tensor(hit[:], bcast(partf[:, s], K16, 2), bcast(iota[:], NJ, 1), ALU.is_equal))
                        link(dve.tensor_tensor(hit4, hit4, bcast(id4[:, :, s, :], K16, 2), ALU.mult))
                        link(dve.reduce_sum(found[:, t % 2, s, :], hit[:], AX))
                    dve.tensor_tensor(tv[:], tv[:], bcast(total[:], K16, 2), ALU.subtract).then_inc(centred, 1)
                    dve.wait_ge(exped, t + 1)
                    link(dve.reduce_sum(total[:], tv[:], AX))
                    link(dve.reciprocal(total[:], total[:]))
                    dve.tensor_tensor(found[:, t % 2, 2, :].rearrange("p (h n) -> p h n", h=PH), tv[:], bcast(total[:], K16, 2), ALU.mult).then_inc(chosen, 1)


def spread_stage(nc, name, g, e1T, e2T, gT, gates_dram):
    with ExitStack() as stack:
        r = Room(nc, stack, name)
        iota = r.sb("iota", [P, NK])
        oh1, oh2 = [[r.sb(f"oh{x}_{u}", [P, 4, NK]) for u in range(2)] for x in (1, 2)]
        tile = [r.sb(f"tile{u}", [P, NK, SUB]) for u in range(2)]
        ps = [r.ps(f"ps{u}") for u in range(4)]
        loaded, hot1, hot2, made, kept = r.sem("loaded", "hot1", "hot2", "made", "kept")
        stored = [r.sem(f"stored{u}") for u in range(2)]
        GROUPS = SUB // 4
        with nc.Block() as block:
            @block.sync
            def _(sp):
                sp.dma_start(iota[:], g["iota128"].to_broadcast([P, NK])).then_inc(loaded, 16)
                for u in range(2):
                    sp.sem_inc(stored[u], 16)
                with sp.Fori(0, S // SUB // 2) as i:
                    for u in range(2):
                        sp.wait_ge(kept, 2 * GROUPS * i + GROUPS * (u + 1) + 4)
                        sp.dma_start(gates_dram[ds(2 * i + u, 1)].rearrange("a p e t -> (a p) e t"), tile[u][:]).then_inc(stored[u], 16)
                for u in range(2):
                    sp.wait_ge(stored[u], 16 * (S // SUB // 2) + 16)

            def turns(eng, body):
                with eng.Fori(0, S // SUB // 2) as i:
                    for u in range(2):
                        if eng is acting[0]:
                            eng.wait_ge(stored[u], 16 * i + 16)
                        with eng.Fori(0, GROUPS // 4) as j:
                            for b in range(4):
                                body(2 * GROUPS * i + GROUPS * u + 4 * j + b, u, 4 * j + b, b)

            acting = [None]

            @block.vector
            def _(dve):
                dve.wait_ge(loaded, 16)

                def body(n, u, q, b):
                    dve.wait_ge(made, n + 1)
                    for x in range(4):
                        tok = ds(4 * n + x, 1)
                        ins = dve.tensor_scalar(oh1[b % 2][:, x, :], iota[:], e1T[:, tok], gT[:, tok], ALU.is_equal, ALU.mult)
                    ins.then_inc(hot1, 1)
                    for x in range(4):
                        tok = ds(4 * n + x, 1)
                        ins = dve.tensor_scalar(oh2[b % 2][:, x, :], iota[:], e2T[:, tok], None, ALU.is_equal)
                    ins.then_inc(hot2, 1)

                turns(dve, body)

            @block.tensor
            def _(pe):
                def body(n, u, q, b):
                    pe.wait_ge(hot1, n + 1)
                    pe.wait_ge(hot2, n + 1)
                    pe.wait_ge(kept, n + 1)
                    for x in range(4):
                        last = pe.matmul(ps[b][:, x * NK:(x + 1) * NK], oh2[b % 2][:, x, :], oh1[b % 2][:, x, :], start=True, stop=True)
                    last.then_inc(made, 1)

                pe.sem_inc(made, 2)
                turns(pe, body)

            @block.scalar
            def _(act):
                acting[0] = act

                def body(n, u, q, b):
                    act.wait_ge(made, n + 3)
                    act.activation(tile[u][:, :, ds(q * 4, 4)].rearrange("p e t -> p t e"),
                                   ps[b][:].rearrange("p (t e) -> p t e", e=NK), ACT.Copy).then_inc(kept, 1)

                act.sem_inc(kept, 4)
                turns(act, body)


def wait_above(eng, sem, value):
    if not isinstance(value, int) or value > 0:
        eng.wait_ge(sem, value)


def experts_stage(nc, name, k, hT, downT, up, gates_dram, acc, gelu):
    NB = NK
    IT = NB // 8
    with ExitStack() as stack:
        r = Room(nc, stack, name)
        hhi, hlo = r.sb("hhi", [P, DC, S], F32R), r.sb("hlo", [P, DC, S], F32R)
        uraw, uhi, ulo = [[r.sb(f"{n}{u}", [P, DC, P], dt) for u in range(2)] for n, dt in (("uraw", F32), ("uhi", F32R), ("ulo", F32R))]
        vraw = [r.sb(f"vraw{u}", [P, D]) for u in range(2)]
        vhi, vlo = r.sb("vhi", [P, 4, D], F32R), r.sb("vlo", [P, 4, D], F32R)
        gate = [r.sb(f"gate{u}", [P, S // SUB, 4, SUB]) for u in range(2)]
        actv = [r.sb(f"act{u}", [P, S]) for u in range(2)]
        wfull = [r.sb(f"w{u}", [P, S]) for u in range(2)]
        whi, wlo = [[r.sb(f"{n}{u}", [P, 4, S], F32R) for u in range(2)] for n in ("whi", "wlo")]
        pa = [r.ps(f"pa{u}") for u in range(2)]
        po = [r.ps(f"po{u}") for u in range(4)]
        u_hi, u_lo, v_hi, v_lo, a_made, act_made, w_made, w_hi, w_lo, o_made, o_added, h_hi, h_lo = r.sem(
            "u_hi", "u_lo", "v_hi", "v_lo", "a_made", "act_made", "w_made", "w_hi", "w_lo", "o_made", "o_added", "h_hi", "h_lo")
        u_in, v_in, g_in = [[r.sem(f"{n}{u}") for u in range(2)] for n in ("u_in", "v_in", "g_in")]

        def loop(eng, body):
            body(0)
            with eng.Fori(1, IT - 1) as i:
                body(i)
            body(IT - 1)

        last_turn = lambda i: isinstance(i, int) and i == IT - 1

        with nc.Block() as block:
            @block.sync
            def _(sp):
                def body(i):
                    for j in range(8):
                        n = 8 * i + j
                        if j % 4 == 0:
                            grp, gp = 2 * i + j // 4, j // 4
                            wait_above(sp, w_made, 4 * grp - 4)
                            src = gates_dram[:, :, ds(4 * grp, 4), :] if not isinstance(grp, int) else gates_dram[:, :, 4 * grp:4 * grp + 4, :]
                            sp.dma_start(gate[gp][:], src.rearrange("s p e t -> p s e t")).then_inc(g_in[gp], 16)
                        wait_above(sp, u_lo, n - 1)
                        src = downT[n] if isinstance(n, int) else downT[ds(n, 1)].rearrange("a p c e -> (a p) c e")
                        sp.dma_start(uraw[j % 2][:], src).then_inc(u_in[j % 2], 16)

                loop(sp, body)

            @block.scalar
            def _(act):
                def split_u(n, j):
                    act.wait_ge(u_in[j % 2], 8 * n + 16 - 8 * (j % 2))
                    wait_above(act, a_made, n - 1)
                    act.activation(uhi[j % 2][:], uraw[j % 2][:], ACT.Copy).then_inc(u_hi, 1)

                def split_v(n, j):
                    act.wait_ge(v_in[j % 2], 8 * n + 16 - 8 * (j % 2))
                    wait_above(act, o_made, 2 * (n - j % 4))
                    act.activation(vhi[:, j % 4, :], vraw[j % 2][:], ACT.Copy).then_inc(v_hi, 1)

                def load_v(n, j):
                    wait_above(act, v_lo, n - 1)
                    src = up[n] if isinstance(n, int) else up[ds(n, 1)].rearrange("a p d -> (a p) d")
                    act.dma_start(vraw[j % 2][:], src).then_inc(v_in[j % 2], 16)

                def body(i):
                    for j in range(8):
                        n = 8 * i + j
                        act.wait_ge(a_made, n + 1)
                        wait_above(act, w_made, n - 1)
                        act.activation(actv[j % 2][:], pa[j % 2][:], gelu).then_inc(act_made, 1)
                        if not (last_turn(i) and j >= 6):
                            split_u(n + 2, (j + 2) % 8)
                        if j % 4 != 1 and not (last_turn(i) and j == 7):
                            load_v(n + 1, j + 1)
                        act.wait_ge(w_made, n + 1)
                        act.activation(whi[j // 4][:, j % 4, :], wfull[j % 2][:], ACT.Copy).then_inc(w_hi, 1)
                        if j % 4 == 1:
                            split_v(n - 1, j - 1)
                        if j % 4:
                            split_v(n, j)
                        if j % 4 == 1:
                            load_v(n + 1, j + 1)

                load_v(0, 0)
                for c in range(DC):
                    act.activation(hhi[:, c, :], hT[:, c, :], ACT.Copy).then_inc(h_hi, 1)
                split_u(0, 0)
                split_u(1, 1)
                loop(act, body)

            @block.vector
            def _(dve):
                def split_u(n, j):
                    dve.wait_ge(u_hi, n + 1)
                    dve.tensor_tensor(ulo[j % 2][:], uraw[j % 2][:], uhi[j % 2][:].bitcast(F32), ALU.subtract).then_inc(u_lo, 1)

                def split_v(n, j):
                    dve.wait_ge(v_hi, n + 1)
                    dve.tensor_tensor(vlo[:, j % 4, :], vraw[j % 2][:], vhi[:, j % 4, :].bitcast(F32), ALU.subtract).then_inc(v_lo, 1)

                def add_group(grp):
                    for d in range(DC):
                        dve.wait_ge(o_made, 8 * grp + d + 1)
                        dve.tensor_tensor(acc[:, d, :], po[d % 4][:], acc[:, d, :], ALU.add).then_inc(o_added, 1)

                def body(i):
                    for j in range(8):
                        n, grp = 8 * i + j, 2 * i + j // 4
                        if j % 4 == 0:
                            dve.wait_ge(g_in[j // 4], 16 * i + 16)
                        dve.wait_ge(act_made, n + 1)
                        wait_above(dve, w_lo, n - 1)
                        q3 = lambda ap: ap.rearrange("p (s t) -> p s t", t=SUB)
                        dve.tensor_tensor(q3(wfull[j % 2][:]), q3(actv[j % 2][:]), gate[j // 4][:, :, j % 4, :], ALU.mult).then_inc(w_made, 1)
                        if not (last_turn(i) and j >= 6):
                            split_u(n + 2, (j + 2) % 8)
                        dve.wait_ge(w_hi, n + 1)
                        dve.tensor_tensor(wlo[j // 4][:, j % 4, :], wfull[j % 2][:], whi[j // 4][:, j % 4, :].bitcast(F32), ALU.subtract).then_inc(w_lo, 1)
                        if j % 4 == 1:
                            split_v(n - 1, j - 1)
                        if j % 4:
                            split_v(n, j)
                        if j % 4 == 0 and not (isinstance(n, int) and n == 0):
                            add_group(grp - 1)

                dve.memset(acc[:], 0.0)
                for c in range(DC):
                    dve.wait_ge(h_hi, c + 1)
                    dve.tensor_tensor(hlo[:, c, :], hT[:, c, :], hhi[:, c, :].bitcast(F32), ALU.subtract).then_inc(h_lo, 1)
                split_u(0, 0)
                split_u(1, 1)
                loop(dve, body)
                add_group(NB // 4 - 1)

            @block.tensor
            def _(pe):
                def down(n, j):
                    pe.wait_ge(u_lo, n + 1)
                    wait_above(pe, act_made, n - 1)
                    a = pa[j % 2][:]
                    for c in range(DC):
                        hi, lo = uhi[j % 2][:, c, :], ulo[j % 2][:, c, :]
                        pe.matmul(a, hi, hhi[:, c, :], start=c == 0, stop=False)
                        pe.matmul(a, hi, hlo[:, c, :], start=False, stop=False)
                        last = pe.matmul(a, lo, hhi[:, c, :], start=False, stop=c == DC - 1)
                    last.then_inc(a_made, 1)

                def up_group(grp, gp):
                    pe.wait_ge(w_lo, 4 * grp + 4)
                    pe.wait_ge(v_lo, 4 * grp + 4)
                    for d in range(DC):
                        wait_above(pe, o_added, 8 * grp + d - 3)
                        for q in range(4):
                            hi, lo = vhi[:, q, d * P:(d + 1) * P], vlo[:, q, d * P:(d + 1) * P]
                            o = po[d % 4][:]
                            pe.matmul(o, hi, whi[gp][:, q, :], start=q == 0, stop=False)
                            pe.matmul(o, hi, wlo[gp][:, q, :], start=False, stop=False)
                            last = pe.matmul(o, lo, whi[gp][:, q, :], start=False, stop=q == 3)
                        last.then_inc(o_made, 1)

                def body(i):
                    for j in range(8):
                        n, grp = 8 * i + j, 2 * i + j // 4
                        down(n, j)
                        if j % 4 == 0 and not (isinstance(n, int) and n == 0):
                            up_group(grp - 1, 1 - j // 4)

                pe.wait_ge(h_lo, DC)
                loop(pe, body)
                up_group(NB // 4 - 1, 1)


def residual_stage(nc, name, x, acc, gain=None):
    with ExitStack() as stack:
        r = Room(nc, stack, name)
        with nc.Block() as block:
            @block.vector
            def _(dve):
                for c in range(DC):
                    if gain is None:
                        dve.tensor_tensor(x[:, c, :], x[:, c, :], acc[:, c, :], ALU.add)
                    else:
                        dve.scalar_tensor_tensor(x[:, c, :], acc[:, c, :], gain[:, c:c + 1], x[:, c, :], ALU.mult, ALU.add)


def peer(nc, name, k, ins, xT, hT, w_query, keys, keys_of, downT, up, gates_dram, gelu, gain=None):
    with ExitStack() as stack:
        r = Room(nc, stack, name)
        e1T, e2T, gT = r.sb("e1T", [P, S]), r.sb("e2T", [P, S]), r.sb("gT", [P, S])
        with ExitStack() as inner:
            qT = Room(nc, inner, name).sb("qT", [P, 2 * PH, S])
            project_stage(nc, name + "q", w_query, hT, DC, 2 * PH, qT)
            choose_stage(nc, name + "c", k, ins, qT, keys, keys_of, e1T, e2T, gT)
        spread_stage(nc, name + "s", ins, e1T, e2T, gT, gates_dram)
    with ExitStack() as stack:
        acc = Room(nc, stack, name).sb("acc", [P, DC, S])
        experts_stage(nc, name + "e", k, hT, downT, up, gates_dram, acc, gelu)
        residual_stage(nc, name + "r", xT, acc, gain)

def head_norm_stage(nc, name, k, chunks, tokens=S):
    N = len(chunks)
    with ExitStack() as stack:
        r = Room(nc, stack, name)
        sq, mean, root = [[r.sb(f"{n}{u}", [P, tokens]) for u in range(2)] for n in ("sq", "mean", "root")]
        gains = r.sb("gains", [P, N])
        ps = [r.ps(f"ps{u}") for u in range(2)]
        squared, summed, mean_ready, rooted, done, chain = r.sem("squared", "summed", "mean_ready", "rooted", "done", "chain")
        with nc.Block() as block:
            @block.scalar
            def _(act):
                for n in range(N + 1):
                    if n < N:
                        if n >= 2:
                            act.wait_ge(summed, n - 1)
                        act.activation(sq[n % 2][:], chunks[n][0], ACT.Square).then_inc(squared, 1)
                    if n >= 1:
                        act.wait_ge(mean_ready, n)
                        act.activation(root[(n - 1) % 2][:], mean[(n - 1) % 2][:], ACT.Sqrt).then_inc(rooted, 1)

            @block.tensor
            def _(pe):
                for n, (_, _, width, _) in enumerate(chunks):
                    pe.wait_ge(squared, n + 1)
                    if n >= 2:
                        pe.wait_ge(mean_ready, n - 1)
                    ones = k.ones if width == P else k.pair_ones
                    pe.matmul(ps[n % 2][:, 0:tokens], ones[:], sq[n % 2][:], start=True, stop=True).then_inc(summed, 1)

            @block.vector
            def _(dve):
                link = Chain(dve, chain)

                def finish(n):
                    chunk = chunks[n][0]
                    dve.wait_ge(rooted, n + 1)
                    link(dve.reciprocal(root[n % 2][:], root[n % 2][:]))
                    dve.scalar_tensor_tensor(chunk, chunk, gains[:, n:n + 1], root[n % 2][:], ALU.mult, ALU.mult).then_inc(done, 1)

                for n, (_, gain, _, times) in enumerate(chunks):
                    ins = dve.tensor_scalar(gains[:, n:n + 1], gain, times, None, ALU.mult)
                link(ins)
                for n in range(N + 1):
                    if n < N:
                        if n >= 2:
                            dve.wait_ge(done, n - 1)
                        dve.wait_ge(summed, n + 1)
                        dve.tensor_scalar(mean[n % 2][:], ps[n % 2][:, 0:tokens], 1.0 / chunks[n][2], EPS, ALU.mult, ALU.add).then_inc(mean_ready, 1)
                    if n >= 1:
                        finish(n - 1)


def turn_stage(nc, name, k, units):
    with ExitStack() as stack:
        r = Room(nc, stack, name)
        pt = [r.ps(f"pt{u}") for u in range(4)]
        turned, copied = r.sem("turned", "copied")
        with nc.Block() as block:
            @block.tensor
            def _(pe):
                for n, (srcs, _) in enumerate(units):
                    if n >= 4:
                        pe.wait_ge(copied, n - 3)
                    for j, src in enumerate(srcs):
                        last = pe.transpose(pt[n % 4][:, j * P:(j + 1) * P], src, k.ident[:])
                    last.then_inc(turned, 1)

            @block.vector
            def _(dve):
                for n, (srcs, dst) in enumerate(units):
                    dve.wait_ge(turned, n + 1)
                    dve.tensor_copy(dst, pt[n % 4][:, 0:len(srcs) * P].rearrange("p (t n) -> p t n", n=P)).then_inc(copied, 1)


def forget_stage(nc, k, z, bias, fq, fk):
    with ExitStack() as stack:
        r = Room(nc, stack, "forget")
        v, low, mag, c, neg, ones = [r.sb(n, [FH, S]) for n in ("v", "low", "mag", "c", "neg", "ones")]
        raised, absed, logged, summed, filled, moved, chain = r.sem("raised", "absed", "logged", "summed", "filled", "moved", "chain")
        with nc.Block() as block:
            @block.scalar
            def _(act):
                act.wait_ge(raised, 1)
                act.activation(mag[:], v[:], ACT.Abs).then_inc(absed, 1)
                act.wait_ge(absed, 1)
                act.activation(mag[:], mag[:], ACT.Exp, scale=-1.0).then_inc(absed, 1)
                act.wait_ge(absed, 2)
                act.activation(mag[:], mag[:], ACT.Ln, bias=1.0).then_inc(logged, 1)

            @block.vector
            def _(dve):
                link = Chain(dve, chain)
                dve.memset(fq, 1.0)
                dve.memset(fk, 1.0).then_inc(filled, 1)
                dve.memset(ones[:], 1.0)
                link.announce(dve.tensor_scalar(v[:], z[0:FH, Y_FF, :], bias, None, ALU.add), raised, 1)
                link(dve.tensor_scalar(low[:], v[:], 0.0, None, ALU.min))
                dve.wait_ge(logged, 1)
                link(dve.tensor_tensor(low[:], low[:], mag[:], ALU.subtract))
                link(dve.tensor_tensor_scan(c[:], ones[:], low[:], 0.0, ALU.mult, ALU.add))
                dve.tensor_scalar(neg[:], c[:], -1.0, None, ALU.mult).then_inc(summed, 1)

            @block.sync
            def _(sp):
                sp.wait_ge(summed, 1)
                sp.wait_ge(filled, 1)
                for h in range(FH):
                    sp.dma_start(fq[0:1, h, :], c[h:h + 1, :]).then_inc(moved, 16)
                    sp.dma_start(fk[1:2, h, :], neg[h:h + 1, :]).then_inc(moved, 16)
                sp.wait_ge(moved, 2 * 16 * FH)


def second_mixer(nc, k, ins, cols, xT, hT):
    with ExitStack() as mixer:
        m = Room(nc, mixer, "mix2")
        z = m.sb("z", [P, Y_N, S])
        project_stage(nc, "p2", ins["w_in_2"], hT, DC, Y_N, z)
        foxT, swaT, memT = m.sb("foxT", [P, 4, S]), m.sb("swaT", [P, 4, S]), m.sb("memT", [P, 4, S])
        heads = [(z[:, Y_FQ + i, :], cols("fox_q_g"), FD, FD ** -0.5) for i in range(4)]
        heads += [(z[:, Y_FK + i, :], cols("fox_k_g"), FD, 1.0) for i in range(4)]
        heads += [(z[:, Y_SQ + i, :], cols("swa_q_g"), SD, SD ** -0.5) for i in range(4)]
        heads += [(z[:, Y_SKV, :], cols("swa_k_g"), SD, 1.0)]
        heads += [(z[:, Y_MQ + i, :], cols("mem_q_g"), GD, GD ** -0.5) for i in range(4)]
        head_norm_stage(nc, "hn", k, heads)
        tiles = lambda chunk: [chunk[:, t * P:(t + 1) * P] for t in range(chunk.shape[-1] // P)]
        with ExitStack() as local, ExitStack() as fox:
            vs, a = Room(nc, local, "local"), Room(nc, fox, "fox")
            v_tp = vs.sb("v", [P, 5, TT, P])
            fq, fk = hT[0:2], a.sb("fk", [2, FH, S])[:]
            forget_stage(nc, k, z, cols("b_forget")[0:FH], fq, fk)
            turn_stage(nc, "vt", k, [(tiles(z[:, Y_FV + i, :]), v_tp[:, i]) for i in range(4)] + [(tiles(z[:, Y_SKV + 1, :]), v_tp[:, 4])])
            items = []
            for h in range(FH):
                c, half = h // 2, slice(h % 2 * FD, h % 2 * FD + FD)
                for t in range(TT):
                    items.append((z[half, Y_FQ + c, t * P:(t + 1) * P], z[half, Y_FK + c, 0:(t + 1) * P], k.causal[:],
                                  [v_tp[:, c, j, half] for j in range(t + 1)], h, t,
                                  (fq[:, h, t * P:(t + 1) * P], fk[:, h, 0:(t + 1) * P])))
            attention_stage(nc, "foxa", k, items, FH, FD, foxT)
            fox.close()
            alibi, sinks = vs.sb("alibi", [P, SH, 2 * P]), vs.sb("sinks", [P, SH])
            load_stage(nc, "swal", [(alibi[:], ins["alibi"]), (sinks[:], ins["swa_sinks"].to_broadcast([P, SH]))])
            items = []
            for h in range(SH):
                grp = h // (SH // SG)
                half = slice(grp * SD, grp * SD + SD)
                for t in range(TT):
                    k0 = max(t - 1, 0)
                    items.append((z[half, Y_SQ + h % 4, t * P:(t + 1) * P], z[half, Y_SKV, k0 * P:(t + 1) * P],
                                  alibi[:, h, (0 if t else P):2 * P], [v_tp[:, 4, j, half] for j in range(k0, t + 1)], h, t, None))
            attention_stage(nc, "swaa", k, items, SH, SD, swaT, sinks=sinks)
        with ExitStack() as memory:
            a = Room(nc, memory, "mem")
            mT = hT[:, :, 0:NMEM]
            mkv, mv = a.sb("mkv", [P, DC, NMEM]), a.sb("mv", [P, 4, 2, P])
            load_stage(nc, "meml", [(mT, ins["memT"].rearrange("(c p) t -> p c t", p=P))])
            norm_stage(nc, "mn", k, mT, DC, D, cols("mem_norm_g_2"), mT, tokens=NMEM)
            project_stage(nc, "mp", ins["w_mem_kv"], mT, DC, DC, mkv, tokens=NMEM)
            head_norm_stage(nc, "mh", k, [(mkv[:, i, :], cols("mem_k_g"), GD, 1.0) for i in range(4)], tokens=NMEM)
            turn_stage(nc, "mt", k, [(tiles(mkv[:, 4 + i, :]), mv[:, i]) for i in range(4)])
            items = [(z[:, Y_MQ + h, t * P:(t + 1) * P], mkv[:, h, :], None, [mv[:, h, j, :] for j in range(2)], h, t, None)
                     for h in range(GH) for t in range(TT)]
            attention_stage(nc, "mema", k, items, GH, GD, memT)
        squash_stage(nc, "sg2", z, Y_GATE, 3 * DC, bias=cols("b_gate_2"))
        merge_stage(nc, "mg2", z, Y_GATE, [(ins["w_fox_o"], foxT), (ins["w_swa_o"], swaT), (ins["w_mem_o"], memT)], hT)
    project_stage(nc, "po2", ins["w_out_2"], hT, DC, DC, xT, add=(k.ones, xT))

def y_of(t):
    return t[:].rearrange("p t (h n) -> p t h n", n=RN)


class Held:
    pass


def build(nc, ins, where, out):
    with ExitStack() as whole:
        r = Room(nc, whole, "held")
        k = Held()
        k.ident, k.ones = r.sb("ident", [P, P]), r.sb("ones", [P, P])
        k.columns = r.sb("columns", [P, ins["columns"].shape[1]])
        k.causal, k.pair_ones = r.sb("causal", [P, P]), r.sb("pair_ones", [P, P])
        xT, hT, mod = r.sb("xT", [P, DC, S]), r.sb("hT", [P, DC, S]), r.sb("mod", [P, 48])
        gain = r.sb("gain", [P, DC])
        cols = lambda n: k.columns[:, where[n][0]:where[n][1]]
        load_stage(nc, "first", [(k.ident[:], ins["ident"]), (k.columns[:], ins["columns"]), (k.causal[:], ins["causal"]), (k.pair_ones[:], ins["pair_ones"]),
                                 (xT[:], ins["xT"].rearrange("(c p) t -> p c t", p=P))])
        ada_stage(nc, k, cols("c"), ins["w_ada"], cols("b_ada"), mod)
        gain_stage(nc, "g1", gain, cols("norm_mix"), mod[:, DC:2 * DC])
        norm_stage(nc, "n1", k, xT, DC, D, gain, hT, shift=mod[:, 0:DC])
        with ExitStack() as mixer:
            m = Room(nc, mixer, "mix")
            z = m.sb("z", [P, Z_N, S])
            project_stage(nc, "p1", ins["w_in"], hT, DC, Z_N, z)
            oT = m.sb("oT", [P, 4, S])
            with ExitStack() as mla:
                a = Room(nc, mla, "mla")
                qT, kT, v_tp = a.sb("qT", [QH, MH, S]), a.sb("kT", [QH, MH, S]), a.sb("v", [P, TT, MH, VH])
                norm_stage(nc, "nq", k, z[:, Z_QA:Z_KV], 2, 256, cols("q_a_norm"), z[:, Z_QA:Z_KV])
                norm_stage(nc, "nk", k, z[:, Z_KV:Z_R], 1, 128, cols("kv_a_norm"), z[:, Z_KV:Z_R])
                mla_heads_stage(nc, k, z, ins, z[:, Z_QA:Z_KV], z[:, Z_KV:Z_R], ins["w_uq"], ins["w_ukv"], qT, kT, v_tp, hT)
                items = [(qT[:, h, t * P:(t + 1) * P], kT[:, h, 0:(t + 1) * P], k.causal[:],
                          [v_tp[:, j, h, :] for j in range(t + 1)], h, t, None) for h in range(MH) for t in range(TT)]
                attention_stage(nc, "mlaa", k, items, MH, VH, oT)
            with ExitStack() as rwkv:
                a = Room(nc, rwkv, "rwkv")
                KR, sgate = a.sb("KR", [P, RP, TT, 2, P]), a.sb("sgate", [P, S])
                mid_e, end_e, bonus = a.sb("mid_e", [P, RP * TT]), a.sb("end_e", [P, RP * TT]), a.sb("bonus", [P, TT, RH])
                tile4 = lambda ap: ap.rearrange("p m (t n) -> p m t n", n=P)
                vT = a.sb("vT", [P, RP, TT, P])
                with ExitStack() as early:
                    rk = Room(nc, early, "early").sb("rk", [P, RP, S])
                    rwkv_prepare_stage(nc, k, z, ins, cols, hT, KR, rk, sgate, mid_e, end_e)
                    kkT, bT, kdT = tile4(hT[:, 0:4, :]), tile4(hT[:, 4:8, :]), tile4(z[:, Z_V:Z_WA, :])
                    rwkv_turn_stage(nc, k, z, ins, KR, rk, kkT, bT, kdT, vT, bonus)
                rT = a.sb("rT", [P, 4, S])
                rwkv_solve_stage(nc, k, ins, KR, z[:, Z_R:Z_K, :], z[:, Z_K:Z_V, :], kkT, bT, kdT, vT, mid_e, end_e, y_of(rT))
                yT = a.sb("yT", [P, 4, S])
                rwkv_finish_stage(nc, k, ins, y_of(rT), vT[:], bonus, sgate, yT, None)
                squash_stage(nc, "sg1", z, Z_GATE, 2 * DC)
                merge_stage(nc, "mg1", z, Z_GATE, [(ins["w_o_mla"], oT), (ins["w_o_rwkv"], yT)], hT)
            project_stage(nc, "po1", ins["w_out"], hT, DC, DC, xT, add=(mod[:, 2 * DC:3 * DC], xT))
        gates_dram = nc.dram_tensor("gates_scratch", [S // SUB, P, NK, SUB], F32, kind="Internal").ap()
        gain_stage(nc, "g2", gain, cols("norm_ffn"), mod[:, 4 * DC:5 * DC])
        norm_stage(nc, "n2", k, xT, DC, D, gain, hT, shift=mod[:, 3 * DC:4 * DC])
        peer(nc, "e1", k, ins, xT, hT, ins["w_query"], ins["keys1"], lambda c: c % 2, ins["down1"], ins["up1"],
             gates_dram, ACT.Gelu_apprx_tanh, gain=mod[:, 5 * DC:6 * DC])
        norm_stage(nc, "n3", k, xT, DC, D, cols("norm1_g_2"), hT)
        second_mixer(nc, k, ins, cols, xT, hT)
        norm_stage(nc, "n4", k, xT, DC, D, cols("norm2_g_2"), hT)
        peer(nc, "e2", k, ins, xT, hT, ins["w_peer_q"], ins["keys2"], lambda c: c, ins["down2"], ins["up2"],
             gates_dram, ACT.Gelu)
        with ExitStack() as stack:
            stored = Room(nc, stack, "end").sem("stored")
            with nc.Block() as block:
                @block.sync
                def _(sp):
                    sp.dma_start(out.rearrange("(c p) t -> p c t", p=P), xT[:]).then_inc(stored, 16)
                    sp.wait_ge(stored, 16)


def gain_stage(nc, name, gain, g, scale):
    with ExitStack() as stack:
        r = Room(nc, stack, name)
        chain = r.sem("chain")
        with nc.Block() as block:
            @block.vector
            def _(dve):
                link = Chain(dve, chain)
                link(dve.tensor_scalar(gain[:], scale, 1.0, None, ALU.add))
                dve.tensor_tensor(gain[:], gain[:], g, ALU.mult)

def _cols(v):
    return np.ascontiguousarray(np.asarray(v).reshape(-1, P).T)


def _chunks(w):
    kk, m = w.shape
    return w.reshape(kk // P, P, m // P, P).transpose(2, 1, 0, 3)


def _layout(inp):
    f = {n: np.asarray(v) for n, v in inp.items()}
    first = lambda n: f[n][0]
    zeros = lambda *s: np.zeros(s, np.float32)
    a = {}
    a["xT"] = f["x"][0].T
    a["positions"] = _cols(f["positions"][0])
    a["w_ada"] = first("w_ada").reshape(DC, P, 12, 512).transpose(2, 1, 0, 3)
    w = first("w_in")
    a["w_in"] = np.concatenate([w[:, 0:384], w[:, 416:], w[:, 384:416], zeros(D, 96)], axis=1)
    a["w_uq"], a["w_ukv"] = first("w_uq"), first("w_ukv")
    a["q_norm"], a["k_norm"] = f["q_norm"], f["k_norm"]
    a["inv_freq"] = (np.float32(10000.0) ** (-np.arange(16, dtype=np.float32) / np.float32(16))).astype(np.float32)[None]
    a["ident"] = np.eye(P, dtype=np.float32)
    q = np.arange(P)
    a["causal"] = np.where(q[None, :] <= q[:, None], 0.0, NEG).astype(np.float32)
    b16 = q[:, None] // 16 == q[None, :] // 16
    lower, upper = q[None, :] < q[:, None], q[None, :] > q[:, None]
    up_incl = q[None, :] >= q[:, None]
    a["masks"] = np.stack([np.where(upper & b16, -1.0, 0.0), np.where(lower & b16, -1.0, 0.0), np.where(lower & ~b16, -1.0, 0.0),
                           np.where(upper, 1.0, 0.0), np.where(up_incl, 1.0, 0.0)]).astype(np.float32)
    a["pair_ones"] = (q[:, None] // RN == q[None, :] // RN).astype(np.float32)
    a["pair_sel"] = (q[:, None] // RN == np.arange(2)[None, :]).astype(np.float32)
    a["id64"] = (q[:, None] % RN == np.arange(RN)[None, :]).astype(np.float32)
    for n in ("w_decay_up", "w_aaa_up", "w_gate_up", "w_o_mla", "w_o_rwkv", "w_out"):
        a[n] = first(n)
    w = first("w_in_2")
    sq = w[:, 1544:2056].reshape(D, 2, 4, SD).transpose(0, 2, 1, 3).reshape(D, 512)
    a["w_in_2"] = np.concatenate([w[:, 0:1536], sq, w[:, 2056:2312], w[:, 2312:2824], w[:, 2824:], w[:, 1536:1544], zeros(D, 120)], axis=1)
    dist = q[:, None] + P - np.arange(2 * P)[None, :]
    slopes = 2.0 ** -(np.arange(SH) + 1.0)
    a["alibi"] = np.where(((dist >= 0) & (dist < P))[:, None, :], -slopes[None, :, None] * dist[:, None, :], NEG).astype(np.float32)
    a["swa_sinks"] = f["swa_sinks_2"]
    a["memT"] = f["mem_2"][0].T
    for n in ("w_mem_kv", "w_fox_o", "w_swa_o", "w_mem_o"):
        a[n] = first(n + "_2")
    a["w_out_2"], a["w_peer_q"] = first("w_out_2"), first("w_peer_q_2")
    a["keys2"] = np.stack([first("peer_keys1_2"), first("peer_keys2_2")], axis=1).reshape(2 * PH, NK, P).transpose(2, 0, 1)
    a["down2"] = first("peer_u_2").reshape(NK, NK, DC, P).transpose(0, 3, 2, 1)
    a["up2"] = first("peer_v_2").reshape(NK, NK, D)
    a["w_query"] = first("w_query")
    a["keys1"] = np.stack([first("sub_keys1").T, first("sub_keys2").T], axis=1)
    a["down1"] = first("expert_down").reshape(NK, NK, DC, P).transpose(0, 3, 2, 1)
    a["up1"] = first("expert_up").reshape(NK, NK, D)
    a["iota16"], a["iota128"] = np.arange(K16, dtype=np.float32)[None], np.arange(NK, dtype=np.float32)[None]
    a["ln_x_w"], a["ln_x_b"] = f["ln_x_w"], f["ln_x_b"]
    for n in ("w_in", "w_in_2", "w_out", "w_out_2", "w_query", "w_peer_q", "w_mem_kv"):
        a[n] = _chunks(a[n])
    vecs = [("c", f["c"][0]), ("b_ada", first("b_ada")), ("norm_mix", first("norm_mix")), ("q_a_norm", first("q_a_norm")), ("kv_a_norm", first("kv_a_norm"))]
    vecs += [(n, first(n)) for n in ("mu_shift", "decay_base", "aaa_base", "k_k", "k_a")]
    vecs += [("r_k", first("r_k").reshape(-1)), ("norm_ffn", first("norm_ffn"))]
    vecs += [("norm1_g_2", first("norm1_g_2")), ("mem_norm_g_2", first("mem_norm_g_2")), ("norm2_g_2", first("norm2_g_2")),
             ("b_gate_2", first("b_gate_2"))]
    twice = lambda v: np.concatenate([v, v])
    vecs += [(n, twice(first(n + "_2"))) for n in ("fox_q_g", "fox_k_g", "swa_q_g", "swa_k_g")]
    vecs += [(n, first(n + "_2")) for n in ("mem_q_g", "mem_k_g")]
    vecs += [("b_forget", np.concatenate([first("b_forget_2"), zeros(P - FH)]))]
    at, parts, where = 0, [], {}
    for n, v in vecs:
        m = _cols(v)
        where[n] = (at, at + m.shape[1])
        at += m.shape[1]
        parts.append(m)
    a["columns"] = np.concatenate(parts, axis=1)
    return {n: np.ascontiguousarray(v) for n, v in a.items()}, where


def kernel(**inputs):
    import concourse.bacc as _bacc
    from concourse.bass_utils import run_bass_kernel_spmd as _run

    nc = _bacc.Bacc("TRN2", target_bir_lowering=False, num_devices=1)
    arrays, where = _layout(inputs)
    ins = {n: nc.dram_tensor(f"in_{n}", list(v.shape), mybir.dt.from_np(v.dtype), kind="ExternalInput").ap()
           for n, v in arrays.items()}
    out = nc.dram_tensor("out_xT", [D, S], F32, kind="ExternalOutput").ap()
    build(nc, ins, where, out)
    res = _run(nc, [{f"in_{n}": v for n, v in arrays.items()}], core_ids=[0])
    return np.ascontiguousarray(res.results[0]["out_xT"].T)[None]
```

```python
import numpy as np
import concourse.bass as bass
from concourse import mybir
from contextlib import ExitStack

F32 = mybir.dt.float32
F32R = mybir.dt.float32r
U32 = mybir.dt.uint32
I32 = mybir.dt.int32
ALU = mybir.AluOpType
ACT = mybir.ActivationFunctionType
AX = mybir.AxisListType.X
ds = bass.ds

P = 128
S = 512
D = 1024
TT = S // P
DC = D // P
EPS = 1e-6
EARLY_ADA = 4
NEG = -1e30
MH, NOPE, ROPE, VH = 8, 64, 32, 64
QH = NOPE + ROPE
RH, RN = 8, 64
RP = RH // 2
GN_EPS = 64e-5
Z_QA, Z_KV, Z_R, Z_K, Z_V, Z_WA, Z_GD, Z_GATE, Z_ROPE, Z_N = 0, 2, 3, 7, 11, 15, 16, 17, 33, 34
FH, FD = 8, 64
SH, SG, SD = 8, 2, 64
GH, GD = 4, 128
NMEM = 256
Y_FQ, Y_FK, Y_FV, Y_SQ, Y_SKV, Y_MQ, Y_GATE, Y_FF, Y_N = 0, 4, 8, 12, 16, 18, 22, 46, 47
HN = 17
PH, NK, K16 = 8, 128, 16
NJ = PH * K16
SUB = 64


class Chain:

    def __init__(self, eng, sem):
        self.eng, self.sem, self.n = eng, sem, 0

    def __call__(self, ins):
        self.n += 1
        ins.then_inc(self.sem, 1)
        self.eng.wait_ge(self.sem, self.n)

    def lag(self, ins):
        self.n += 1
        ins.then_inc(self.sem, 1)
        if self.n > 1:
            self.eng.wait_ge(self.sem, self.n - 1)

    def settle(self):
        self.eng.wait_ge(self.sem, self.n)

    def announce(self, ins, sem, count):
        ins.then_inc(sem, 1)
        self.eng.wait_ge(sem, count)


class Room:

    def __init__(self, nc, stack, name):
        self.nc, self.stack, self.name, self.sems = nc, stack, name, []
        stack.callback(lambda: [nc.gpsimd.sem_clear(s) for s in self.sems])

    def sb(self, name, shape, dt=F32):
        return self.stack.enter_context(self.nc.sbuf_tensor(f"{self.name}_{name}", shape, dt))

    def ps(self, name, shape=(P, 512), dt=F32):
        return self.stack.enter_context(self.nc.psum_tensor(f"{self.name}_{name}", list(shape), dt))

    def sem(self, *names):
        got = [self.stack.enter_context(self.nc.semaphore(f"{self.name}_{n}")) for n in names]
        self.sems += got
        return got[0] if len(got) == 1 else got


def bcast(ap, n, axis):
    shape = list(ap.shape)
    a = ap.unsqueeze(axis)
    shape.insert(axis, n)
    return a.to_broadcast(shape)


def row(t, m):
    return t[:, m, :] if isinstance(m, int) else t[:, ds(m, 1), :].rearrange("p a t -> p (a t)")


def col(t, m):
    return t[:, m:m + 1] if isinstance(m, int) else t[:, ds(m, 1)]


def load_stage(nc, name, pairs):
    with ExitStack() as stack:
        r = Room(nc, stack, name)
        loaded = r.sem("loaded")
        with nc.Block() as block:
            @block.sync
            def _(sp):
                for dst, src in pairs:
                    sp.dma_start(dst, src).then_inc(loaded, 16)
                sp.wait_ge(loaded, 16 * len(pairs))


def ada_stage(nc, k, ccol, w_ada, bcol, mod, groups, sc):
    with ExitStack() as stack:
        r = Room(nc, stack, "ada")
        sig = r.sb("sig", [P, DC])
        w = [r.sb(f"w{u}", [P, DC, 512]) for u in range(3)]
        acc = [[r.sb(f"acc{u}{v}", [P, 512]) for v in range(2)] for u in range(2)]
        ps = r.ps("ps")
        sig_ready, silu_ready, summed, product_ready, chain = r.sem("sig_ready", "silu_ready", "summed", "product_ready", "chain")
        w_ready = [r.sem(f"w_ready{u}") for u in range(3)]
        with nc.Block() as block:
            @block.sync
            def _(sp):
                for n in range(groups):
                    if n >= 3:
                        sp.wait_ge(summed, n - 2)
                    sp.dma_start(w[n % 3][:], w_ada[n]).then_inc(w_ready[n % 3], 16)

            @block.scalar
            def _(act):
                act.activation(sig[:], ccol, ACT.Sigmoid).then_inc(sig_ready, 1)

            @block.tensor
            def _(pe):
                for n in range(groups):
                    pe.wait_ge(summed, n + 1)
                    for j in range(4):
                        last = pe.matmul(ps[:, 4 * n + j:4 * n + j + 1], acc[n % 2][1][:, j * P:(j + 1) * P], k.ones[:, 0:1],
                                         start=True, stop=True)
                    last.then_inc(product_ready, 1)

            @block.vector
            def _(dve):
                link = Chain(dve, chain)
                dve.memset(k.ones[:], 1.0)
                dve.wait_ge(sig_ready, 1)
                link(dve.tensor_tensor(sc[:], ccol, sig[:], ALU.mult))
                for n in range(groups):
                    dve.wait_ge(w_ready[n % 3], 16 * (n // 3) + 16)
                    if n >= 2:
                        dve.wait_ge(product_ready, n - 1)
                    link(dve.tensor_scalar(acc[n % 2][0][:], w[n % 3][:, 0, :], sc[:, 0:1], None, ALU.mult))
                    for c in range(1, DC):
                        ins = dve.scalar_tensor_tensor(acc[n % 2][c % 2][:], w[n % 3][:, c, :], sc[:, c:c + 1],
                                                       acc[n % 2][1 - c % 2][:], ALU.mult, ALU.add)
                        if c < DC - 1:
                            link(ins)
                    ins.then_inc(summed, 1)
                dve.wait_ge(product_ready, groups)
                dve.tensor_tensor(mod[:, 0:4 * groups], ps[:, 0:4 * groups], bcol[:, 0:4 * groups], ALU.add)


class AdaBeside:

    def __init__(self, r, k, w_ada, bcol, mod, first, sc):
        self.k, self.w_ada, self.bcol, self.mod, self.first, self.sc = k, w_ada, bcol, mod, first, sc
        self.groups = w_ada.shape[0] - first
        self.w = [r.sb(f"w_ada{h}", [P, DC // 2, 512]) for h in range(2)]
        self.acc = [r.sb(f"acc{v}", [P, 512]) for v in range(2)]
        self.ps = r.ps("ps_ada")
        self.summed, self.used, self.product_ready = r.sem("ada_summed", "ada_used", "ada_product")
        self.w_ready = [r.sem(f"ada_in{h}") for h in range(2)]

    def load(self, sp, i, h):
        sp.wait_ge(self.used, 2 * i + h + 1)
        src = self.w_ada[self.first:, :, h * DC // 2:(h + 1) * DC // 2]
        sp.dma_start(self.w[h][:], src[ds(i, 1)].rearrange("a p c n -> (a p) c n")).then_inc(self.w_ready[h], 16)

    def sums(self, dve, i, q):
        w, acc = self.w[q // 2], self.acc
        if q % 2 == 0:
            dve.wait_ge(self.w_ready[q // 2], 16 * i + 16)
        if q == 0:
            dve.wait_ge(self.product_ready, i + 1)
            dve.tensor_scalar(acc[0][:], w[:, 0, :], self.sc[:, 0:1], None, ALU.mult).then_inc(self.summed, 1)
        for c in range(max(2 * q, 1), 2 * q + 2):
            dve.wait_ge(self.summed, DC * i + c)
            ins = dve.scalar_tensor_tensor(acc[c % 2][:], w[:, c % 4, :], self.sc[:, c:c + 1], acc[1 - c % 2][:], ALU.mult, ALU.add)
            ins.then_inc(self.summed, 1)
        if q % 2:
            dve.wait_ge(self.summed, DC * i + 2 * q + 2)
            dve.sem_inc(self.used, 1)

    def product(self, pe, i):
        pe.wait_ge(self.summed, DC * i + DC)
        for j in range(4):
            last = pe.matmul(self.ps[:, ds(4 * i + j, 1)], self.acc[1][:, j * P:(j + 1) * P], self.k.ones[:, 0:1], start=True, stop=True)
        last.then_inc(self.product_ready, 1)

    def finish(self, dve):
        at = slice(4 * self.first, 4 * (self.first + self.groups))
        dve.wait_ge(self.product_ready, self.groups + 1)
        dve.tensor_tensor(self.mod[:, at], self.ps[:, 0:4 * self.groups], self.bcol[:, at], ALU.add)


def norm_stage(nc, name, k, src, chunks, width, gain, dst, shift=None, tokens=S):
    with ExitStack() as stack:
        r = Room(nc, stack, name)
        sq, mean, root, rstd = r.sb("sq", [P, chunks, tokens]), r.sb("mean", [P, tokens]), r.sb("root", [P, tokens]), r.sb("rstd", [P, tokens])
        ss = r.ps("ss")
        sq_ready, ss_ready, mean_ready, root_ready, chain = r.sem("sq_ready", "ss_ready", "mean_ready", "root_ready", "chain")
        with nc.Block() as block:
            @block.scalar
            def _(act):
                for c in range(chunks):
                    act.activation(sq[:, c, :], src[:, c, :], ACT.Square).then_inc(sq_ready, 1)
                act.wait_ge(mean_ready, 1)
                act.activation(root[:], mean[:], ACT.Sqrt).then_inc(root_ready, 1)

            @block.tensor
            def _(pe):
                for c in range(chunks):
                    pe.wait_ge(sq_ready, c + 1)
                    last = pe.matmul(ss[:, 0:tokens], k.ones[:], sq[:, c, :], start=c == 0, stop=c == chunks - 1)
                last.then_inc(ss_ready, 1)

            @block.vector
            def _(dve):
                link = Chain(dve, chain)
                dve.wait_ge(ss_ready, 1)
                dve.tensor_scalar(mean[:], ss[:, 0:tokens], 1.0 / width, EPS, ALU.mult, ALU.add).then_inc(mean_ready, 1)
                dve.wait_ge(root_ready, 1)
                link(dve.reciprocal(rstd[:], root[:]))
                for c in range(chunks):
                    ins = dve.scalar_tensor_tensor(dst[:, c, :], src[:, c, :], gain[:, c:c + 1], rstd[:], ALU.mult, ALU.mult)
                    if shift is not None:
                        link(ins)
                        dve.tensor_scalar(dst[:, c, :], dst[:, c, :], shift[:, c:c + 1], None, ALU.add)


def project_stage(nc, name, k, w_dram, act_in, kc, chunks, dst, tokens=S, add=None, parts=None, ada=None):
    with ExitStack() as stack:
        r = Room(nc, stack, name)
        hhi, hlo = parts or (r.sb("hhi", [P, kc, tokens], F32R), r.sb("hlo", [P, kc, tokens], F32R))
        raw, whi, wlo = [[r.sb(f"{n}{u}", [P, kc, P], dt) for u in range(2)] for n, dt in (("raw", F32), ("whi", F32R), ("wlo", F32R))]
        ps = [r.ps(f"ps{u}") for u in range(4)]
        h_hi, h_lo, w_hi, split, made, used = r.sem("h_hi", "h_lo", "w_hi", "split", "made", "used")
        w_ready = [r.sem(f"w_ready{u}") for u in range(2)]
        turns = (chunks - 1) // 4
        beside = AdaBeside(r, k, *ada) if ada else None
        assert beside is None or beside.groups == turns

        def loop(eng, body):
            if turns:
                with eng.Fori(0, turns) as i:
                    for q in range(4):
                        body(4 * i + q, q, i)
            for n in range(4 * turns, chunks):
                body(n, n % 4, None)

        with nc.Block() as block:
            @block.sync
            def _(sp):
                def body(n, q, i):
                    sp.wait_ge(split, n + 1)
                    src = w_dram[n] if isinstance(n, int) else w_dram[ds(n, 1)].rearrange("a p c e -> (a p) c e")
                    sp.dma_start(raw[q % 2][:], src).then_inc(w_ready[q % 2], 16)
                    if beside and q % 2 == 0 and i is not None:
                        beside.load(sp, i, q // 2)

                loop(sp, body)

            @block.scalar
            def _(act):
                def body(n, q, i):
                    act.wait_ge(w_ready[q % 2], 8 * n + 16 - 8 * (q % 2))
                    act.wait_ge(made, n + 1)
                    act.activation(whi[q % 2][:], raw[q % 2][:], ACT.Copy).then_inc(w_hi, 1)

                for c in range(kc):
                    act.activation(hhi[:, c, :], act_in[:, c, :], ACT.Copy).then_inc(h_hi, 1)
                loop(act, body)

            @block.tensor
            def _(pe):
                def body(n, q, i):
                    pe.wait_ge(split, n + 3)
                    pe.wait_ge(used, n + 1)
                    out = ps[q][:, 0:tokens]
                    for c in range(kc):
                        hi, lo = whi[q % 2][:, c, :], wlo[q % 2][:, c, :]
                        pe.matmul(out, hi, hhi[:, c, :], start=c == 0, stop=False)
                        pe.matmul(out, hi, hlo[:, c, :], start=False, stop=False)
                        last = pe.matmul(out, lo, hhi[:, c, :], start=False, stop=c == kc - 1)
                    last.then_inc(made, 1)
                    if beside and q == 3 and i is not None:
                        beside.product(pe, i)

                pe.sem_inc(made, 2)
                if beside:
                    pe.sem_inc(beside.product_ready, 1)
                pe.wait_ge(h_lo, kc)
                loop(pe, body)

            @block.vector
            def _(dve):
                def split_w(n, q):
                    dve.wait_ge(w_hi, n + 1)
                    dve.tensor_tensor(wlo[q % 2][:], raw[q % 2][:], whi[q % 2][:].bitcast(F32), ALU.subtract).then_inc(split, 1)

                def body(n, q, i):
                    if not (isinstance(n, int) and n == chunks - 1):
                        split_w(n + 1, q + 1)
                    if beside and i is not None:
                        beside.sums(dve, i, q)
                    dve.wait_ge(made, n + 3)
                    got = ps[q][:, 0:tokens]
                    if add is None:
                        ins = dve.tensor_copy(row(dst, n), got)
                    else:
                        gain, base = add
                        ins = dve.scalar_tensor_tensor(row(dst, n), got, col(gain, n), row(base, n), ALU.mult, ALU.add)
                    ins.then_inc(used, 1)

                dve.sem_inc(split, 2)
                dve.sem_inc(used, 4)
                if beside:
                    dve.sem_inc(beside.used, 2)
                for c in range(kc):
                    dve.wait_ge(h_hi, c + 1)
                    dve.tensor_tensor(hlo[:, c, :], act_in[:, c, :], hhi[:, c, :].bitcast(F32), ALU.subtract).then_inc(h_lo, 1)
                split_w(0, 0)
                loop(dve, body)
                if beside:
                    beside.finish(dve)

def mla_heads_stage(nc, k, z, g, cq, ckv, w_uq_in, w_ukv_in, qT, kT, v_tp, spare):
    with ExitStack() as stack:
        r = Room(nc, stack, "mlah")
        w_uq, w_ukv = r.sb("w_uq", [P, 2, MH * QH]), r.sb("w_ukv", [P, MH * (NOPE + VH)])
        gq, gk = r.sb("gq", [P, QH]), r.sb("gk", [P, QH])
        pos_i, pos = r.sb("pos_i", [P, TT], I32), r.sb("pos", [P, TT])
        freq = r.sb("freq", [P, 16])
        ang, turns, trig = r.sb("ang", [P, TT, 16]), r.sb("turns", [P, TT, 16]), r.sb("trig", [P, 2, TT, 16])
        q, kk = r.sb("q", [P, TT, MH, QH]), r.sb("kk", [P, TT, MH, QH])
        kr = r.sb("kr", [P, TT, ROPE])
        sq = r.sb("sq", [P, TT * MH, QH])
        ss, root = r.sb("ss", [P, 4, TT * MH]), r.sb("root", [P, 4, TT * MH])
        rot = spare[:, 0:4, :].rearrange("p a (g n) -> p a g n", n=16)
        ps = [r.ps(f"ps{u}") for u in range(4)]
        pt = [r.ps(f"pt{u}") for u in range(2)]
        loaded, made, taken, sums, roots, heads, turned, turned_used, reduced, sines, chain = r.sem(
            "loaded", "made", "taken", "sums", "roots", "heads", "turned", "turned_used", "reduced", "sines", "chain")
        TWO_PI = 2 * np.pi
        C1 = float(np.float32(6.28125))
        C2 = float(np.float32(np.float32((TWO_PI - C1) * 4096) // 1 / 4096))
        C3 = float(np.float32(TWO_PI - C1 - C2))
        MAGIC = 12582912.0
        with nc.Block() as block:
            @block.sync
            def _(sp):
                sp.dma_start(w_uq[:], w_uq_in.rearrange("(c p) n -> p c n", p=P)).then_inc(loaded, 16)
                sp.dma_start(w_ukv[:], w_ukv_in).then_inc(loaded, 16)
                sp.dma_start(gq[:], g["q_norm"].to_broadcast([P, QH])).then_inc(loaded, 16)
                sp.dma_start(gk[:], g["k_norm"].to_broadcast([P, QH])).then_inc(loaded, 16)
                sp.dma_start(pos_i[:], g["positions"]).then_inc(loaded, 16)
                sp.dma_start(freq[:], g["inv_freq"].to_broadcast([P, 16])).then_inc(loaded, 16)

            @block.tensor
            def _(pe):
                pe.wait_ge(loaded, 96)
                for t in range(TT):
                    tok = slice(t * P, t * P + P)
                    if t:
                        pe.wait_ge(taken, t)
                    for u, n0, n1 in ((0, 0, 384), (1, 384, 768)):
                        for c in range(2):
                            pe.matmul(ps[u][:, 0:384], cq[:, c, tok], w_uq[:, c, n0:n1], start=c == 0, stop=c == 1)
                    for u in range(2):
                        pe.matmul(ps[2 + u][:], ckv[:, 0, tok], w_ukv[:, u * 512:(u + 1) * 512], start=True, stop=True)
                    pe.transpose(pt[0][:, 0:P], z[:, Z_ROPE, tok], k.ident[:]).then_inc(made, 1)
                pe.wait_ge(taken, TT)
                for n in range(2 * MH):
                    src, h = (q, n) if n < MH else (kk, n - MH)
                    pe.wait_ge(heads, TT if n < MH else TT + 1)
                    if n >= 2:
                        pe.wait_ge(turned_used, n - 1)
                    for t in range(TT):
                        last = pe.transpose(pt[n % 2][0:QH, t * P:(t + 1) * P], src[:, t, h, :], k.ident[:])
                    last.then_inc(turned, 1)

            @block.scalar
            def _(act):
                act.wait_ge(sines, 2)
                act.activation(trig[:], trig[:], ACT.Sin).then_inc(sines, 1)
                act.wait_ge(sums, 4)
                act.activation(root[:], ss[:], ACT.Sqrt).then_inc(roots, 1)
                for n in range(2 * MH):
                    dst, h = (qT, n) if n < MH else (kT, n - MH)
                    act.wait_ge(turned, n + 1)
                    act.activation(dst[:, h, :], pt[n % 2][0:QH, :], ACT.Copy).then_inc(turned_used, 1)

            @block.vector
            def _(dve):
                link = Chain(dve, chain)
                dve.wait_ge(loaded, 96)
                link(dve.tensor_scalar(gq[:], gq[:], QH ** -0.5, None, ALU.mult))
                link(dve.tensor_copy(pos[:], pos_i[:]))
                link(dve.tensor_tensor(ang[:], bcast(pos[:], 16, 2), bcast(freq[:], TT, 1), ALU.mult))
                for j in range(2):
                    link(dve.tensor_scalar(turns[:], ang[:], 1 / TWO_PI, 0.25 * j, ALU.mult, ALU.add))
                    link(dve.tensor_scalar(turns[:], turns[:], MAGIC, None, ALU.add))
                    link(dve.tensor_scalar(turns[:], turns[:], MAGIC, None, ALU.subtract))
                    link(dve.scalar_tensor_tensor(trig[:, j], turns[:], -C1, ang[:], ALU.mult, ALU.add))
                    link(dve.scalar_tensor_tensor(trig[:, j], turns[:], -C2, trig[:, j], ALU.mult, ALU.add))
                    link(dve.scalar_tensor_tensor(trig[:, j], turns[:], -C3, trig[:, j], ALU.mult, ALU.add))
                    if j:
                        link(dve.tensor_scalar(trig[:, j], trig[:, j], np.pi / 2, None, ALU.add))
                    link.announce(dve.tensor_scalar(trig[:, j], trig[:, j], 3.1415925, -3.1415925, ALU.min, ALU.max), sines, j + 1)
                for t in range(TT):
                    dve.wait_ge(made, t + 1)
                    dve.tensor_copy(q[:, t, 0:4, :], ps[0][:, 0:384].rearrange("p (h d) -> p h d", h=4))
                    dve.tensor_copy(q[:, t, 4:8, :], ps[1][:, 0:384].rearrange("p (h d) -> p h d", h=4))
                    for u in range(2):
                        both = ps[2 + u][:].rearrange("p (h d) -> p h d", h=4)
                        dve.tensor_copy(kk[:, t, 4 * u:4 * u + 4, 0:NOPE], both[:, :, 0:NOPE])
                        dve.tensor_copy(v_tp[:, t, 4 * u:4 * u + 4, :], both[:, :, NOPE:NOPE + VH])
                    link.announce(dve.tensor_copy(kr[:, t, :], pt[0][:, 0:ROPE]), taken, t + 1)
                qg, kg = q[:].rearrange("p t h d -> p (t h) d"), kk[:].rearrange("p t h d -> p (t h) d")
                link(dve.tensor_tensor(sq[:], qg, qg, ALU.mult))
                link(dve.reduce_sum(ss[:, 0], sq[:, :, 0:NOPE], AX))
                link(dve.reduce_sum(ss[:, 1], sq[:, :, NOPE:QH], AX))
                link(dve.tensor_tensor(sq[:, :, 0:NOPE], kg[:, :, 0:NOPE], kg[:, :, 0:NOPE], ALU.mult))
                link(dve.reduce_sum(ss[:, 2], sq[:, :, 0:NOPE], AX))
                link(dve.tensor_tensor(sq[:, 0:TT, 0:ROPE], kr[:], kr[:], ALU.mult))
                link(dve.memset(ss[:, 3], 1.0))
                link(dve.reduce_sum(ss[:, 3, 0:TT], sq[:, 0:TT, 0:ROPE], AX))
                for j, n in enumerate((NOPE, ROPE, NOPE, ROPE)):
                    link.announce(dve.tensor_scalar(ss[:, j], ss[:, j], 1.0 / n, EPS, ALU.mult, ALU.add), sums, j + 1)
                dve.wait_ge(roots, 1)
                link(dve.reciprocal(ss[:], root[:]))
                TH = TT * MH
                link(dve.tensor_tensor(qg[:, :, 0:NOPE], qg[:, :, 0:NOPE], bcast(ss[:, 0], NOPE, 2), ALU.mult))
                link(dve.tensor_tensor(qg[:, :, NOPE:QH], qg[:, :, NOPE:QH], bcast(ss[:, 1], ROPE, 2), ALU.mult))
                link(dve.tensor_tensor(kg[:, :, 0:NOPE], kg[:, :, 0:NOPE], bcast(ss[:, 2], NOPE, 2), ALU.mult))
                link(dve.tensor_tensor(kr[:], kr[:], bcast(ss[:, 3, 0:TT], ROPE, 2), ALU.mult))
                link(dve.tensor_tensor(qg, qg, bcast(gq[:], TH, 1), ALU.mult))
                link(dve.tensor_tensor(kg[:, :, 0:NOPE], kg[:, :, 0:NOPE], bcast(gk[:, 0:NOPE], TH, 1), ALU.mult))
                link(dve.tensor_tensor(kr[:], kr[:], bcast(gk[:, NOPE:QH], TT, 1), ALU.mult))
                dve.wait_ge(sines, 3)
                r4 = rot.rearrange("p a (t h) n -> p a t h n", t=TT)
                for t in range(TT):
                    x1, x2 = q[:, t, :, NOPE:NOPE + 16], q[:, t, :, NOPE + 16:QH]
                    sin, cos = bcast(trig[:, 0, t], MH, 1), bcast(trig[:, 1, t], MH, 1)
                    dve.tensor_tensor(r4[:, 0, t], x1, cos, ALU.mult)
                    dve.tensor_tensor(r4[:, 1, t], x2, sin, ALU.mult)
                    dve.tensor_tensor(r4[:, 2, t], x1, sin, ALU.mult)
                    link(dve.tensor_tensor(r4[:, 3, t], x2, cos, ALU.mult))
                    dve.tensor_tensor(x1, r4[:, 0, t], r4[:, 1, t], ALU.subtract)
                    link.announce(dve.tensor_tensor(x2, r4[:, 2, t], r4[:, 3, t], ALU.add), heads, t + 1)
                x1, x2 = kr[:, :, 0:16], kr[:, :, 16:32]
                sin, cos = trig[:, 0], trig[:, 1]
                dve.tensor_tensor(rot[:, 0, 0:TT], x1, cos, ALU.mult)
                dve.tensor_tensor(rot[:, 1, 0:TT], x2, sin, ALU.mult)
                dve.tensor_tensor(rot[:, 2, 0:TT], x1, sin, ALU.mult)
                link(dve.tensor_tensor(rot[:, 3, 0:TT], x2, cos, ALU.mult))
                dve.tensor_tensor(x1, rot[:, 0, 0:TT], rot[:, 1, 0:TT], ALU.subtract)
                link(dve.tensor_tensor(x2, rot[:, 2, 0:TT], rot[:, 3, 0:TT], ALU.add))
                dve.tensor_copy(kk[:, :, :, NOPE:QH], bcast(kr[:], MH, 2)).then_inc(heads, 1)


def attention_stage(nc, name, k, items, heads, vdim, oT, sinks=None):
    per = P // vdim
    N = len(items)
    with ExitStack() as stack:
        r = Room(nc, stack, name)
        p = [r.sb(f"p{u}", [P, 512]) for u in range(3)]
        pT = [r.sb(f"pT{u}", [P, 512]) for u in range(2)]
        nmax, total, inv = r.sb("nmax", [P, N]), r.sb("total", [P, N]), r.sb("inv", [P, N])
        esink = r.sb("esink", [P, N])
        ps = [r.ps(f"ps{u}") for u in range(3)]
        pt = [r.ps(f"pt{u}") for u in range(2)]
        po = [r.ps(f"po{u}") for u in range(2)]
        scored, biased, maxed, exped, sunk, weighed, turned, copied, summed, taken, chain = r.sem(
            "scored", "biased", "maxed", "exped", "sunk", "weighed", "turned", "copied", "summed", "taken", "chain")
        width = [it[1].shape[-1] for it in items]
        with nc.Block() as block:
            @block.tensor
            def _(pe):
                def score(n):
                    q_ap, k_ap, more = items[n][0], items[n][1], items[n][6]
                    if n >= 3:
                        pe.wait_ge(exped, n - 2)
                    out = ps[n % 3][:, 0:width[n]]
                    last = pe.matmul(out, q_ap, k_ap, start=True, stop=more is None)
                    if more is not None:
                        last = pe.matmul(out, more[0], more[1], start=False, stop=True)
                    last.then_inc(scored, 1)

                def turn(n):
                    pe.wait_ge(weighed, n + 1)
                    if n >= 2:
                        pe.wait_ge(copied, n - 1)
                    for j in range(width[n] // P):
                        last = pe.transpose(pt[n % 2][:, j * P:(j + 1) * P], p[n % 3][:, j * P:(j + 1) * P], k.ident[:])
                    last.then_inc(turned, 1)

                def weigh_values(n):
                    vs, at = items[n][3], (items[n][4] % per) * vdim
                    pe.wait_ge(copied, n + 1)
                    if n >= 2:
                        pe.wait_ge(taken, n - 1)
                    for j, v in enumerate(vs):
                        last = pe.matmul(po[n % 2][at:at + vdim, 0:P], v, pT[n % 2][:, j * P:(j + 1) * P],
                                         start=j == 0, stop=j == len(vs) - 1)
                    last.then_inc(summed, 1)

                for step in range(N + 3):
                    if step < N:
                        score(step)
                    if 2 <= step < N + 2:
                        turn(step - 2)
                    if 3 <= step:
                        weigh_values(step - 3)

            @block.scalar
            def _(act):
                for step in range(N + 2):
                    if step < N:
                        n = step
                        act.wait_ge(maxed, n + 1)
                        if n >= 3:
                            act.wait_ge(turned, n - 2)
                        act.activation(p[n % 3][:, 0:width[n]], ps[n % 3][:, 0:width[n]], ACT.Exp, bias=nmax[:, n:n + 1],
                                       accum_out=total[:, n:n + 1]).then_inc(exped, 1)
                        if sinks is not None:
                            h = items[n][4]
                            act.activation(esink[:, n:n + 1], sinks[:, h:h + 1], ACT.Exp,
                                           bias=nmax[:, n:n + 1]).then_inc(sunk, 1)
                    if step >= 2:
                        n = step - 2
                        act.wait_ge(turned, n + 1)
                        if n >= 2:
                            act.wait_ge(summed, n - 1)
                        act.activation(pT[n % 2][:, 0:width[n]], pt[n % 2][:, 0:width[n]], ACT.Copy).then_inc(copied, 1)

            @block.vector
            def _(dve):
                link = Chain(dve, chain)
                masked = [0]

                def peak(n):
                    bias, w, h = items[n][2], width[n], items[n][4]
                    dve.wait_ge(scored, n + 1)
                    if bias is not None:
                        part = ps[n % 3][:, w - bias.shape[-1]:w]
                        masked[0] += 1
                        link.announce(dve.tensor_tensor(part, part, bias, ALU.add), biased, masked[0])
                    link(dve.reduce_max(nmax[:, n:n + 1], ps[n % 3][:, 0:w], AX))
                    if sinks is not None:
                        link(dve.tensor_tensor(nmax[:, n:n + 1], nmax[:, n:n + 1], sinks[:, h:h + 1], ALU.max))
                    dve.tensor_scalar(nmax[:, n:n + 1], nmax[:, n:n + 1], -1.0, None, ALU.mult).then_inc(maxed, 1)

                def weigh(n):
                    dve.wait_ge(exped, n + 1)
                    if sinks is not None:
                        dve.wait_ge(sunk, n + 1)
                        link(dve.tensor_tensor(total[:, n:n + 1], total[:, n:n + 1], esink[:, n:n + 1], ALU.add))
                    link(dve.reciprocal(inv[:, n:n + 1], total[:, n:n + 1]))
                    dve.tensor_scalar(p[n % 3][:, 0:width[n]], p[n % 3][:, 0:width[n]], inv[:, n:n + 1], None, ALU.mult).then_inc(weighed, 1)

                def take(n):
                    h, t = items[n][4], items[n][5]
                    at = (h % per) * vdim
                    dve.wait_ge(summed, n + 1)
                    dve.tensor_copy(oT[at:at + vdim, h // per, t * P:(t + 1) * P], po[n % 2][at:at + vdim, 0:P]).then_inc(taken, 1)

                for step in range(N + 4):
                    if step < N:
                        peak(step)
                    if 1 <= step <= N:
                        weigh(step - 1)
                    if 4 <= step:
                        take(step - 4)

def rwkv_prepare_stage(nc, k, z, g, cols, hT, KR, rk, sgate, mid_e, end_e):
    with ExitStack() as stack:
        r = Room(nc, stack, "rprep")
        d = r.sb("d", [P, 14, S])
        kk, kh, b = d[:, 0:4, :], d[:, 4:8, :], d[:, 8:12, :]
        ld, a, c, eprev = [r.sb(n, [P, RP, S]) for n in ("ld", "a", "c", "eprev")]
        einc, eneg = hT[:, 0:4, :], hT[:, 4:8, :]
        pair_ones, ones = k.pair_ones, k.ones
        lora, tw = rk[:, 0, :], rk[0:64, 1, :]
        ps = [r.ps(f"ps{u}") for u in range(8)]
        loaded, shifted, squashed, products, gated, used, squares, norms, roots, cums, exps, chain = r.sem(
            "loaded", "shifted", "squashed", "products", "gated", "used", "squares", "norms", "roots", "cums", "exps", "chain")
        with nc.Block() as block:
            @block.sync
            def _(sp):
                sp.dma_start(lora[0:64, :], g["w_decay_up"]).then_inc(loaded, 16)
                sp.dma_start(lora[64:128, :], g["w_aaa_up"]).then_inc(loaded, 16)

            @block.tensor
            def _(pe):
                pe.wait_ge(loaded, 32)
                pe.wait_ge(squashed, 1)
                for m in range(4):
                    pe.matmul(ps[m][:], lora[0:64, m * P:(m + 1) * P], tw, start=True, stop=True).then_inc(products, 1)
                for m in range(4):
                    pe.matmul(ps[4 + m][:], lora[64:128, m * P:(m + 1) * P], z[64:128, Z_WA, :], start=True, stop=True).then_inc(products, 1)
                pe.wait_ge(gated, 8)
                pe.wait_ge(squares, 1)
                for m in range(4):
                    pe.matmul(ps[m][:], pair_ones[:], c[:, m, :], start=True, stop=True).then_inc(norms, 1)

            @block.scalar
            def _(act):
                act.wait_ge(shifted, 1)
                act.activation(tw, z[0:64, Z_WA, :], ACT.Tanh).then_inc(squashed, 1)
                act.activation(sgate[:], z[:, Z_GD, :], ACT.Sigmoid)
                for m in range(8):
                    act.wait_ge(products, m + 1)
                    dst, base = (ld, cols("decay_base")) if m < 4 else (a, cols("aaa_base"))
                    act.activation(dst[:, m % 4, :], ps[m][:], ACT.Sigmoid, bias=base[:, m % 4:m % 4 + 1]).then_inc(gated, 1)
                for m in range(4):
                    act.wait_ge(norms, m + 1)
                    act.activation(eprev[:, m, :], ps[m][:], ACT.Sqrt).then_inc(roots, 1)
                act.wait_ge(cums, 1)
                act.activation(einc, c[:], ACT.Exp).then_inc(exps, 1)
                act.activation(eneg, c[:], ACT.Exp, scale=-1.0).then_inc(exps, 1)
                act.wait_ge(cums, 2)
                act.activation(eprev[:], ld[:], ACT.Exp).then_inc(exps, 1)
                act.activation(mid_e[:], mid_e[:], ACT.Exp).then_inc(exps, 1)

            @block.vector
            def _(dve):
                link = Chain(dve, chain)
                zs = z[:, Z_R:Z_GATE, :]
                link(dve.tensor_tensor(d[:, :, 1:S], zs[:, :, 0:S - 1], zs[:, :, 1:S], ALU.subtract))
                link(dve.tensor_scalar(d[:, :, 0:1], zs[:, :, 0:1], -1.0, None, ALU.mult))
                mu = cols("mu_shift")
                for m in range(14):
                    ins = dve.scalar_tensor_tensor(zs[:, m, :], d[:, m, :], mu[:, m:m + 1], zs[:, m, :], ALU.mult, ALU.add)
                link.announce(ins, shifted, 1)
                rr, kz = z[:, Z_R:Z_K, :], z[:, Z_K:Z_V, :]
                for m in range(4):
                    ins = dve.tensor_scalar(kk[:, m, :], kz[:, m, :], cols("k_k")[:, m:m + 1], None, ALU.mult)
                link(ins)
                dve.tensor_tensor(c[:], kk, kk, ALU.mult).then_inc(squares, 1)
                dve.wait_ge(gated, 8)
                for m in range(4):
                    ins = dve.tensor_scalar(kh[:, m, :], a[:, m, :], 1.0, cols("k_a")[:, m:m + 1], ALU.subtract, ALU.mult)
                link(ins)
                link(dve.scalar_tensor_tensor(kh, kh, 1.0, kz, ALU.add, ALU.mult))
                for m in range(4):
                    ins = dve.scalar_tensor_tensor(rk[:, m, :], rr[:, m, :], cols("r_k")[:, m:m + 1], kh[:, m, :], ALU.mult, ALU.mult)
                link(ins)
                dve.wait_ge(roots, 4)
                link(dve.tensor_scalar(eprev[:], eprev[:], 1e-12, None, ALU.max))
                link(dve.reciprocal(eprev[:], eprev[:]))
                link(dve.tensor_tensor(kk, kk, eprev[:], ALU.mult))
                link(dve.tensor_tensor(b, kk, a[:], ALU.mult))
                link(dve.tensor_scalar(ld[:], ld[:], -float(np.exp(-0.5)), None, ALU.mult))
                for m in range(RP):
                    for t in range(TT):
                        seg = slice(t * P, t * P + P)
                        ins = dve.tensor_tensor_scan(c[:, m, seg], ones[:], ld[:, m, seg], 0.0, ALU.mult, ALU.add)
                link(ins)
                c3, ld3 = c[:].rearrange("p m (t n) -> p (m t) n", n=P), ld[:].rearrange("p m (t n) -> p (m t) n", n=P)
                link(dve.tensor_copy(mid_e[:], c3[:, :, P // 2 - 1]))
                ins = dve.tensor_tensor(c3, c3, bcast(mid_e[:], P, 2), ALU.subtract)
                link.announce(ins, cums, 1)
                link.announce(dve.tensor_tensor(ld[:], c[:], ld[:], ALU.subtract), cums, 2)
                dve.wait_ge(exps, 1)
                cut = lambda ap: ap.rearrange("p m (t n) -> p m t n", n=P)
                link(dve.tensor_tensor(KR[:, :, :, 1, :], cut(rr), cut(einc), ALU.mult))
                dve.tensor_copy(end_e[:], einc.rearrange("p m (t n) -> p (m t) n", n=P)[:, :, P - 1])
                dve.wait_ge(exps, 2)
                dve.tensor_tensor(rr, b, eneg, ALU.mult)
                dve.tensor_tensor(kz, kh, eneg, ALU.mult)
                dve.wait_ge(exps, 3)
                dve.tensor_tensor(KR[:, :, :, 0, :], cut(kk), cut(eprev[:]), ALU.mult)


def rwkv_turn_stage(nc, k, z, g, KR, rk, kkT, bT, kdT, vT, bonus):
    with ExitStack() as stack:
        r = Room(nc, stack, "rturn")
        pt = [r.ps(f"pt{u}") for u in range(4)]
        pb = r.ps("pb")
        sel = r.sb("sel", [P, 2])
        loaded, turned, copied, summed = r.sem("loaded", "turned", "copied", "summed")
        kz, rr, vz = z[:, Z_K:Z_V, :], z[:, Z_R:Z_K, :], z[:, Z_V:Z_WA, :]
        units = [(src, dst, m) for src, dst in ((vz, vT), (rr, bT), (None, kkT), (kz, kdT)) for m in range(RP)]
        with nc.Block() as block:
            @block.sync
            def _(sp):
                sp.dma_start(sel[:], g["pair_sel"]).then_inc(loaded, 16)

            @block.tensor
            def _(pe):
                for n, (src, _, m) in enumerate(units):
                    if n >= 4:
                        pe.wait_ge(copied, n - 3)
                    for t in range(TT):
                        data = KR[:, m, t, 0, :] if src is None else src[:, m, t * P:(t + 1) * P]
                        last = pe.transpose(pt[n % 4][:, t * P:(t + 1) * P], data, k.ident[:])
                    last.then_inc(turned, 1)
                pe.wait_ge(loaded, 16)
                for t in range(TT):
                    for m in range(RP):
                        last = pe.matmul(pb[:, t * 8 + 2 * m:t * 8 + 2 * m + 2], rk[:, m, t * P:(t + 1) * P], sel[:], start=True, stop=True)
                last.then_inc(summed, 1)

            @block.vector
            def _(dve):
                for n, (_, dst, m) in enumerate(units):
                    dve.wait_ge(turned, max(n + 1, RP + 1 if n >= 3 * RP else 0))
                    dve.tensor_copy(dst[:, m, :, :], pt[n % 4][:].rearrange("p (t n) -> p t n", n=P)).then_inc(copied, 1)
                dve.wait_ge(summed, 1)
                dve.tensor_copy(bonus[:], pb[:, 0:TT * RH].rearrange("p (t h) -> p t h", h=RH))


def rwkv_solve_stage(nc, k, g, KR, Bd, Kd, kkT, bT, kdT, vT, mid_e, end_e, y):
    with ExitStack() as stack:
        r = Room(nc, stack, "rsolve")
        masks = r.sb("masks", [P, 5, P])
        MdT, Md, Moff, T, A2T, A3T, A4T, Pa, Pb, Pc, Pd = [
            r.sb(n, [P, RH, P]) for n in ("MdT", "Md", "Moff", "T", "A2T", "A3T", "A4T", "Pa", "Pb", "Pc", "Pd")]
        state = r.sb("state", [P, RP, RN])
        id64 = r.sb("id64", [P, RN])
        escale = r.sb("escale", [P, RP, TT])
        bank = [r.ps(f"bank{u}") for u in range(8)]
        loaded, made, taken, ready = r.sem("loaded", "made", "taken", "ready")
        STEPS = 27
        N, NT, X, X1, WU, RtT, PTI, Z = Md, MdT, Moff, Md, MdT, Pa, Pb, Pd

        def products(pe, c, step, h, out):
            o, m = divmod(h, 4)
            half = slice(o * RN, o * RN + RN)
            seg = slice(c * P, c * P + P)
            KKd, Rd = KR[half, m, c, 0, :], KR[half, m, c, 1, :]
            bd, kd = Bd[half, m, seg], Kd[half, m, seg]
            V, bt, kt = [x[:, m, c, half] for x in (vT, bT, kdT)]
            U0, W = WU[:, h, RN:P], WU[:, h, 0:RN]
            s0 = state[half, m, :]
            table = {
                0: [(bd, KKd)], 1: [(KKd, bd)], 2: [(kd, KKd)], 3: [(bd, Rd)], 4: [(kd, Rd)],
                5: [(MdT[:, h], Md[:, h])], 6: [(Md[:, h], MdT[:, h])], 7: [(Pa[:, h], T[:, h])],
                8: [(Pb[:, h], Pa[:, h])], 9: [(Pa[:, h], Pb[:, h])], 10: [(Pc[:, h], T[:, h])],
                11: [(Pd[:, h], Pc[:, h])], 12: [(Pa[:, h], T[:, h])],
                13: [(T[:, h], Moff[:, h])], 14: [(Moff[:, h], T[:, h])],
                15: [(NT[:, h], N[:, h])], 16: [(N[:, h], NT[:, h])], 17: [(Pa[:, h], Z[:, h])],
                18: [(Pb[:, h], Pa[:, h])], 19: [(Pc[:, h], Z[:, h])],
                20: [(A2T[:, h], V)], 21: [(T[:, h], X[:, h])], 22: [(Z[:, h], X1[:, h])],
                23: [(W, A3T[:, h])], 24: [(W, bt)],
                25: [(A3T[:, h], U0), (A4T[:, h], V), (RtT[half, m, :], s0)],
                26: [(bt, U0), (kt, V), (PTI[half, m, 0:RN], s0)],
            }[step]
            for n, (lhs, rhs) in enumerate(table):
                last = pe.matmul(out, lhs, rhs, start=n == 0, stop=n == len(table) - 1)
            return last

        def out_of(step, h, ps):
            o, m = divmod(h, 4)
            rows = slice(o * RN, o * RN + RN) if step in (23, 24, 26) else slice(0, P)
            return ps[rows, m * P:m * P + (RN if step in (20, 24, 25, 26) else P)]

        with nc.Block() as block:
            @block.sync
            def _(sp):
                sp.dma_start(masks[:], g["masks"].rearrange("m p n -> p m n")).then_inc(loaded, 16)
                sp.dma_start(id64[:], g["id64"]).then_inc(loaded, 16)

            @block.tensor
            def _(pe):
                pe.wait_ge(ready, 1)
                n = 0
                for c in range(TT):
                    for step in range(STEPS):
                        for hf in range(2):
                            if n >= 2:
                                pe.wait_ge(taken, n - 1)
                            for h in range(4 * hf, 4 * hf + 4):
                                last = products(pe, c, step, h, out_of(step, h, bank[n % 8]))
                            last.then_inc(made, 1)
                            n += 1

            @block.vector
            def _(dve):
                dve.wait_ge(loaded, 32)
                dve.memset(state[:], 0.0)
                dve.tensor_copy(escale[:, :, TT - 1:TT], end_e[:].rearrange("p (m t) -> p m t", t=TT)[:, :, TT - 1:TT])
                dve.tensor_tensor(escale[:, :, 0:TT - 1], end_e[:].rearrange("p (m t) -> p m t", t=TT)[:, :, 0:TT - 1],
                                  mid_e[:].rearrange("p (m t) -> p m t", t=TT)[:, :, 1:TT], ALU.mult).then_inc(ready, 1)
                dve.wait_ge(ready, 1)
                mask = lambda j: bcast(masks[:, j, :], 4, 1)
                ident = bcast(k.ident[:], 4, 1)
                n = 0
                for c in range(TT):
                    for step in range(STEPS):
                        for hf in range(2):
                            hs, half = slice(4 * hf, 4 * hf + 4), slice(RN * hf, RN * hf + RN)
                            full = bank[n % 8][:].rearrange("p (h n) -> p h n", n=P)
                            dve.wait_ge(made, n + 1)
                            tt, cp = dve.tensor_tensor, dve.tensor_copy
                            if step == 0:
                                tt(MdT[:, hs], full, mask(0), ALU.mult).then_inc(ready, 1)
                                dve.wait_ge(ready, 2 + 2 * c + hf)
                                ins = tt(T[:, hs], MdT[:, hs], ident, ALU.add)
                            elif step == 1:
                                tt(Md[:, hs], full, mask(1), ALU.mult)
                                ins = tt(Moff[:, hs], full, mask(2), ALU.mult)
                            elif step == 2:
                                ins = tt(A2T[:, hs], full, mask(3), ALU.mult)
                            elif step in (3, 4):
                                ins = tt((A3T if step == 3 else A4T)[:, hs], full, mask(4), ALU.mult)
                            elif step in (7, 10, 12):
                                ins = tt(T[:, hs], full, T[:, hs], ALU.add)
                            elif step in (17, 19):
                                ins = tt(Z[:, hs], full, Z[:, hs], ALU.add)
                            elif step in (5, 6, 8, 9, 11, 13, 15, 16, 18, 21):
                                dst = {5: Pa, 6: Pb, 8: Pc, 9: Pd, 11: Pa, 13: N, 15: Pa, 16: Pb, 18: Pc, 21: X1}[step]
                                ins = cp(dst[:, hs], full)
                            elif step == 14:
                                cp(NT[:, hs], full)
                                ins = tt(Z[:, hs], full, ident, ALU.add)
                            elif step == 20:
                                cp(X[:, hs, 0:RN], kkT[:, :, c, half])
                                ins = cp(X[:, hs, RN:P], full[:, :, 0:RN])
                            elif step == 22:
                                ins = dve.tensor_scalar(WU[:, hs], full, -1.0, None, ALU.mult)
                            elif step == 23:
                                ins = tt(RtT[half, 0:4], full[half], KR[half, :, c, 1, :], ALU.add)
                            elif step == 24:
                                ins = tt(PTI[half, 0:4, 0:RN], full[half, :, 0:RN], bcast(id64[half], 4, 1), ALU.add)
                            elif step == 25:
                                ins = cp(y[:, c].rearrange("p (m o) n -> p m o n", o=2)[:, :, hf, :], full[:, :, 0:RN])
                            else:
                                for m in range(RP):
                                    ins = dve.tensor_scalar(state[half, m, :], full[half, m, 0:RN], escale[half, m, c:c + 1], None, ALU.mult)
                            ins.then_inc(taken, 1)
                            n += 1


def rwkv_finish_stage(nc, k, g, y, v_tp, bonus, sgate, oT, bufs):
    with ExitStack() as stack:
        r = Room(nc, stack, "rfin")
        lnw, lnb, wg = r.sb("lnw", [P, S]), r.sb("lnb", [P, S]), r.sb("wg", [P, S])
        mean, var, root = [r.sb(n, [P, TT * RH]) for n in ("mean", "var", "root")]
        sq = r.sb("sq", [P, TT * RH, RN])
        ps = [r.ps(f"ps{u}") for u in range(8)]
        loaded, gates, vars_, roots, rows, turned, chain = r.sem("loaded", "gates", "vars", "roots", "rows", "turned", "chain")
        with nc.Block() as block:
            @block.sync
            def _(sp):
                sp.dma_start(lnw[:], g["ln_x_w"].to_broadcast([P, S])).then_inc(loaded, 16)
                sp.dma_start(lnb[:], g["ln_x_b"].to_broadcast([P, S])).then_inc(loaded, 16)
                sp.dma_start(wg[:], g["w_gate_up"]).then_inc(loaded, 16)

            @block.tensor
            def _(pe):
                pe.wait_ge(loaded, 48)
                for t in range(TT):
                    pe.matmul(ps[t][:], sgate[:, t * P:(t + 1) * P], wg[:], start=True, stop=True).then_inc(gates, 1)
                for m in range(4):
                    pe.wait_ge(rows, TT)
                    for t in range(TT):
                        last = pe.transpose(ps[4 + m][:, t * P:(t + 1) * P], y[:, t, 2 * m:2 * m + 2, :].rearrange("p h n -> p (h n)"), k.ident[:])
                    last.then_inc(turned, 1)

            @block.scalar
            def _(act):
                act.wait_ge(vars_, 1)
                act.activation(root[:], var[:], ACT.Sqrt).then_inc(roots, 1)
                for m in range(4):
                    act.wait_ge(turned, m + 1)
                    act.activation(oT[:, m, :], ps[4 + m][:], ACT.Copy)

            @block.vector
            def _(dve):
                link = Chain(dve, chain)
                yg = y[:].rearrange("p t h n -> p (t h) n")
                link(dve.reduce_sum(mean[:], yg, AX))
                link(dve.tensor_scalar(mean[:], mean[:], 1.0 / RN, None, ALU.mult))
                link(dve.tensor_tensor(yg, yg, bcast(mean[:], RN, 2), ALU.subtract))
                link(dve.tensor_tensor(sq[:], yg, yg, ALU.mult))
                link(dve.reduce_sum(var[:], sq[:], AX))
                dve.tensor_scalar(var[:], var[:], 1.0 / RN, GN_EPS, ALU.mult, ALU.add).then_inc(vars_, 1)
                dve.wait_ge(roots, 1)
                link(dve.reciprocal(root[:], root[:]))
                link(dve.tensor_tensor(yg, yg, bcast(root[:], RN, 2), ALU.mult))
                dve.wait_ge(loaded, 48)
                yt = y[:].rearrange("p t h n -> p t (h n)")
                link(dve.tensor_tensor(yt, yt, bcast(lnw[:], TT, 1), ALU.mult))
                link(dve.tensor_tensor(yt, yt, bcast(lnb[:], TT, 1), ALU.add))
                v4 = v_tp.rearrange("p m t (o n) -> p m t o n", n=RN)
                s4 = sq[:].rearrange("p (t m o) n -> p t m o n", m=RP, o=2)
                b4 = bonus[:].rearrange("p t (m o) -> p t m o", o=2)
                for t in range(TT):
                    ins = dve.tensor_tensor(s4[:, t], v4[:, :, t], bcast(b4[:, t], RN, 3), ALU.mult)
                link(ins)
                link(dve.tensor_tensor(yg, yg, sq[:], ALU.add))
                for t in range(TT):
                    dve.wait_ge(gates, t + 1)
                    dve.tensor_tensor(yt[:, t], yt[:, t], ps[t][:], ALU.mult).then_inc(rows, 1)


def merge_stage(nc, name, z, gate0, branches, out, kc=4, bias=None):
    nb = len(branches)
    with ExitStack() as stack:
        r = Room(nc, stack, name)
        w = [[r.sb(f"w{i}_{u}", [P, kc, P]) for u in range(2)] for i in range(nb)]
        part = r.sb("part", [P, nb, S])
        ps = [[r.ps(f"ps{i}_{u}") for u in range(2)] for i in range(nb)]
        made, taken, squashed, chain = r.sem("made", "taken", "squashed", "chain")
        w_ready = [[r.sem(f"w_ready{i}_{u}") for u in range(2)] for i in range(nb)]
        srcs = [w_dram.rearrange("(c p) (m n) -> m p c n", p=P, n=P) for w_dram, _ in branches]
        with nc.Block() as block:
            @block.sync
            def _(sp):
                for m in range(DC):
                    for i in range(nb):
                        if m >= 2:
                            sp.wait_ge(made, nb * (m - 2) + i + 1)
                        sp.dma_start(w[i][m % 2][:], srcs[i][m]).then_inc(w_ready[i][m % 2], 16)

            @block.scalar
            def _(act):
                for m in range(DC):
                    for i in range(nb):
                        gate = z[:, gate0 + i * DC + m, :]
                        extra = {} if bias is None else {"bias": bias[:, i * DC + m:i * DC + m + 1]}
                        act.activation(gate, gate, ACT.Sigmoid, **extra).then_inc(squashed, 1)

            @block.tensor
            def _(pe):
                for m in range(DC):
                    for i, (_, o) in enumerate(branches):
                        pe.wait_ge(w_ready[i][m % 2], 16 * (m // 2 + 1))
                        if m >= 2:
                            pe.wait_ge(taken, m - 1)
                        for c in range(kc):
                            last = pe.matmul(ps[i][m % 2][:], w[i][m % 2][:, c, :], o[:, c, :], start=c == 0, stop=c == kc - 1)
                        last.then_inc(made, 1)

            @block.vector
            def _(dve):
                link = Chain(dve, chain)
                for m in range(DC):
                    for i in range(nb):
                        dve.wait_ge(squashed, nb * m + i + 1)
                        dve.wait_ge(made, nb * m + i + 1)
                        ins = dve.tensor_tensor(part[:, i, :], ps[i][m % 2][:], z[:, gate0 + i * DC + m, :], ALU.mult)
                        if i == nb - 1:
                            ins.then_inc(taken, 1)
                            dve.wait_ge(taken, m + 1)
                    for i in range(1, nb):
                        last = i == nb - 1
                        link(dve.tensor_tensor(out[:, m, :] if last else part[:, 0, :], part[:, 0, :], part[:, i, :], ALU.add))

SPILL_CHOOSE, SPILL_SPREAD = 48, 32
SPILL = SPILL_CHOOSE + SPILL_SPREAD


class Down:

    def __init__(self, r, parts, downT, spill, gelu, base):
        self.hhi, self.hlo = parts
        self.downT, self.spill, self.gelu, self.base = downT, spill, gelu, base
        self.raw, self.hi, self.lo = [[r.sb(f"{n}{u}", [P, DC, P], dt) for u in range(2)] for n, dt in (("uraw", F32), ("uhi", F32R), ("ulo", F32R))]
        self.actv = [r.sb(f"act{u}", [P, S]) for u in range(2)]
        self.pa = [r.ps(f"pa{u}") for u in range(2)]
        self.u_hi, self.u_lo, self.a_made, self.act_made = r.sem("u_hi", "u_lo", "a_made", "act_made")
        self.u_in, self.stored = [[r.sem(f"{n}{u}") for u in range(2)] for n in ("u_in", "act_stored")]

    def load(self, sp, n, j):
        wait_above(sp, self.u_lo, n - 1)
        sp.dma_start(self.raw[j][:], block_of(self.downT, self.base + n)).then_inc(self.u_in[j], 16)

    def split_high(self, act, n, j):
        act.wait_ge(self.u_in[j], 8 * n + 16 - 8 * j)
        wait_above(act, self.a_made, n)
        act.activation(self.hi[j][:], self.raw[j][:], ACT.Copy).then_inc(self.u_hi, 1)

    def split_low(self, dve, n, j):
        dve.wait_ge(self.u_hi, n + 1)
        dve.tensor_tensor(self.lo[j][:], self.raw[j][:], self.hi[j][:].bitcast(F32), ALU.subtract).then_inc(self.u_lo, 1)

    def products(self, pe, n, j, chunks):
        if chunks[0] == 0:
            pe.wait_ge(self.u_lo, n + 1)
            pe.wait_ge(self.act_made, n + 1)
        a = self.pa[j][:]
        for c in chunks:
            hi, lo = self.hi[j][:, c, :], self.lo[j][:, c, :]
            pe.matmul(a, hi, self.hhi[:, c, :], start=c == 0, stop=False)
            pe.matmul(a, hi, self.hlo[:, c, :], start=False, stop=False)
            last = pe.matmul(a, lo, self.hhi[:, c, :], start=False, stop=c == DC - 1)
        if chunks[-1] == DC - 1:
            last.then_inc(self.a_made, 1)

    def store(self, act, n, j):
        act.wait_ge(self.a_made, n + 2)
        act.wait_ge(self.stored[j], 8 * n + 16 - 8 * j)
        act.activation(self.actv[j][:], self.pa[j][:], self.gelu).then_inc(self.act_made, 1)
        act.wait_ge(self.act_made, n + 3)
        act.dma_start(block_of(self.spill, self.base + n), self.actv[j][:]).then_inc(self.stored[j], 16)


def block_of(dram, n):
    if isinstance(n, int):
        return dram[n]
    got = dram[ds(n, 1)]
    return got.rearrange("a p c e -> (a p) c e") if len(dram.shape) == 4 else got.rearrange("a p d -> (a p) d")


def choose_stage(nc, name, k, g, qT, keys_in, keys_of, e1T, e2T, gT, parts, downT, spill, gelu):
    with ExitStack() as stack:
        r = Room(nc, stack, name)
        nkeys = keys_in.shape[1]
        down = Down(r, parts, downT, spill, gelu, 0)
        PER, FIRST, N = SPILL_CHOOSE // TT, 4, SPILL_CHOOSE

        def blocks(eng, lo, hi, body):
            with eng.Fori(lo // 2, hi // 2) as i:
                for j in range(2):
                    body(2 * i + j, j)

        keys = r.sb("keys", [P, nkeys, NK])
        v, idx, left = r.sb("v", [P, 2 * PH, K16]), r.sb("idx", [P, 2 * PH, K16], U32), r.sb("left", [P, 2, NK])
        idf = r.sb("idf", [P, 2 * PH, K16])
        cand, cleft = r.sb("cand", [P, PH, 256]), r.sb("cleft", [P, PH, 256])
        tv, pos = r.sb("tv", [P, PH, K16]), r.sb("pos", [P, PH, K16], U32)
        part, partf = r.sb("part", [P, 2, PH * K16], U32), r.sb("partf", [P, 2, PH * K16])
        iota, hit = r.sb("iota", [P, K16]), r.sb("hit", [P, PH * K16, K16])
        found = r.sb("found", [P, 2, 3, NJ])
        total = r.sb("total", [P, PH])
        ps = [r.ps(f"ps{u}") for u in range(4)]
        pt = r.ps("pt")
        loaded, scored, read, centred, exped, chosen, turned, kept, chain = r.sem(
            "loaded", "scored", "read", "centred", "exped", "chosen", "turned", "kept", "chain")
        scores = lambda c: ps[c // 4][:, (c % 4) * NK:(c % 4 + 1) * NK]
        with nc.Block() as block:
            @block.sync
            def _(sp):
                sp.dma_start(keys[:], keys_in).then_inc(loaded, 16)
                sp.dma_start(iota[:], g["iota16"].to_broadcast([P, K16])).then_inc(loaded, 16)
                for u in range(2):
                    sp.sem_inc(down.stored[u], 16)
                    down.load(sp, u, u)
                blocks(sp, 2, N, lambda n, j: down.load(sp, n, j))
                for u in range(2):
                    sp.wait_ge(down.stored[u], 8 * N + 16)

            @block.tensor
            def _(pe):
                def score(t):
                    for c in range(2 * PH):
                        last = pe.matmul(scores(c), qT[:, c, t * P:(t + 1) * P], keys[:, keys_of(c), :], start=True, stop=True)
                    last.then_inc(scored, 1)

                def turn(t):
                    pe.wait_ge(chosen, t + 1)
                    if t:
                        pe.wait_ge(kept, t)
                    for j in range(3):
                        last = pe.transpose(pt[:, j * P:(j + 1) * P], found[:, t % 2, j, :], k.ident[:])
                    last.then_inc(turned, 1)

                products = lambda n, j: down.products(pe, n, j, range(DC))
                pe.sem_inc(down.a_made, 1)
                pe.wait_ge(loaded, 32)
                score(0)
                for t in range(TT):
                    blocks(pe, PER * t, PER * t + 2, products)
                    if t:
                        turn(t - 1)
                    blocks(pe, PER * t + 2, PER * t + FIRST, products)
                    if t < TT - 1:
                        pe.wait_ge(read, t + 1)
                        score(t + 1)
                    blocks(pe, PER * t + FIRST, PER * (t + 1), products)
                turn(TT - 1)

            @block.scalar
            def _(act):
                def store_and_split(n, j):
                    down.store(act, n, j)
                    if not (isinstance(n, int) and n >= N - 2):
                        down.split_high(act, n + 2, j)

                def keep(t):
                    act.wait_ge(turned, t + 1)
                    for j, dst in enumerate((e1T, e2T, gT)):
                        ins = act.activation(dst[:, t * P:(t + 1) * P], pt[:, j * P:(j + 1) * P], ACT.Copy)
                    ins.then_inc(kept, 1)

                act.sem_inc(down.act_made, 2)
                for u in range(2):
                    down.split_high(act, u, u)
                for t in range(TT):
                    blocks(act, PER * t, PER * t + 2, store_and_split)
                    if t:
                        keep(t - 1)
                    blocks(act, PER * t + 2, PER * (t + 1) - 4, store_and_split)
                    act.wait_ge(centred, t + 1)
                    act.activation(tv[:], tv[:], ACT.Exp).then_inc(exped, 1)
                    if t < TT - 1:
                        blocks(act, PER * (t + 1) - 4, PER * (t + 1), store_and_split)
                    else:
                        blocks(act, N - 4, N - 2, store_and_split)
                        store_and_split(N - 2, 0)
                        store_and_split(N - 1, 1)
                keep(TT - 1)

            @block.vector
            def _(dve):
                link = Chain(dve, chain)

                def top16(*lists):
                    lag = link.lag
                    for vals, index, data, rest in lists:
                        lag(dve.max(vals[:, 0:8], data))
                    for vals, index, data, rest in lists:
                        lag(dve.max_index(index[:, 0:8], vals[:, 0:8], data))
                    for vals, index, data, rest in lists:
                        lag(dve.match_replace(rest, vals[:, 0:8], data, -3e38))
                    for vals, index, data, rest in lists:
                        lag(dve.max(vals[:, 8:16], rest))
                    for vals, index, data, rest in lists:
                        lag(dve.max_index(index[:, 8:16], vals[:, 8:16], rest))

                def split_low(n):
                    if n < N:
                        down.split_low(dve, n, n % 2)

                dve.wait_ge(loaded, 32)
                split_low(0)
                for t in range(TT):
                    dve.wait_ge(scored, t + 1)
                    for c in range(0, 2 * PH, 2):
                        top16(*[(v[:, d], idx[:, d], scores(d), left[:, d % 2, :]) for d in (c, c + 1)])
                        if c % 4 == 2:
                            split_low(PER * t + 1 + c // 4)
                    link.settle()
                    dve.sem_inc(read, 1)
                    v4 = v[:].rearrange("p (h s) n -> p h s n", s=2)
                    link(dve.tensor_tensor(cand[:].rearrange("p h (a b) -> p h a b", b=K16),
                                           bcast(v4[:, :, 0, :], K16, 3), bcast(v4[:, :, 1, :], K16, 2), ALU.add))
                    split_low(PER * t + 5)
                    for h in range(0, PH, 2):
                        top16(*[(tv[:, d], pos[:, d], cand[:, d], cleft[:, d]) for d in (h, h + 1)])
                        if h:
                            split_low(PER * t + 5 + h // 2)
                    link.settle()
                    link(dve.tensor_copy(total[:], tv[:, :, 0]))
                    dve.tensor_tensor(tv[:], tv[:], bcast(total[:], K16, 2), ALU.subtract).then_inc(centred, 1)
                    split_low(PER * t + 9)
                    posf = pos[:].rearrange("p h n -> p (h n)")
                    link(dve.tensor_single_scalar(part[:, 0], posf, 4, ALU.logical_shift_right))
                    link(dve.tensor_single_scalar(part[:, 1], posf, 15, ALU.bitwise_and))
                    link(dve.tensor_copy(partf[:], part[:]))
                    link(dve.tensor_copy(idf[:], idx[:]))
                    id4 = idf[:].rearrange("p (h s) n -> p h s n", s=2)
                    hit4 = hit[:].rearrange("p (h n) a -> p h n a", h=PH)
                    if t >= 2:
                        dve.wait_ge(turned, t - 1)
                    for s in range(2):
                        link(dve.tensor_tensor(hit[:], bcast(partf[:, s], K16, 2), bcast(iota[:], NJ, 1), ALU.is_equal))
                        link(dve.tensor_tensor(hit4, hit4, bcast(id4[:, :, s, :], K16, 2), ALU.mult))
                        link(dve.reduce_sum(found[:, t % 2, s, :], hit[:], AX))
                        split_low(PER * t + 10 + s)
                    dve.wait_ge(exped, t + 1)
                    link(dve.reduce_sum(total[:], tv[:], AX))
                    link(dve.reciprocal(total[:], total[:]))
                    dve.tensor_tensor(found[:, t % 2, 2, :].rearrange("p (h n) -> p h n", h=PH), tv[:], bcast(total[:], K16, 2), ALU.mult).then_inc(chosen, 1)
                    split_low(PER * t + 12)


def spread_stage(nc, name, g, e1T, e2T, gT, gates_dram, parts, downT, spill, gelu):
    with ExitStack() as stack:
        r = Room(nc, stack, name)
        iota = r.sb("iota", [P, NK])
        oh1, oh2 = [[r.sb(f"oh{x}_{u}", [P, 4, NK]) for u in range(2)] for x in (1, 2)]
        tile = [r.sb(f"tile{u}", [P, NK, SUB]) for u in range(2)]
        ps = [r.ps(f"ps{u}") for u in range(4)]
        loaded, hot1, hot2, made, kept = r.sem("loaded", "hot1", "hot2", "made", "kept")
        stored = [r.sem(f"stored{u}") for u in range(2)]
        down = Down(r, parts, downT, spill, gelu, SPILL_CHOOSE)
        N = SPILL_SPREAD
        GROUPS, SUBS = SUB // 4, S // SUB
        assert N * 4 == GROUPS * SUBS and SUBS % 2 == 0

        def turns(eng, body, before=None, after=None):
            with eng.Fori(0, SUBS // 2) as i:
                for u in range(2):
                    if before:
                        before(i, u)
                    with eng.Fori(0, GROUPS // 8) as h:
                        for j in range(2):
                            body(8 * i + 4 * u + 2 * h + j, j, u, 2 * h + j)
                    if after:
                        after(i, u)

        with nc.Block() as block:
            @block.sync
            def _(sp):
                sp.dma_start(iota[:], g["iota128"].to_broadcast([P, NK])).then_inc(loaded, 16)
                for u in range(2):
                    sp.sem_inc(stored[u], 16)
                    sp.sem_inc(down.stored[u], 16)
                    down.load(sp, u, u)
                down.load(sp, 2, 0)
                with sp.Fori(1, N // 2) as i:
                    for j in range(2):
                        down.load(sp, 2 * i + 1 + j, 1 - j)
                for u in range(2):
                    sp.wait_ge(stored[u], 16 * (SUBS // 2) + 16)
                    sp.wait_ge(down.stored[u], 8 * N + 16)

            @block.vector
            def _(dve):
                def body(m, j, u, place):
                    for b in range(4):
                        n = 4 * m + b
                        dve.wait_ge(made, n + 1)
                        for x in range(4):
                            tok = ds(4 * n + x, 1)
                            ins = dve.tensor_scalar(oh1[b % 2][:, x, :], iota[:], e1T[:, tok], gT[:, tok], ALU.is_equal, ALU.mult)
                        ins.then_inc(hot1, 1)
                        dve.tensor_tensor(oh2[b % 2][:], bcast(iota[:], 4, 1), bcast(e2T[:, ds(4 * n, 4)], NK, 2), ALU.is_equal).then_inc(hot2, 1)
                        if b == 2:
                            down.split_low(dve, m + 1, 1 - j)

                dve.wait_ge(loaded, 16)
                down.split_low(dve, 0, 0)
                turns(dve, body)

            @block.tensor
            def _(pe):
                def body(m, j, u, place):
                    for b in range(4):
                        n = 4 * m + b
                        down.products(pe, m, j, (2 * b, 2 * b + 1))
                        pe.wait_ge(hot1, n + 1)
                        pe.wait_ge(hot2, n + 1)
                        pe.wait_ge(kept, n + 1)
                        for x in range(4):
                            last = pe.matmul(ps[b][:, x * NK:(x + 1) * NK], oh2[b % 2][:, x, :], oh1[b % 2][:, x, :], start=True, stop=True)
                        last.then_inc(made, 1)

                pe.sem_inc(made, 2)
                pe.sem_inc(down.a_made, 1)
                turns(pe, body)

            @block.scalar
            def _(act):
                def before(i, u):
                    act.wait_ge(stored[u], 16 * i + 16)

                def body(m, j, u, place):
                    down.split_high(act, m + 1, 1 - j)
                    for b in range(4):
                        act.wait_ge(made, 4 * m + b + 3)
                        act.activation(tile[u][:, :, ds(place * 16 + 4 * b, 4)].rearrange("p e t -> p t e"),
                                       ps[b][:].rearrange("p (t e) -> p t e", e=NK), ACT.Copy).then_inc(kept, 1)
                    down.store(act, m, j)

                def after(i, u):
                    act.wait_ge(kept, 2 * GROUPS * i + GROUPS * (u + 1) + 4)
                    act.dma_start(block_of(gates_dram, 2 * i + u), tile[u][:]).then_inc(stored[u], 16)

                act.sem_inc(kept, 4)
                act.sem_inc(down.act_made, 2)
                down.split_high(act, 0, 0)
                turns(act, body, before, after)


def wait_above(eng, sem, value):
    if not isinstance(value, int) or value > 0:
        eng.wait_ge(sem, value)


def experts_stage(nc, name, parts, downT, up, gates_dram, acc, gelu):
    NB = NK - SPILL
    assert NB % 8 == 0
    downT, up, gates_dram, (hhi, hlo) = downT[SPILL:], up[SPILL:], gates_dram[:, :, SPILL:], parts
    IT = NB // 8
    with ExitStack() as stack:
        r = Room(nc, stack, name)
        uraw, uhi, ulo = [[r.sb(f"{n}{u}", [P, DC, P], dt) for u in range(2)] for n, dt in (("uraw", F32), ("uhi", F32R), ("ulo", F32R))]
        vraw = [r.sb(f"vraw{u}", [P, D]) for u in range(2)]
        vhi, vlo = r.sb("vhi", [P, 4, D], F32R), r.sb("vlo", [P, 4, D], F32R)
        gate = [r.sb(f"gate{u}", [P, S // SUB, 4, SUB]) for u in range(2)]
        actv = [r.sb(f"act{u}", [P, S]) for u in range(2)]
        wfull = [r.sb(f"w{u}", [P, S]) for u in range(2)]
        whi, wlo = [[r.sb(f"{n}{u}", [P, 4, S], F32R) for u in range(2)] for n in ("whi", "wlo")]
        pa = [r.ps(f"pa{u}") for u in range(2)]
        po = [r.ps(f"po{u}") for u in range(4)]
        u_hi, u_lo, v_hi, v_lo, a_made, act_made, w_made, w_hi, w_lo, o_made, o_added = r.sem(
            "u_hi", "u_lo", "v_hi", "v_lo", "a_made", "act_made", "w_made", "w_hi", "w_lo", "o_made", "o_added")
        u_in, v_in, g_in = [[r.sem(f"{n}{u}") for u in range(2)] for n in ("u_in", "v_in", "g_in")]

        def loop(eng, body):
            body(0)
            with eng.Fori(1, IT - 1) as i:
                body(i)
            body(IT - 1)

        last_turn = lambda i: isinstance(i, int) and i == IT - 1

        with nc.Block() as block:
            @block.sync
            def _(sp):
                def body(i):
                    for j in range(8):
                        n = 8 * i + j
                        if j % 4 == (2 if isinstance(n, int) and n < 4 else 0):
                            grp, gp = 2 * i + j // 4, j // 4
                            wait_above(sp, w_made, 4 * grp - 4)
                            src = gates_dram[:, :, ds(4 * grp, 4), :] if not isinstance(grp, int) else gates_dram[:, :, 4 * grp:4 * grp + 4, :]
                            sp.dma_start(gate[gp][:], src.rearrange("s p e t -> p s e t")).then_inc(g_in[gp], 16)
                        wait_above(sp, u_lo, n - 1)
                        src = downT[n] if isinstance(n, int) else downT[ds(n, 1)].rearrange("a p c e -> (a p) c e")
                        sp.dma_start(uraw[j % 2][:], src).then_inc(u_in[j % 2], 16)

                loop(sp, body)

            @block.scalar
            def _(act):
                def split_u(n, j):
                    act.wait_ge(u_in[j % 2], 8 * n + 16 - 8 * (j % 2))
                    wait_above(act, a_made, n - 1)
                    act.activation(uhi[j % 2][:], uraw[j % 2][:], ACT.Copy).then_inc(u_hi, 1)

                def split_v(n, j):
                    act.wait_ge(v_in[j % 2], 8 * n + 16 - 8 * (j % 2))
                    wait_above(act, o_made, 2 * (n - j % 4))
                    act.activation(vhi[:, j % 4, :], vraw[j % 2][:], ACT.Copy).then_inc(v_hi, 1)

                def load_v(n, j):
                    wait_above(act, v_lo, n - 1)
                    src = up[n] if isinstance(n, int) else up[ds(n, 1)].rearrange("a p d -> (a p) d")
                    act.dma_start(vraw[j % 2][:], src).then_inc(v_in[j % 2], 16)

                def body(i):
                    for j in range(8):
                        n = 8 * i + j
                        act.wait_ge(a_made, n + 1)
                        wait_above(act, w_made, n - 1)
                        act.activation(actv[j % 2][:], pa[j % 2][:], gelu).then_inc(act_made, 1)
                        if not (last_turn(i) and j >= 6):
                            split_u(n + 2, (j + 2) % 8)
                        if j % 4 != 1 and not (last_turn(i) and j == 7):
                            load_v(n + 1, j + 1)
                        act.wait_ge(w_made, n + 1)
                        act.activation(whi[j // 4][:, j % 4, :], wfull[j % 2][:], ACT.Copy).then_inc(w_hi, 1)
                        if j % 4 == 1:
                            split_v(n - 1, j - 1)
                        if j % 4:
                            split_v(n, j)
                        if j % 4 == 1:
                            load_v(n + 1, j + 1)

                load_v(0, 0)
                split_u(0, 0)
                split_u(1, 1)
                loop(act, body)

            @block.vector
            def _(dve):
                def split_u(n, j):
                    dve.wait_ge(u_hi, n + 1)
                    dve.tensor_tensor(ulo[j % 2][:], uraw[j % 2][:], uhi[j % 2][:].bitcast(F32), ALU.subtract).then_inc(u_lo, 1)

                def split_v(n, j):
                    dve.wait_ge(v_hi, n + 1)
                    dve.tensor_tensor(vlo[:, j % 4, :], vraw[j % 2][:], vhi[:, j % 4, :].bitcast(F32), ALU.subtract).then_inc(v_lo, 1)

                def add_group(grp):
                    for d in range(DC):
                        dve.wait_ge(o_made, 8 * grp + d + 1)
                        dve.tensor_tensor(acc[:, d, :], po[d % 4][:], acc[:, d, :], ALU.add).then_inc(o_added, 1)

                def body(i):
                    for j in range(8):
                        n, grp = 8 * i + j, 2 * i + j // 4
                        if j % 4 == 0:
                            dve.wait_ge(g_in[j // 4], 16 * i + 16)
                        dve.wait_ge(act_made, n + 1)
                        wait_above(dve, w_lo, n - 1)
                        q3 = lambda ap: ap.rearrange("p (s t) -> p s t", t=SUB)
                        dve.tensor_tensor(q3(wfull[j % 2][:]), q3(actv[j % 2][:]), gate[j // 4][:, :, j % 4, :], ALU.mult).then_inc(w_made, 1)
                        if not (last_turn(i) and j >= 6):
                            split_u(n + 2, (j + 2) % 8)
                        dve.wait_ge(w_hi, n + 1)
                        dve.tensor_tensor(wlo[j // 4][:, j % 4, :], wfull[j % 2][:], whi[j // 4][:, j % 4, :].bitcast(F32), ALU.subtract).then_inc(w_lo, 1)
                        if j % 4 == 1:
                            split_v(n - 1, j - 1)
                        if j % 4:
                            split_v(n, j)
                        if j % 4 == 0 and not (isinstance(n, int) and n == 0):
                            add_group(grp - 1)

                dve.memset(acc[:], 0.0)
                split_u(0, 0)
                split_u(1, 1)
                loop(dve, body)
                add_group(NB // 4 - 1)

            @block.tensor
            def _(pe):
                def down(n, j):
                    pe.wait_ge(u_lo, n + 1)
                    wait_above(pe, act_made, n - 1)
                    a = pa[j % 2][:]
                    for c in range(DC):
                        hi, lo = uhi[j % 2][:, c, :], ulo[j % 2][:, c, :]
                        pe.matmul(a, hi, hhi[:, c, :], start=c == 0, stop=False)
                        pe.matmul(a, hi, hlo[:, c, :], start=False, stop=False)
                        last = pe.matmul(a, lo, hhi[:, c, :], start=False, stop=c == DC - 1)
                    last.then_inc(a_made, 1)

                def up_group(grp, gp):
                    pe.wait_ge(w_lo, 4 * grp + 4)
                    pe.wait_ge(v_lo, 4 * grp + 4)
                    for d in range(DC):
                        wait_above(pe, o_added, 8 * grp + d - 3)
                        for q in range(4):
                            hi, lo = vhi[:, q, d * P:(d + 1) * P], vlo[:, q, d * P:(d + 1) * P]
                            o = po[d % 4][:]
                            pe.matmul(o, hi, whi[gp][:, q, :], start=q == 0, stop=False)
                            pe.matmul(o, hi, wlo[gp][:, q, :], start=False, stop=False)
                            last = pe.matmul(o, lo, whi[gp][:, q, :], start=False, stop=q == 3)
                        last.then_inc(o_made, 1)

                def body(i):
                    for j in range(8):
                        n, grp = 8 * i + j, 2 * i + j // 4
                        down(n, j)
                        if j % 4 == 0 and not (isinstance(n, int) and n == 0):
                            up_group(grp - 1, 1 - j // 4)

                loop(pe, body)
                up_group(NB // 4 - 1, 1)


def spilled_stage(nc, name, up, gates_dram, spill, acc):
    with ExitStack() as stack:
        r = Room(nc, stack, name)
        vraw = [r.sb(f"vraw{u}", [P, D]) for u in range(2)]
        gate = [r.sb(f"gate{u}", [P, S // SUB, 4, SUB]) for u in range(2)]
        actv = [r.sb(f"act{u}", [P, 4, S]) for u in range(2)]
        wfull = [r.sb(f"w{u}", [P, S]) for u in range(2)]
        vhi, vlo = [[r.sb(f"{n}{u}", [P, 4, D], F32R) for u in range(2)] for n in ("vhi", "vlo")]
        whi, wlo = [[r.sb(f"{n}{u}", [P, 4, S], F32R) for u in range(2)] for n in ("whi", "wlo")]
        po = [r.ps(f"po{u}") for u in range(DC)]
        v_hi, v_lo, w_made, w_hi, w_lo, o_made, o_added = r.sem("v_hi", "v_lo", "w_made", "w_hi", "w_lo", "o_made", "o_added")
        v_in, g_in = [[r.sem(f"{n}{u}") for u in range(2)] for n in ("v_in", "g_in")]
        GRPS = SPILL // 4
        assert GRPS % 2 == 0

        def loop(eng, body):
            for gp in range(2):
                body(gp, gp)
            with eng.Fori(1, GRPS // 2) as i:
                for gp in range(2):
                    body(2 * i + gp, gp)

        def four(dram, grp, axis):
            at = slice(4 * grp, 4 * grp + 4) if isinstance(grp, int) else ds(4 * grp, 4)
            return dram[at] if axis == 0 else dram[:, :, at, :]

        with nc.Block() as block:
            @block.sync
            def _(sp):
                def body(grp, gp):
                    wait_above(sp, w_made, 4 * grp - 4)
                    sp.dma_start(actv[gp][:], four(spill, grp, 0).rearrange("e p t -> p e t")).then_inc(g_in[gp], 16)
                    sp.dma_start(gate[gp][:], four(gates_dram, grp, 2).rearrange("s p e t -> p s e t")).then_inc(g_in[gp], 16)
                    for q in range(4):
                        n = 4 * grp + q
                        wait_above(sp, v_lo, n - 1)
                        sp.dma_start(vraw[q % 2][:], block_of(up, n)).then_inc(v_in[q % 2], 16)

                loop(sp, body)

            @block.scalar
            def _(act):
                def body(grp, gp):
                    wait_above(act, o_made, DC * grp - DC)
                    for q in range(4):
                        n = 4 * grp + q
                        act.wait_ge(v_in[q % 2], 8 * n + 16 - 8 * (q % 2))
                        act.activation(vhi[gp][:, q, :], vraw[q % 2][:], ACT.Copy).then_inc(v_hi, 1)
                        act.wait_ge(w_made, n + 1)
                        act.activation(whi[gp][:, q, :], wfull[q % 2][:], ACT.Copy).then_inc(w_hi, 1)

                loop(act, body)

            @block.vector
            def _(dve):
                def add(grp, d):
                    dve.wait_ge(o_made, DC * grp + d + 1)
                    dve.tensor_tensor(acc[:, d, :], po[d][:], acc[:, d, :], ALU.add).then_inc(o_added, 1)

                def body(grp, gp):
                    dve.wait_ge(g_in[gp], 16 * grp + 32 - 16 * gp)
                    for q in range(4):
                        n = 4 * grp + q
                        wait_above(dve, w_lo, n - 1)
                        q3 = lambda ap: ap.rearrange("p (s t) -> p s t", t=SUB)
                        dve.tensor_tensor(q3(wfull[q % 2][:]), q3(actv[gp][:, q, :]), gate[gp][:, :, q, :], ALU.mult).then_inc(w_made, 1)
                        dve.wait_ge(v_hi, n + 1)
                        dve.tensor_tensor(vlo[gp][:, q, :], vraw[q % 2][:], vhi[gp][:, q, :].bitcast(F32), ALU.subtract).then_inc(v_lo, 1)
                        dve.wait_ge(w_hi, n + 1)
                        dve.tensor_tensor(wlo[gp][:, q, :], wfull[q % 2][:], whi[gp][:, q, :].bitcast(F32), ALU.subtract).then_inc(w_lo, 1)
                        if not (isinstance(grp, int) and grp == 0):
                            for d in (2 * q, 2 * q + 1):
                                add(grp - 1, d)

                loop(dve, body)
                for d in range(DC):
                    add(GRPS - 1, d)

            @block.tensor
            def _(pe):
                def body(grp, gp):
                    pe.wait_ge(w_lo, 4 * grp + 4)
                    pe.wait_ge(v_lo, 4 * grp + 4)
                    for d in range(DC):
                        if not (isinstance(grp, int) and grp == 0):
                            pe.wait_ge(o_added, DC * grp - DC + d + 1)
                        for q in range(4):
                            hi, lo = vhi[gp][:, q, d * P:(d + 1) * P], vlo[gp][:, q, d * P:(d + 1) * P]
                            pe.matmul(po[d][:], hi, whi[gp][:, q, :], start=q == 0, stop=False)
                            pe.matmul(po[d][:], hi, wlo[gp][:, q, :], start=False, stop=False)
                            last = pe.matmul(po[d][:], lo, whi[gp][:, q, :], start=False, stop=q == 3)
                        last.then_inc(o_made, 1)

                loop(pe, body)


def residual_stage(nc, name, x, acc, gain=None):
    with ExitStack() as stack:
        r = Room(nc, stack, name)
        with nc.Block() as block:
            @block.vector
            def _(dve):
                for c in range(DC):
                    if gain is None:
                        dve.tensor_tensor(x[:, c, :], x[:, c, :], acc[:, c, :], ALU.add)
                    else:
                        dve.scalar_tensor_tensor(x[:, c, :], acc[:, c, :], gain[:, c:c + 1], x[:, c, :], ALU.mult, ALU.add)


def peer(nc, name, k, ins, xT, hT, w_query, keys, keys_of, downT, up, gates_dram, spill, gelu, gain=None):
    with ExitStack() as split:
        r = Room(nc, split, name + "h")
        parts = r.sb("hhi", [P, DC, S], F32R), r.sb("hlo", [P, DC, S], F32R)
        with ExitStack() as stack:
            r = Room(nc, stack, name)
            e1T, e2T, gT = r.sb("e1T", [P, S]), r.sb("e2T", [P, S]), r.sb("gT", [P, S])
            with ExitStack() as inner:
                qT = Room(nc, inner, name).sb("qT", [P, 2 * PH, S])
                project_stage(nc, name + "q", k, w_query, hT, DC, 2 * PH, qT, parts=parts)
                choose_stage(nc, name + "c", k, ins, qT, keys, keys_of, e1T, e2T, gT, parts, downT, spill, gelu)
            spread_stage(nc, name + "s", ins, e1T, e2T, gT, gates_dram, parts, downT, spill, gelu)
        experts_stage(nc, name + "e", parts, downT, up, gates_dram, hT, gelu)
    spilled_stage(nc, name + "v", up, gates_dram, spill, hT)
    residual_stage(nc, name + "r", xT, hT, gain)

def head_norm_stage(nc, name, row_pick, chunks, tokens=S):
    N = len(chunks)
    with ExitStack() as stack:
        r = Room(nc, stack, name)
        sq = [r.sb(f"sq{u}", [P, tokens]) for u in range(2)]
        rstd, gains, pick = r.sb("rstd", [2 * N, tokens]), r.sb("gains", [P, N]), r.sb("pick", [2 * N, N, P])
        ones = {width: r.sb(f"ones{width}", [P, 4 * N]) for width in sorted({c[2] for c in chunks})}
        mean, ps = r.ps("mean"), [r.ps(f"ps{u}") for u in range(4)]
        loaded, ones_ready, squared, summed, mean_ready, rooted, inverted, spread, done, chain = r.sem(
            "loaded", "ones_ready", "squared", "summed", "mean_ready", "rooted", "inverted", "spread", "done", "chain")
        with nc.Block() as block:
            @block.sync
            def _(sp):
                sp.dma_start(pick[:], row_pick[0:2 * N, 0:N, :]).then_inc(loaded, 16)

            @block.scalar
            def _(act):
                for n in range(N):
                    if n >= 2:
                        act.wait_ge(summed, n - 1)
                    act.activation(sq[n % 2][:], chunks[n][0], ACT.Square).then_inc(squared, 1)
                act.wait_ge(mean_ready, 1)
                act.activation(rstd[:], rstd[:], ACT.Sqrt).then_inc(rooted, 1)

            @block.tensor
            def _(pe):
                pe.wait_ge(ones_ready, 1)
                for n, (_, _, width, _) in enumerate(chunks):
                    pe.wait_ge(squared, n + 1)
                    pe.matmul(mean[0:2 * N, 0:tokens], ones[width][:, 2 * (N - n):2 * (2 * N - n)], sq[n % 2][:],
                              start=n == 0, stop=n == N - 1).then_inc(summed, 1)
                pe.wait_ge(loaded, 16)
                pe.wait_ge(inverted, 1)
                for n in range(N):
                    if n >= 4:
                        pe.wait_ge(done, n - 3)
                    pe.matmul(ps[n % 4][:, 0:tokens], pick[:, n, :], rstd[:], start=True, stop=True).then_inc(spread, 1)

            @block.vector
            def _(dve):
                link = Chain(dve, chain)
                for width, at in ones.items():
                    ins = dve.memset(at[:], 0.0)
                link(ins)
                for width, at in ones.items():
                    for u in range(2):
                        half = slice(u * P // 2, (u + 1) * P // 2) if width < P else slice(0, P)
                        ins = dve.memset(at[half, 2 * N + u:2 * N + u + 1], 1.0 / width)
                ins.then_inc(ones_ready, 1)
                for n, (_, gain, _, times) in enumerate(chunks):
                    ins = dve.tensor_scalar(gains[:, n:n + 1], gain, times, None, ALU.mult)
                link(ins)
                dve.wait_ge(summed, N)
                dve.tensor_scalar(rstd[:], mean[0:2 * N, 0:tokens], EPS, None, ALU.add).then_inc(mean_ready, 1)
                dve.wait_ge(rooted, 1)
                dve.reciprocal(rstd[:], rstd[:]).then_inc(inverted, 1)
                for n in range(N):
                    chunk = chunks[n][0]
                    dve.wait_ge(spread, n + 1)
                    dve.scalar_tensor_tensor(chunk, chunk, gains[:, n:n + 1], ps[n % 4][:, 0:tokens], ALU.mult, ALU.mult).then_inc(done, 1)


def turn_stage(nc, name, k, units):
    with ExitStack() as stack:
        r = Room(nc, stack, name)
        pt = [r.ps(f"pt{u}") for u in range(4)]
        turned, copied = r.sem("turned", "copied")
        with nc.Block() as block:
            @block.tensor
            def _(pe):
                for n, (srcs, _) in enumerate(units):
                    if n >= 4:
                        pe.wait_ge(copied, n - 3)
                    for j, src in enumerate(srcs):
                        last = pe.transpose(pt[n % 4][:, j * P:(j + 1) * P], src, k.ident[:])
                    last.then_inc(turned, 1)

            @block.vector
            def _(dve):
                for n, (srcs, dst) in enumerate(units):
                    dve.wait_ge(turned, n + 1)
                    dve.tensor_copy(dst, pt[n % 4][:, 0:len(srcs) * P].rearrange("p (t n) -> p t n", n=P)).then_inc(copied, 1)


def forget_stage(nc, k, z, bias, fq, fk):
    with ExitStack() as stack:
        r = Room(nc, stack, "forget")
        v, low, mag, c, neg, ones = [r.sb(n, [FH, S]) for n in ("v", "low", "mag", "c", "neg", "ones")]
        raised, absed, logged, summed, filled, moved, chain = r.sem("raised", "absed", "logged", "summed", "filled", "moved", "chain")
        with nc.Block() as block:
            @block.scalar
            def _(act):
                act.wait_ge(raised, 1)
                act.activation(mag[:], v[:], ACT.Abs).then_inc(absed, 1)
                act.wait_ge(absed, 1)
                act.activation(mag[:], mag[:], ACT.Exp, scale=-1.0).then_inc(absed, 1)
                act.wait_ge(absed, 2)
                act.activation(mag[:], mag[:], ACT.Ln, bias=1.0).then_inc(logged, 1)
                act.wait_ge(summed, 1)
                act.wait_ge(filled, 1)
                for h in range(FH):
                    act.dma_start(fk[1:2, h, :], neg[h:h + 1, :]).then_inc(moved, 16)

            @block.vector
            def _(dve):
                link = Chain(dve, chain)
                dve.memset(fq, 1.0)
                dve.memset(fk, 1.0).then_inc(filled, 1)
                dve.memset(ones[:], 1.0)
                link.announce(dve.tensor_scalar(v[:], z[0:FH, Y_FF, :], bias, None, ALU.add), raised, 1)
                link(dve.tensor_scalar(low[:], v[:], 0.0, None, ALU.min))
                dve.wait_ge(logged, 1)
                link(dve.tensor_tensor(low[:], low[:], mag[:], ALU.subtract))
                link(dve.tensor_tensor_scan(c[:], ones[:], low[:], 0.0, ALU.mult, ALU.add))
                dve.tensor_scalar(neg[:], c[:], -1.0, None, ALU.mult).then_inc(summed, 1)

            @block.sync
            def _(sp):
                sp.wait_ge(summed, 1)
                sp.wait_ge(filled, 1)
                for h in range(FH):
                    sp.dma_start(fq[0:1, h, :], c[h:h + 1, :]).then_inc(moved, 16)
                sp.wait_ge(moved, 2 * 16 * FH)


def second_mixer(nc, k, ins, cols, xT, hT):
    with ExitStack() as mixer:
        m = Room(nc, mixer, "mix2")
        z = m.sb("z", [P, Y_N, S])
        project_stage(nc, "p2", k, ins["w_in_2"], hT, DC, Y_N, z)
        foxT, swaT, memT = m.sb("foxT", [P, 4, S]), m.sb("swaT", [P, 4, S]), m.sb("memT", [P, 4, S])
        heads = [(z[:, Y_FQ + i, :], cols("fox_q_g"), FD, FD ** -0.5) for i in range(4)]
        heads += [(z[:, Y_FK + i, :], cols("fox_k_g"), FD, 1.0) for i in range(4)]
        heads += [(z[:, Y_SQ + i, :], cols("swa_q_g"), SD, SD ** -0.5) for i in range(4)]
        heads += [(z[:, Y_SKV, :], cols("swa_k_g"), SD, 1.0)]
        heads += [(z[:, Y_MQ + i, :], cols("mem_q_g"), GD, GD ** -0.5) for i in range(4)]
        head_norm_stage(nc, "hn", ins["row_pick"], heads)
        tiles = lambda chunk: [chunk[:, t * P:(t + 1) * P] for t in range(chunk.shape[-1] // P)]
        with ExitStack() as local, ExitStack() as fox:
            vs, a = Room(nc, local, "local"), Room(nc, fox, "fox")
            v_tp = vs.sb("v", [P, 5, TT, P])
            fq, fk = hT[0:2], a.sb("fk", [2, FH, S])[:]
            forget_stage(nc, k, z, cols("b_forget")[0:FH], fq, fk)
            turn_stage(nc, "vt", k, [(tiles(z[:, Y_FV + i, :]), v_tp[:, i]) for i in range(4)] + [(tiles(z[:, Y_SKV + 1, :]), v_tp[:, 4])])
            items = []
            for h in range(FH):
                c, half = h // 2, slice(h % 2 * FD, h % 2 * FD + FD)
                for t in range(TT):
                    items.append((z[half, Y_FQ + c, t * P:(t + 1) * P], z[half, Y_FK + c, 0:(t + 1) * P], k.causal[:],
                                  [v_tp[:, c, j, half] for j in range(t + 1)], h, t,
                                  (fq[:, h, t * P:(t + 1) * P], fk[:, h, 0:(t + 1) * P])))
            attention_stage(nc, "foxa", k, items, FH, FD, foxT)
            fox.close()
            alibi, sinks = vs.sb("alibi", [P, SH, 2 * P]), vs.sb("sinks", [P, SH])
            load_stage(nc, "swal", [(alibi[:], ins["alibi"]), (sinks[:], ins["swa_sinks"].to_broadcast([P, SH]))])
            items = []
            for h in range(SH):
                grp = h // (SH // SG)
                half = slice(grp * SD, grp * SD + SD)
                for t in range(TT):
                    k0 = max(t - 1, 0)
                    items.append((z[half, Y_SQ + h % 4, t * P:(t + 1) * P], z[half, Y_SKV, k0 * P:(t + 1) * P],
                                  alibi[:, h, (0 if t else P):2 * P], [v_tp[:, 4, j, half] for j in range(k0, t + 1)], h, t, None))
            attention_stage(nc, "swaa", k, items, SH, SD, swaT, sinks=sinks)
        with ExitStack() as memory:
            a = Room(nc, memory, "mem")
            mT = hT[:, :, 0:NMEM]
            mkv, mv = a.sb("mkv", [P, DC, NMEM]), a.sb("mv", [P, 4, 2, P])
            load_stage(nc, "meml", [(mT, ins["memT"].rearrange("(c p) t -> p c t", p=P))])
            norm_stage(nc, "mn", k, mT, DC, D, cols("mem_norm_g_2"), mT, tokens=NMEM)
            project_stage(nc, "mp", k, ins["w_mem_kv"], mT, DC, DC, mkv, tokens=NMEM)
            head_norm_stage(nc, "mh", ins["row_pick"], [(mkv[:, i, :], cols("mem_k_g"), GD, 1.0) for i in range(4)], tokens=NMEM)
            turn_stage(nc, "mt", k, [(tiles(mkv[:, 4 + i, :]), mv[:, i]) for i in range(4)])
            items = [(z[:, Y_MQ + h, t * P:(t + 1) * P], mkv[:, h, :], None, [mv[:, h, j, :] for j in range(2)], h, t, None)
                     for h in range(GH) for t in range(TT)]
            attention_stage(nc, "mema", k, items, GH, GD, memT)
        merge_stage(nc, "mg2", z, Y_GATE, [(ins["w_fox_o"], foxT), (ins["w_swa_o"], swaT), (ins["w_mem_o"], memT)], hT, bias=cols("b_gate_2"))
    project_stage(nc, "po2", k, ins["w_out_2"], hT, DC, DC, xT, add=(k.ones, xT))

def y_of(t):
    return t[:].rearrange("p t (h n) -> p t h n", n=RN)


class Held:
    pass


def build(nc, ins, where, out):
    with ExitStack() as whole:
        r = Room(nc, whole, "held")
        k = Held()
        k.ident, k.ones = r.sb("ident", [P, P]), r.sb("ones", [P, P])
        k.columns = r.sb("columns", [P, ins["columns"].shape[1]])
        k.causal, k.pair_ones = r.sb("causal", [P, P]), r.sb("pair_ones", [P, P])
        xT, hT, mod = r.sb("xT", [P, DC, S]), r.sb("hT", [P, DC, S]), r.sb("mod", [P, 48])
        gain = r.sb("gain", [P, DC])
        cols = lambda n: k.columns[:, where[n][0]:where[n][1]]
        load_stage(nc, "first", [(k.ident[:], ins["ident"]), (k.columns[:], ins["columns"]), (k.causal[:], ins["causal"]), (k.pair_ones[:], ins["pair_ones"]),
                                 (xT[:], ins["xT"].rearrange("(c p) t -> p c t", p=P))])
        sc = r.sb("silu", [P, DC])
        ada_stage(nc, k, cols("c"), ins["w_ada"], cols("b_ada"), mod, EARLY_ADA, sc)
        gain_stage(nc, "g1", gain, cols("norm_mix"), mod[:, DC:2 * DC])
        norm_stage(nc, "n1", k, xT, DC, D, gain, hT, shift=mod[:, 0:DC])
        with ExitStack() as mixer:
            m = Room(nc, mixer, "mix")
            z = m.sb("z", [P, Z_N, S])
            project_stage(nc, "p1", k, ins["w_in"], hT, DC, Z_N, z,
                          ada=(ins["w_ada"], cols("b_ada"), mod, EARLY_ADA, sc))
            oT = m.sb("oT", [P, 4, S])
            with ExitStack() as mla:
                a = Room(nc, mla, "mla")
                qT, kT, v_tp = a.sb("qT", [QH, MH, S]), a.sb("kT", [QH, MH, S]), a.sb("v", [P, TT, MH, VH])
                norm_stage(nc, "nq", k, z[:, Z_QA:Z_KV], 2, 256, cols("q_a_norm"), z[:, Z_QA:Z_KV])
                norm_stage(nc, "nk", k, z[:, Z_KV:Z_R], 1, 128, cols("kv_a_norm"), z[:, Z_KV:Z_R])
                mla_heads_stage(nc, k, z, ins, z[:, Z_QA:Z_KV], z[:, Z_KV:Z_R], ins["w_uq"], ins["w_ukv"], qT, kT, v_tp, hT)
                items = [(qT[:, h, t * P:(t + 1) * P], kT[:, h, 0:(t + 1) * P], k.causal[:],
                          [v_tp[:, j, h, :] for j in range(t + 1)], h, t, None) for h in range(MH) for t in range(TT)]
                attention_stage(nc, "mlaa", k, items, MH, VH, oT)
            with ExitStack() as rwkv:
                a = Room(nc, rwkv, "rwkv")
                KR, sgate = a.sb("KR", [P, RP, TT, 2, P]), a.sb("sgate", [P, S])
                mid_e, end_e, bonus = a.sb("mid_e", [P, RP * TT]), a.sb("end_e", [P, RP * TT]), a.sb("bonus", [P, TT, RH])
                tile4 = lambda ap: ap.rearrange("p m (t n) -> p m t n", n=P)
                vT = a.sb("vT", [P, RP, TT, P])
                with ExitStack() as early:
                    rk = Room(nc, early, "early").sb("rk", [P, RP, S])
                    rwkv_prepare_stage(nc, k, z, ins, cols, hT, KR, rk, sgate, mid_e, end_e)
                    kkT, bT, kdT = tile4(hT[:, 0:4, :]), tile4(hT[:, 4:8, :]), tile4(z[:, Z_V:Z_WA, :])
                    rwkv_turn_stage(nc, k, z, ins, KR, rk, kkT, bT, kdT, vT, bonus)
                rT = a.sb("rT", [P, 4, S])
                rwkv_solve_stage(nc, k, ins, KR, z[:, Z_R:Z_K, :], z[:, Z_K:Z_V, :], kkT, bT, kdT, vT, mid_e, end_e, y_of(rT))
                yT = a.sb("yT", [P, 4, S])
                rwkv_finish_stage(nc, k, ins, y_of(rT), vT[:], bonus, sgate, yT, None)
                merge_stage(nc, "mg1", z, Z_GATE, [(ins["w_o_mla"], oT), (ins["w_o_rwkv"], yT)], hT)
            project_stage(nc, "po1", k, ins["w_out"], hT, DC, DC, xT, add=(mod[:, 2 * DC:3 * DC], xT))
        gates_dram = nc.dram_tensor("gates_scratch", [S // SUB, P, NK, SUB], F32, kind="Internal").ap()
        spill = nc.dram_tensor("act_scratch", [SPILL, P, S], F32, kind="Internal").ap()
        gain_stage(nc, "g2", gain, cols("norm_ffn"), mod[:, 4 * DC:5 * DC])
        norm_stage(nc, "n2", k, xT, DC, D, gain, hT, shift=mod[:, 3 * DC:4 * DC])
        peer(nc, "e1", k, ins, xT, hT, ins["w_query"], ins["keys1"], lambda c: c % 2, ins["down1"], ins["up1"],
             gates_dram, spill, ACT.Gelu_apprx_tanh, gain=mod[:, 5 * DC:6 * DC])
        norm_stage(nc, "n3", k, xT, DC, D, cols("norm1_g_2"), hT)
        second_mixer(nc, k, ins, cols, xT, hT)
        norm_stage(nc, "n4", k, xT, DC, D, cols("norm2_g_2"), hT)
        peer(nc, "e2", k, ins, xT, hT, ins["w_peer_q"], ins["keys2"], lambda c: c, ins["down2"], ins["up2"],
             gates_dram, spill, ACT.Gelu)
        with ExitStack() as stack:
            stored = Room(nc, stack, "end").sem("stored")
            with nc.Block() as block:
                @block.sync
                def _(sp):
                    sp.dma_start(out.rearrange("(c p) t -> p c t", p=P), xT[:]).then_inc(stored, 16)
                    sp.wait_ge(stored, 16)


def gain_stage(nc, name, gain, g, scale):
    with ExitStack() as stack:
        r = Room(nc, stack, name)
        chain = r.sem("chain")
        with nc.Block() as block:
            @block.vector
            def _(dve):
                link = Chain(dve, chain)
                link(dve.tensor_scalar(gain[:], scale, 1.0, None, ALU.add))
                dve.tensor_tensor(gain[:], gain[:], g, ALU.mult)

def _cols(v):
    return np.ascontiguousarray(np.asarray(v).reshape(-1, P).T)


def _chunks(w):
    kk, m = w.shape
    return w.reshape(kk // P, P, m // P, P).transpose(2, 1, 0, 3)


def _layout(inp):
    f = {n: np.asarray(v) for n, v in inp.items()}
    first = lambda n: f[n][0]
    zeros = lambda *s: np.zeros(s, np.float32)
    a = {}
    a["xT"] = f["x"][0].T
    a["positions"] = _cols(f["positions"][0])
    a["w_ada"] = first("w_ada").reshape(DC, P, 12, 512).transpose(2, 1, 0, 3)
    w = first("w_in")
    a["w_in"] = np.concatenate([w[:, 0:384], w[:, 416:], w[:, 384:416], zeros(D, 96)], axis=1)
    a["w_uq"], a["w_ukv"] = first("w_uq"), first("w_ukv")
    a["q_norm"], a["k_norm"] = f["q_norm"], f["k_norm"]
    a["inv_freq"] = (np.float32(10000.0) ** (-np.arange(16, dtype=np.float32) / np.float32(16))).astype(np.float32)[None]
    a["ident"] = np.eye(P, dtype=np.float32)
    q = np.arange(P)
    a["causal"] = np.where(q[None, :] <= q[:, None], 0.0, NEG).astype(np.float32)
    b16 = q[:, None] // 16 == q[None, :] // 16
    lower, upper = q[None, :] < q[:, None], q[None, :] > q[:, None]
    up_incl = q[None, :] >= q[:, None]
    a["masks"] = np.stack([np.where(upper & b16, -1.0, 0.0), np.where(lower & b16, -1.0, 0.0), np.where(lower & ~b16, -1.0, 0.0),
                           np.where(upper, 1.0, 0.0), np.where(up_incl, 1.0, 0.0)]).astype(np.float32)
    a["pair_ones"] = (q[:, None] // RN == q[None, :] // RN).astype(np.float32)
    a["pair_sel"] = (q[:, None] // RN == np.arange(2)[None, :]).astype(np.float32)
    a["id64"] = (q[:, None] % RN == np.arange(RN)[None, :]).astype(np.float32)
    for n in ("w_decay_up", "w_aaa_up", "w_gate_up", "w_o_mla", "w_o_rwkv", "w_out"):
        a[n] = first(n)
    w = first("w_in_2")
    sq = w[:, 1544:2056].reshape(D, 2, 4, SD).transpose(0, 2, 1, 3).reshape(D, 512)
    a["w_in_2"] = np.concatenate([w[:, 0:1536], sq, w[:, 2056:2312], w[:, 2312:2824], w[:, 2824:], w[:, 1536:1544], zeros(D, 120)], axis=1)
    dist = q[:, None] + P - np.arange(2 * P)[None, :]
    slopes = 2.0 ** -(np.arange(SH) + 1.0)
    a["alibi"] = np.where(((dist >= 0) & (dist < P))[:, None, :], -slopes[None, :, None] * dist[:, None, :], NEG).astype(np.float32)
    a["swa_sinks"] = f["swa_sinks_2"]
    a["memT"] = f["mem_2"][0].T
    for n in ("w_mem_kv", "w_fox_o", "w_swa_o", "w_mem_o"):
        a[n] = first(n + "_2")
    a["w_out_2"], a["w_peer_q"] = first("w_out_2"), first("w_peer_q_2")
    a["keys2"] = np.stack([first("peer_keys1_2"), first("peer_keys2_2")], axis=1).reshape(2 * PH, NK, P).transpose(2, 0, 1)
    a["down2"] = first("peer_u_2").reshape(NK, NK, DC, P).transpose(0, 3, 2, 1)
    a["up2"] = first("peer_v_2").reshape(NK, NK, D)
    a["w_query"] = first("w_query")
    a["keys1"] = np.stack([first("sub_keys1").T, first("sub_keys2").T], axis=1)
    a["down1"] = first("expert_down").reshape(NK, NK, DC, P).transpose(0, 3, 2, 1)
    a["up1"] = first("expert_up").reshape(NK, NK, D)
    rows = np.arange(2 * HN)
    a["row_pick"] = (rows[:, None, None] == 2 * np.arange(HN)[None, :, None] + (np.arange(P) // RN)[None, None, :]).astype(np.float32)
    a["iota16"], a["iota128"] = np.arange(K16, dtype=np.float32)[None], np.arange(NK, dtype=np.float32)[None]
    a["ln_x_w"], a["ln_x_b"] = f["ln_x_w"], f["ln_x_b"]
    for n in ("w_in", "w_in_2", "w_out", "w_out_2", "w_query", "w_peer_q", "w_mem_kv"):
        a[n] = _chunks(a[n])
    vecs = [("c", f["c"][0]), ("b_ada", first("b_ada")), ("norm_mix", first("norm_mix")), ("q_a_norm", first("q_a_norm")), ("kv_a_norm", first("kv_a_norm"))]
    vecs += [(n, first(n)) for n in ("mu_shift", "decay_base", "aaa_base", "k_k", "k_a")]
    vecs += [("r_k", first("r_k").reshape(-1)), ("norm_ffn", first("norm_ffn"))]
    vecs += [("norm1_g_2", first("norm1_g_2")), ("mem_norm_g_2", first("mem_norm_g_2")), ("norm2_g_2", first("norm2_g_2")),
             ("b_gate_2", first("b_gate_2"))]
    twice = lambda v: np.concatenate([v, v])
    vecs += [(n, twice(first(n + "_2"))) for n in ("fox_q_g", "fox_k_g", "swa_q_g", "swa_k_g")]
    vecs += [(n, first(n + "_2")) for n in ("mem_q_g", "mem_k_g")]
    vecs += [("b_forget", np.concatenate([first("b_forget_2"), zeros(P - FH)]))]
    at, parts, where = 0, [], {}
    for n, v in vecs:
        m = _cols(v)
        where[n] = (at, at + m.shape[1])
        at += m.shape[1]
        parts.append(m)
    a["columns"] = np.concatenate(parts, axis=1)
    return {n: np.ascontiguousarray(v) for n, v in a.items()}, where


def kernel(**inputs):
    import concourse.bacc as _bacc
    from concourse.bass_utils import run_bass_kernel_spmd as _run

    nc = _bacc.Bacc("TRN2", target_bir_lowering=False, num_devices=1)
    arrays, where = _layout(inputs)
    ins = {n: nc.dram_tensor(f"in_{n}", list(v.shape), mybir.dt.from_np(v.dtype), kind="ExternalInput").ap()
           for n, v in arrays.items()}
    out = nc.dram_tensor("out_xT", [D, S], F32, kind="ExternalOutput").ap()
    build(nc, ins, where, out)
    res = _run(nc, [{f"in_{n}": v for n, v in arrays.items()}], core_ids=[0])
    return np.ascontiguousarray(res.results[0]["out_xT"].T)[None]
```
